# Optimizing a Trainium2 kernel written in Bass

```python
import math
import jax, jax.numpy as jnp
from jax import lax
import numpy as np

D_MODEL = 1024
BATCH = 1
SEQ = 512
DEPTH = 2

CHUNK = 64
N_A_LAYERS = DEPTH // 2
N_B_LAYERS = DEPTH - N_A_LAYERS

SSM_EXPAND = 2
D_INNER = SSM_EXPAND * D_MODEL
SSM_HEAD_DIM = 64
SSM_HEADS = D_INNER // SSM_HEAD_DIM
SSM_GROUPS = 8
SSM_HEADS_PER_GROUP = SSM_HEADS // SSM_GROUPS
D_STATE = 128
D_CONV = 4
CONV_DIM = D_INNER + 2 * SSM_GROUPS * D_STATE
D_IN_PROJ = 2 * D_INNER + 2 * SSM_GROUPS * D_STATE + SSM_HEADS
DT_MIN = 1e-3
DT_MAX = 1e-1

SB_HEADS = 16
SB_HEAD_DIM = D_MODEL // SB_HEADS
SB_WIDTH = SB_HEADS * SB_HEAD_DIM
Q_BLOCK = 128

D_FF = 4 * D_MODEL

DEEPNORM_ALPHA = (2 * DEPTH) ** 0.25
DEEPNORM_BETA = (8 * DEPTH) ** -0.25
LN_EPS = 1e-5
RMS_EPS = 1e-5


def layer_norm(x, g, b):
    xf = x.astype(jnp.float32)
    mu = jnp.mean(xf, axis=-1, keepdims=True)
    var = jnp.mean(jnp.square(xf - mu), axis=-1, keepdims=True)
    return ((xf - mu) * lax.rsqrt(var + LN_EPS) * g.astype(jnp.float32) + b.astype(jnp.float32)).astype(x.dtype)

def causal_depthwise_conv(u, w, b):
    c = u.shape[-1]
    y = lax.conv_general_dilated(
        u, w[:, None, :], window_strides=(1,), padding=[(D_CONV - 1, 0)],
        dimension_numbers=("NWC", "WIO", "NWC"), feature_group_count=c)
    return y + b

def segsum(a):
    t = a.shape[-1]
    cs = jnp.cumsum(a, axis=-1)
    diff = cs[..., :, None] - cs[..., None, :]
    mask = jnp.tril(jnp.ones((t, t), dtype=bool))
    return jnp.where(mask, diff, -jnp.inf)

def ssd_chunked_scan(x, da, bm, cm):
    b, l, h, p = x.shape
    c = l // CHUNK
    g, r, n = SSM_GROUPS, SSM_HEADS_PER_GROUP, D_STATE
    xc = x.reshape(b, c, CHUNK, g, r, p)
    bc = bm.reshape(b, c, CHUNK, g, n)
    cc = cm.reshape(b, c, CHUNK, g, n)
    a = da.astype(jnp.float32).reshape(b, c, CHUNK, g, r).transpose(0, 1, 3, 4, 2)
    a_cs = jnp.cumsum(a, axis=-1)
    decay_mat = jnp.exp(segsum(a))
    cb = jnp.einsum("bclgn,bcsgn->bcgls", cc, bc)
    y_diag = jnp.einsum("bcgls,bcgrls,bcsgrp->bclgrp", cb, decay_mat, xc)
    decay_states = jnp.exp(a_cs[..., -1:] - a_cs)
    states = jnp.einsum("bclgn,bcgrl,bclgrp->bcgrpn", bc, decay_states, xc).astype(jnp.float32)
    block_decay = jnp.exp(a_cs[..., -1])

    def step(carry, inp):
        s_c, d_c = inp
        return carry * d_c[..., None, None] + s_c, carry

    init = jnp.zeros((b, g, r, p, n), jnp.float32)
    _, prev = lax.scan(step, init, (jnp.moveaxis(states, 1, 0), jnp.moveaxis(block_decay, 1, 0)))
    prev = jnp.moveaxis(prev, 0, 1)
    y_off = jnp.einsum("bclgn,bcgrpn,bcgrl->bclgrp", cc, prev, jnp.exp(a_cs))
    return (y_diag + y_off).reshape(b, l, h, p).astype(x.dtype)

def mamba2_mixer(u, w_in, conv_w, conv_b, dt_bias, a_log, d_skip, norm_w, w_out):
    b, l, _ = u.shape
    zxbcdt = u @ w_in
    z = zxbcdt[..., :D_INNER]
    xbc = zxbcdt[..., D_INNER:D_INNER + CONV_DIM]
    dt_raw = zxbcdt[..., D_INNER + CONV_DIM:]
    xbc = jax.nn.silu(causal_depthwise_conv(xbc, conv_w, conv_b))
    xs = xbc[..., :D_INNER]
    bm = xbc[..., D_INNER:D_INNER + SSM_GROUPS * D_STATE].reshape(b, l, SSM_GROUPS, D_STATE)
    cm = xbc[..., D_INNER + SSM_GROUPS * D_STATE:].reshape(b, l, SSM_GROUPS, D_STATE)
    dt = jax.nn.softplus((dt_raw + dt_bias).astype(jnp.float32))
    a = -jnp.exp(a_log.astype(jnp.float32))
    xh = xs.reshape(b, l, SSM_HEADS, SSM_HEAD_DIM)
    y = ssd_chunked_scan(xh * dt[..., None].astype(xh.dtype), dt * a, bm, cm)
    y = (y + xh * d_skip[:, None]).reshape(b, l, D_INNER)
    yg = (y * jax.nn.silu(z)).astype(jnp.float32).reshape(b, l, SSM_GROUPS, D_INNER // SSM_GROUPS)
    yg = yg * lax.rsqrt(jnp.mean(jnp.square(yg), axis=-1, keepdims=True) + RMS_EPS)
    y = (yg.reshape(b, l, D_INNER) * norm_w.astype(jnp.float32)).astype(u.dtype)
    return y @ w_out

def shared_kv(h, w_k, w_v):
    b, l, _ = h.shape
    k = (h @ w_k).reshape(b, l, SB_HEADS, SB_HEAD_DIM).transpose(0, 2, 1, 3)
    v = (h @ w_v).reshape(b, l, SB_HEADS, SB_HEAD_DIM).transpose(0, 2, 1, 3)
    return k, v

def stick_breaking_attention(u, w_q, k, v, w_o):
    b, l, _ = u.shape
    q = (u @ w_q).reshape(b, l, SB_HEADS, SB_HEAD_DIM).transpose(0, 2, 1, 3) * (SB_HEAD_DIM ** -0.5)
    nb = l // Q_BLOCK
    kb = jnp.moveaxis(k.reshape(b, SB_HEADS, nb, Q_BLOCK, SB_HEAD_DIM), 2, 0)
    vb = jnp.moveaxis(v.reshape(b, SB_HEADS, nb, Q_BLOCK, SB_HEAD_DIM), 2, 0)
    idx = jnp.arange(Q_BLOCK)
    diag_mask = idx[None, :] < idx[:, None]
    later = (idx[:, None] > idx[None, :]).astype(jnp.float32)

    outs = []
    for i in range(nb):
        qi = q[:, :, i * Q_BLOCK:(i + 1) * Q_BLOCK]

        def step(carry, inp, qi=qi):
            acc, o = carry
            kj, vj, is_diag = inp
            z = jnp.einsum("bhqd,bhkd->bhqk", qi, kj).astype(jnp.float32)
            valid = jnp.logical_or(jnp.logical_not(is_diag), diag_mask)
            lo = jnp.where(valid, jax.nn.log_sigmoid(-z), 0.0)
            after = jnp.einsum("bhqj,js->bhqs", lo, later) + acc[..., None]
            logw = jnp.where(valid, z + lo + after, -jnp.inf)
            o = o + jnp.einsum("bhqk,bhkd->bhqd", jnp.exp(logw).astype(vj.dtype), vj).astype(jnp.float32)
            acc = acc + jnp.sum(lo, axis=-1)
            return (acc, o), None

        init = (jnp.zeros((b, SB_HEADS, Q_BLOCK), jnp.float32),
                jnp.zeros((b, SB_HEADS, Q_BLOCK, SB_HEAD_DIM), jnp.float32))
        xs = (kb[:i + 1][::-1], vb[:i + 1][::-1], jnp.arange(i + 1) == 0)
        (_, o_i), _ = lax.scan(step, init, xs)
        outs.append(o_i.astype(u.dtype))
    o = jnp.concatenate(outs, axis=2)
    o = o.transpose(0, 2, 1, 3).reshape(b, l, SB_WIDTH)
    return o @ w_o

def squared_relu_mlp(h, w1, w2):
    return jnp.square(jax.nn.relu(h @ w1)) @ w2

def first_inputs(seed: int = 0) -> dict:
    key = jax.random.key(seed)
    ks = jax.random.split(key, 20)
    f32 = jnp.float32

    def nrm(k, shape, scale):
        return jax.random.normal(k, shape, f32) * scale

    x = nrm(ks[0], (BATCH, SEQ, D_MODEL), 1.0)
    ssm_w_in = nrm(ks[1], (N_A_LAYERS, D_MODEL, D_IN_PROJ), D_MODEL ** -0.5)
    ssm_conv_w = jax.random.uniform(ks[2], (N_A_LAYERS, D_CONV, CONV_DIM), f32, -0.5, 0.5)
    ssm_conv_b = nrm(ks[3], (N_A_LAYERS, CONV_DIM), 0.02)
    dt = jnp.exp(jax.random.uniform(ks[4], (N_A_LAYERS, SSM_HEADS), f32)
                 * (math.log(DT_MAX) - math.log(DT_MIN)) + math.log(DT_MIN))
    dt = jnp.maximum(dt, 1e-4)
    ssm_dt_bias = dt + jnp.log(-jnp.expm1(-dt))
    ssm_a_log = jnp.log(jax.random.uniform(ks[5], (N_A_LAYERS, SSM_HEADS), f32, 1.0, 16.0))
    ssm_d = 1.0 + nrm(ks[6], (N_A_LAYERS, SSM_HEADS), 0.1)
    ssm_norm_w = 1.0 + nrm(ks[7], (N_A_LAYERS, D_INNER), 0.1)
    ssm_w_out = nrm(ks[8], (N_A_LAYERS, D_INNER, D_MODEL), D_INNER ** -0.5 * DEEPNORM_BETA)
    sb_w_k = nrm(ks[9], (D_MODEL, SB_WIDTH), D_MODEL ** -0.5)
    sb_w_v = nrm(ks[10], (D_MODEL, SB_WIDTH), D_MODEL ** -0.5 * DEEPNORM_BETA)
    sb_w_q = nrm(ks[11], (N_B_LAYERS, D_MODEL, SB_WIDTH), D_MODEL ** -0.5)
    sb_w_o = nrm(ks[12], (N_B_LAYERS, SB_WIDTH, D_MODEL), SB_WIDTH ** -0.5 * DEEPNORM_BETA)
    mlp_w1 = nrm(ks[13], (DEPTH, D_MODEL, D_FF), D_MODEL ** -0.5)
    mlp_w2 = nrm(ks[14], (DEPTH, D_FF, D_MODEL), D_FF ** -0.5 * DEEPNORM_BETA)
    ln_mix_g = 1.0 + nrm(ks[15], (DEPTH, D_MODEL), 0.05)
    ln_mix_b = nrm(ks[16], (DEPTH, D_MODEL), 0.02)
    ln_mlp_g = 1.0 + nrm(ks[17], (DEPTH, D_MODEL), 0.05)
    ln_mlp_b = nrm(ks[18], (DEPTH, D_MODEL), 0.02)
    return {"x": x, "ssm_w_in": ssm_w_in, "ssm_conv_w": ssm_conv_w, "ssm_conv_b": ssm_conv_b,
            "ssm_dt_bias": ssm_dt_bias, "ssm_a_log": ssm_a_log, "ssm_d": ssm_d,
            "ssm_norm_w": ssm_norm_w, "ssm_w_out": ssm_w_out, "sb_w_k": sb_w_k, "sb_w_v": sb_w_v,
            "sb_w_q": sb_w_q, "sb_w_o": sb_w_o, "mlp_w1": mlp_w1, "mlp_w2": mlp_w2,
            "ln_mix_g": ln_mix_g, "ln_mix_b": ln_mix_b, "ln_mlp_g": ln_mlp_g, "ln_mlp_b": ln_mlp_b}

def first_block(x, ssm_w_in, ssm_conv_w, ssm_conv_b, ssm_dt_bias, ssm_a_log, ssm_d, ssm_norm_w,
              ssm_w_out, sb_w_k, sb_w_v, sb_w_q, sb_w_o, mlp_w1, mlp_w2,
              ln_mix_g, ln_mix_b, ln_mlp_g, ln_mlp_b):
    h = x
    k = v = None
    for layer in range(DEPTH):
        if layer < N_A_LAYERS:
            i = layer
            mix = mamba2_mixer(h, ssm_w_in[i], ssm_conv_w[i], ssm_conv_b[i], ssm_dt_bias[i],
                               ssm_a_log[i], ssm_d[i], ssm_norm_w[i], ssm_w_out[i])
        else:
            if layer == N_A_LAYERS:
                k, v = shared_kv(h, sb_w_k, sb_w_v)
            j = layer - N_A_LAYERS
            mix = stick_breaking_attention(h, sb_w_q[j], k, v, sb_w_o[j])
        h = layer_norm(DEEPNORM_ALPHA * h + mix, ln_mix_g[layer], ln_mix_b[layer])
        h = layer_norm(DEEPNORM_ALPHA * h + squared_relu_mlp(h, mlp_w1[layer], mlp_w2[layer]),
                       ln_mlp_g[layer], ln_mlp_b[layer])
    return h


DEPTH_2 = 1

HEAD_DIM = 64
RWKV_HEADS = 8
RWKV_WIDTH = RWKV_HEADS * HEAD_DIM
ATT_HEADS = 8
ATT_WIDTH = ATT_HEADS * HEAD_DIM
IDX_HEADS = 8
IDX_DIM = 64
DECAY_RANK = 64
AAA_RANK = 64
GATE_RANK = 128
MAX_TOPK = 256
ROPE_THETA = 10000.0
D_FF_2 = ((8 * D_MODEL // 3 + 255) // 256) * 256
NORM_EPS = 1e-6
LNX_EPS = 64e-5

RWKV_COLS = 3 * RWKV_WIDTH + DECAY_RANK + AAA_RANK + GATE_RANK
ATT_COLS = 3 * ATT_WIDTH
IDX_COLS = IDX_HEADS * IDX_DIM + IDX_DIM + IDX_HEADS
GATE_COLS = 2 * D_MODEL
IN_COLS = RWKV_COLS + ATT_COLS + IDX_COLS + GATE_COLS


def rmsnorm(x, g):
    xf = x.astype(jnp.float32)
    y = xf * lax.rsqrt(jnp.mean(xf * xf, axis=-1, keepdims=True) + NORM_EPS)
    return (y * g.astype(jnp.float32)).astype(x.dtype)

def rope(t):
    S, D = t.shape[1], t.shape[-1]
    half = D // 2
    inv = 1.0 / (ROPE_THETA ** (jnp.arange(half, dtype=jnp.float32) * 2.0 / D))
    ang = jnp.arange(S, dtype=jnp.float32)[:, None] * inv[None, :]
    cos = jnp.cos(ang)[None, :, None, :]
    sin = jnp.sin(ang)[None, :, None, :]
    tf = t.astype(jnp.float32)
    t1, t2 = tf[..., :half], tf[..., half:]
    return jnp.concatenate([t1 * cos - t2 * sin, t1 * sin + t2 * cos], axis=-1).astype(t.dtype)

def token_shift(p, mu):
    prev = jnp.pad(p, ((0, 0), (1, 0), (0, 0)))[:, :-1]
    return p + (prev - p) * mu

def rwkv7_mix(p, w_decay_up, w0, a_up, a0, g_up, k_k, k_a, r_k, lnx_g, lnx_b):
    B, S, _ = p.shape
    H, N = RWKV_HEADS, HEAD_DIM
    c = np.cumsum([RWKV_WIDTH, RWKV_WIDTH, RWKV_WIDTH, DECAY_RANK, AAA_RANK])
    r, k, v, wd, ad, gd = jnp.split(p, c, axis=-1)
    w = -jax.nn.softplus(-(w0 + jnp.tanh(wd) @ w_decay_up)) - 0.5
    a = jax.nn.sigmoid(a0 + ad @ a_up)
    g = jax.nn.sigmoid(gd) @ g_up
    kk = (k * k_k).reshape(B, S, H, N).astype(jnp.float32)
    kk = kk / jnp.maximum(jnp.linalg.norm(kk, axis=-1, keepdims=True), 1e-12)
    k = k * (1.0 + (a - 1.0) * k_a)
    heads = lambda t: t.reshape(B, S, H, N).astype(jnp.float32)
    r_h, k_h, v_h, a_h = heads(r), heads(k), heads(v), heads(a)
    decay = jnp.exp(-jnp.exp(heads(w)))
    tm = lambda t: jnp.moveaxis(t, 1, 0)

    def step(state, inp):
        r_t, d_t, k_t, v_t, kk_t, a_t = inp
        sa = jnp.einsum('bhij,bhj->bhi', state, -kk_t)
        state = (state * d_t[:, :, None, :]
                 + sa[..., None] * (kk_t * a_t)[:, :, None, :]
                 + v_t[..., None] * k_t[:, :, None, :])
        y_t = jnp.einsum('bhij,bhj->bhi', state, r_t)
        return state, y_t

    state0 = jnp.zeros((B, H, N, N), jnp.float32)
    _, y = lax.scan(step, state0, (tm(r_h), tm(decay), tm(k_h), tm(v_h), tm(kk), tm(a_h)))
    y = jnp.moveaxis(y, 0, 1)
    mean = jnp.mean(y, axis=-1, keepdims=True)
    var = jnp.mean(jnp.square(y - mean), axis=-1, keepdims=True)
    y = (y - mean) * lax.rsqrt(var + LNX_EPS)
    y = y * lnx_g.reshape(H, N) + lnx_b.reshape(H, N)
    bonus = jnp.sum(r_h * k_h * r_k.astype(jnp.float32), axis=-1, keepdims=True) * v_h
    y = (y + bonus).reshape(B, S, RWKV_WIDTH).astype(p.dtype)
    return y * g

def dsa_attention(q, k, v, q_idx, k_idx, w_idx):
    B, S, H, Dh = q.shape
    topk = min(MAX_TOPK, S // 4)
    nb = S // Q_BLOCK
    blk = lambda t: jnp.moveaxis(t.reshape((B, nb, Q_BLOCK) + t.shape[2:]), 1, 0)
    key_pos = jnp.arange(S)
    idx_scale = IDX_DIM ** -0.5 * IDX_HEADS ** -0.5

    def one_block(args):
        qb, qib, wib, bi = args
        t = bi * Q_BLOCK + jnp.arange(Q_BLOCK)
        sc = jax.nn.relu(jnp.einsum('bqhd,bsd->bqhs', qib, k_idx).astype(jnp.float32))
        score = jnp.einsum('bqhs,bqh->bqs', sc, wib.astype(jnp.float32)) * idx_scale
        causal = key_pos[None, None, :] <= t[None, :, None]
        score = jnp.where(causal, score, -jnp.inf)
        _, sel = lax.top_k(score, topk)
        valid = sel <= t[None, :, None]
        kg = jax.vmap(lambda kb, ib: kb[ib])(k, sel)
        vg = jax.vmap(lambda vb, ib: vb[ib])(v, sel)
        logits = jnp.einsum('bqhd,bqkhd->bqhk', qb, kg).astype(jnp.float32) * Dh ** -0.5
        logits = jnp.where(valid[:, :, None, :], logits, -jnp.inf)
        prob = jax.nn.softmax(logits, axis=-1).astype(vg.dtype)
        return jnp.einsum('bqhk,bqkhd->bqhd', prob, vg)

    out = lax.map(one_block, (blk(q), blk(q_idx), blk(w_idx), jnp.arange(nb)))
    return jnp.moveaxis(out, 0, 1).reshape(B, S, H * Dh)

def second_inputs(seed: int = 0) -> dict:
    key = jax.random.key(seed)
    ks = jax.random.split(key, 24)
    nrm = lambda k, shape, s: jax.random.normal(k, shape, jnp.float32) * s
    return {
        "x": jax.random.normal(ks[0], (BATCH, SEQ, D_MODEL), jnp.float32),
        "norm1_g": 1.0 + nrm(ks[1], (D_MODEL,), 0.05),
        "w_in": nrm(ks[2], (D_MODEL, IN_COLS), D_MODEL ** -0.5),
        "tshift_mu": jax.random.uniform(ks[3], (RWKV_COLS,), jnp.float32),
        "w_decay_up": nrm(ks[4], (DECAY_RANK, RWKV_WIDTH), 0.5 * DECAY_RANK ** -0.5),
        "w0": nrm(ks[5], (RWKV_WIDTH,), 0.5),
        "a_up": nrm(ks[6], (AAA_RANK, RWKV_WIDTH), 0.5 * AAA_RANK ** -0.5),
        "a0": nrm(ks[7], (RWKV_WIDTH,), 0.5),
        "g_up": nrm(ks[8], (GATE_RANK, RWKV_WIDTH), GATE_RANK ** -0.5),
        "k_k": 0.85 + nrm(ks[9], (RWKV_WIDTH,), 0.05),
        "k_a": 1.0 + nrm(ks[10], (RWKV_WIDTH,), 0.05),
        "r_k": nrm(ks[11], (RWKV_HEADS, HEAD_DIM), 0.1),
        "lnx_g": 1.0 + nrm(ks[12], (RWKV_WIDTH,), 0.05),
        "lnx_b": nrm(ks[13], (RWKV_WIDTH,), 0.01),
        "w_o_rwkv": nrm(ks[14], (RWKV_WIDTH, D_MODEL), RWKV_WIDTH ** -0.5),
        "w_o_att": nrm(ks[15], (ATT_WIDTH, D_MODEL), ATT_WIDTH ** -0.5),
        "w_out": nrm(ks[16], (D_MODEL, D_MODEL), D_MODEL ** -0.5),
        "norm2_g": 1.0 + nrm(ks[17], (D_MODEL,), 0.05),
        "w_ffn_in": nrm(ks[18], (D_MODEL, 2 * D_FF_2), D_MODEL ** -0.5),
        "w_ffn_out": nrm(ks[19], (D_FF_2, D_MODEL), D_FF_2 ** -0.5),
        "normf_g": 1.0 + nrm(ks[20], (D_MODEL,), 0.05),
    }

def second_block(x, norm1_g, w_in, tshift_mu, w_decay_up, w0, a_up, a0, g_up, k_k, k_a, r_k,
              lnx_g, lnx_b, w_o_rwkv, w_o_att, w_out, norm2_g, w_ffn_in, w_ffn_out, normf_g):
    B, S, _ = x.shape
    h = x
    for _layer in range(DEPTH_2):
        u = rmsnorm(h, norm1_g)
        proj = u @ w_in
        c = np.cumsum([RWKV_COLS, ATT_COLS, IDX_COLS])
        p_rwkv, p_att, p_idx, p_gate = jnp.split(proj, c, axis=-1)

        y_a = rwkv7_mix(token_shift(p_rwkv, tshift_mu), w_decay_up, w0, a_up, a0, g_up,
                        k_k, k_a, r_k, lnx_g, lnx_b)

        q, k, v = jnp.split(p_att, 3, axis=-1)
        hv = lambda t: t.reshape(B, S, ATT_HEADS, HEAD_DIM)
        q, k, v = rope(hv(q)), rope(hv(k)), hv(v)
        ci = np.cumsum([IDX_HEADS * IDX_DIM, IDX_DIM])
        q_idx, k_idx, w_idx = jnp.split(p_idx, ci, axis=-1)
        q_idx = rope(q_idx.reshape(B, S, IDX_HEADS, IDX_DIM))
        k_idx = rope(k_idx[:, :, None, :])[:, :, 0, :]
        y_b = dsa_attention(q, k, v, q_idx, k_idx, w_idx)

        g_a, g_b = jnp.split(jax.nn.sigmoid(p_gate), 2, axis=-1)
        merged = g_a * (y_a @ w_o_rwkv) + g_b * (y_b @ w_o_att)
        h = h + merged @ w_out

        z = rmsnorm(h, norm2_g) @ w_ffn_in
        z_gate, z_up = jnp.split(z, 2, axis=-1)
        h = h + (jax.nn.silu(z_gate) * z_up) @ w_ffn_out
    return rmsnorm(h, normf_g)


def setup_inputs(seed=0):
    out = dict(first_inputs(seed))
    for name, value in second_inputs(seed + 1).items():
        if name != "x":
            out[name + "_2"] = value
    return out


def reference(
    x, ssm_w_in, ssm_conv_w, ssm_conv_b, ssm_dt_bias, ssm_a_log, ssm_d, ssm_norm_w, ssm_w_out,
    sb_w_k, sb_w_v, sb_w_q, sb_w_o, mlp_w1, mlp_w2, ln_mix_g, ln_mix_b, ln_mlp_g, ln_mlp_b,
    norm1_g_2, w_in_2, tshift_mu_2, w_decay_up_2, w0_2, a_up_2, a0_2, g_up_2, k_k_2, k_a_2,
    r_k_2, lnx_g_2, lnx_b_2, w_o_rwkv_2, w_o_att_2, w_out_2, norm2_g_2, w_ffn_in_2, w_ffn_out_2,
    normf_g_2,
):
    x = first_block(
        x, ssm_w_in, ssm_conv_w, ssm_conv_b, ssm_dt_bias, ssm_a_log, ssm_d, ssm_norm_w,
        ssm_w_out, sb_w_k, sb_w_v, sb_w_q, sb_w_o, mlp_w1, mlp_w2, ln_mix_g, ln_mix_b, ln_mlp_g,
        ln_mlp_b,
    )
    return second_block(
        x, norm1_g_2, w_in_2, tshift_mu_2, w_decay_up_2, w0_2, a_up_2, a0_2, g_up_2, k_k_2,
        k_a_2, r_k_2, lnx_g_2, lnx_b_2, w_o_rwkv_2, w_o_att_2, w_out_2, norm2_g_2, w_ffn_in_2,
        w_ffn_out_2, normf_g_2,
    )


_drawn_inputs = setup_inputs


def setup_inputs(seed=0):
    import zlib

    import numpy as np

    out = dict(_drawn_inputs(seed))
    spreads = {}
    factors = {'ssm_conv_b': 2.854, 'k_k_2': 46.237, 'k_a_2': 2.833, 'lnx_g_2': 3.516, 'lnx_b_2': 24.234}
    for name, (base, spread) in spreads.items():
        noise = np.random.default_rng([zlib.crc32(name.encode()), seed]).standard_normal(out[name].shape)
        drawn = base * np.exp(spread * noise) if base else spread * noise
        out[name] = __import__('jax').numpy.asarray(drawn.astype(out[name].dtype))
    for name, factor in factors.items():
        out[name] = (out[name] * factor).astype(out[name].dtype)
    return out
```

```python
import math
from contextlib import ExitStack

import numpy as np

import concourse.bass as bass
from concourse import mybir

F32 = mybir.dt.float32
U32 = mybir.dt.uint32
ALU = mybir.AluOpType
ACT = mybir.ActivationFunctionType
AX_X = mybir.AxisListType.X

P = 128
SEQ = 512
NT = SEQ // P
D = 1024
KD = D // P
WIDE = 512
RING = 3
KC = 8
BANKS = 8
LN_EPS = 1e-5
RMS_EPS = 1e-5
NORM_EPS = 1e-6
LNX_EPS = 64e-5
ALPHA = (2 * 2) ** 0.25

D_INNER = 2 * D
SSM_HEADS = D_INNER // 64
SSM_GROUPS = 8
HPG = SSM_HEADS // SSM_GROUPS
XBC = D_INNER + 2 * SSM_GROUPS * P
XBC_TILES = XBC // P
X_TILES = D_INNER // P
D_CONV = 4
SB_HEADS = 16
HD = 64
D_FF = 4 * D
RW = 512
RW_COLS = 3 * RW + 64 + 64 + 128
ATT = 512
IDXW = 512 + 64 + 8
D_FF2 = 2816
TOPK = 128
NHEAD = 8
NHP = NHEAD // 2
DECAY_UNIT = math.exp(-0.5)
REMOVED = -3.0e38
FUTURE = -1.0e38

ROWS = [("mu", RW_COLS // P), ("w0", 4), ("a0", 4), ("k_k", 4), ("k_a", 4), ("r_k", 4), ("lnx_g", 4), ("lnx_b", 4),
        ("conv_b", XBC_TILES), ("norm_w", X_TILES), ("norm1_g", KD), ("norm2_g", KD)]


def host_rope():
    half = HD // 2
    inv = (np.float32(1.0) / (np.float32(10000.0) ** (np.arange(half, dtype=np.float32) * np.float32(2.0) / np.float32(HD)))).astype(np.float32)
    ang = (np.arange(SEQ, dtype=np.float32)[:, None] * inv[None, :]).astype(np.float32)
    return np.concatenate([np.cos(ang), np.sin(ang)], axis=1).astype(np.float32)


class Gemm:

    def __init__(self, kit, w, k_tiles, c0, cols, feature, k_split=KC):
        self.kit, self.feature = kit, feature
        self.chunk0, self.tile0 = len(kit.chunks), kit.tiles
        self.parts = []
        for c in range(c0, c0 + cols, WIDE):
            n = min(WIDE, c0 + cols - c)
            blocks = [(k, min(k_split, k_tiles - k)) for k in range(0, k_tiles, k_split)]
            kit.tiles += -(-n // P) if feature else NT
            for k, nk in blocks:
                kit.chunks.append((w, k, nk, c, n))
                if k + nk == k_tiles:
                    kit.chunk_over.append((kit.tile_ready, kit.tiles))
                else:
                    kit.parts_used += 1
                    kit.chunk_over.append((kit.part_used, kit.parts_used))
            self.parts.append((n, blocks))
        assert not feature or k_tiles <= KC
        self.per_part = [-(-n // P) if feature else NT for n, _ in self.parts]
        self.count = sum(self.per_part)

    def bank(self, n):
        return (self.tile0 + n) % BANKS

    def tensor(self, pe, x):
        kit = self.kit
        i, tile = self.chunk0, self.tile0
        for n, blocks in self.parts:
            for b, (k0, nk) in enumerate(blocks):
                pe.wait_ge(kit.chunk_landed[i % RING], 16 * (i // RING + 1))
                w = kit.ring[i % RING]
                tiles = -(-n // P) if self.feature else NT
                for m in range(tiles):
                    t = tile + m
                    if b == 0 and t >= BANKS:
                        pe.wait_ge(kit.tile_free, t - BANKS + 1)
                    for k in range(nk):
                        first, last = b == 0 and k == 0, b == len(blocks) - 1 and k == nk - 1
                        if self.feature:
                            mp = min(P, n - m * P)
                            mm = pe.matmul(kit.psum[0:mp, t % BANKS, :], w[:, k, m * P:m * P + mp], x[:, k0 + k, :],
                                           start=first, stop=last)
                        else:
                            mm = pe.matmul(kit.psum[:, t % BANKS, 0:n], x[:, k0 + k, m * P:(m + 1) * P], w[:, k, 0:n],
                                           start=first, stop=last)
                    if last:
                        mm.then_inc(kit.tile_ready, 1)
                    elif m == tiles - 1:
                        mm.then_inc(kit.part_used, 1)
                i += 1
            tile += -(-n // P) if self.feature else NT

    def wait_tile(self, eng, n):
        eng.wait_ge(self.kit.tile_ready, self.tile0 + n + 1)
        return self.kit.psum[:, self.bank(n), :]


class Chain:

    def __init__(self, eng, sem):
        self.eng, self.sem, self.n = eng, sem, 0

    def __call__(self, ins):
        self.n += 1
        ins.then_inc(self.sem, 1)
        self.eng.wait_ge(self.sem, self.n)

    def mark(self, ins):
        self.n += 1
        ins.then_inc(self.sem, 1)
        return self.n

    def wait(self):
        self.eng.wait_ge(self.sem, self.n)


class Kit:

    def __init__(self, nc, ctx):
        self.nc, self.ctx = nc, ctx
        self.chunks, self.chunk_over, self.tiles, self.parts_used = [], [], 0, 0
        self.psum = self.tensor_psum("psum", [P, BANKS, WIDE])
        self.ring_mem = self.tensor_sb("weight_ring", [P, RING, KC, WIDE])
        self.ring = [self.ring_mem[:, r] for r in range(RING)]
        self.chunk_landed = [self.sem(f"chunk_landed{r}") for r in range(RING)]
        self.part_used = self.sem("part_used")
        self.tile_ready = self.sem("tile_ready")
        self.tile_free = self.sem("tile_free")
        self.phase_done = self.sem("phase_done")
        self.vector_step, self.chain = self.sem("vector_step"), None
        self.norm_sems = [self.sem(f"norm_{n}") for n in ("variance_ready", "deviation_ready", "normed", "transposed",
                                                          "transpose_read", "rows_landed")]
        self.norms, self.norm_rows = 0, 0

    def tensor_sb(self, name, shape):
        return self.ctx.enter_context(self.nc.sbuf_tensor(name, shape, F32))

    def tensor_psum(self, name, shape):
        return self.ctx.enter_context(self.nc.psum_tensor(name, shape, F32))

    def vector_chain(self, dve):
        if self.chain is None:
            self.chain = Chain(dve, self.vector_step)
        return self.chain

    def sem(self, name):
        return self.ctx.enter_context(self.nc.semaphore(name))


def over(ap, n):
    return ap.unsqueeze(len(ap.shape)).broadcast_to(list(ap.shape) + [n])


def across(ap, n):
    return ap.unsqueeze(1).broadcast_to([ap.shape[0], n, ap.shape[1]])


def norm_rows(nc, kit, m, gemm, alpha, res, mode, eps, tag, final=None):
    s_var, s_std, s_norm, s_tr, s_tf, s_rows = kit.norm_sems
    s_out = kit.sem("out_written") if final is not None else None
    tok0, turn0 = kit.norms * NT, kit.norms * 2 * NT
    kit.norms += 1
    if mode != "rms":
        kit.norm_rows += 32 if mode == "ln" else 16
    rows_in = kit.norm_rows
    src = m.h if mode != "rms" else m.unit
    last = final is not None

    def tensor(pe):
        if gemm is not None:
            gemm.tensor(pe, m.gemm_in)
        if last:
            return
        for t in range(NT):
            pe.wait_ge(s_norm, tok0 + t + 1)
            if gemm is not None and t == 0:
                pe.wait_ge(kit.tile_free, gemm.tile0 + gemm.count)
            for j in range(2):
                n = 2 * t + j
                if n >= BANKS // 2:
                    pe.wait_ge(s_tf, turn0 + n - BANKS // 2 + 1)
                for q in range(4):
                    mm = pe.transpose(kit.psum[:, n % 4, q * P:(q + 1) * P],
                                      src[:, t, (4 * j + q) * P:(4 * j + q + 1) * P], m.ident[:, :])
                mm.then_inc(s_tr, 1)

    def vector(dve):
        step = kit.vector_chain(dve)
        if gemm is not None:
            if m.h_late:
                dve.wait_ge(m.h_landed, 16)
            for n in range(2):
                for t in range(NT):
                    ps = gemm.wait_tile(dve, 4 * n + t)
                    hs = m.h[:, t, n * WIDE:(n + 1) * WIDE]
                    dve.scalar_tensor_tensor(out=hs, in0=hs, scalar=alpha, in1=ps, op0=ALU.mult, op1=ALU.add)\
                       .then_inc(kit.tile_free, 1)
                    dve.wait_ge(kit.tile_free, gemm.tile0 + 4 * n + t + 1)
                    step(dve.bn_stats(m.stats[:, t, n, :], hs))
        else:
            for t in range(NT):
                for n in range(2):
                    step(dve.bn_stats(m.stats[:, t, n, :], m.h[:, t, n * WIDE:(n + 1) * WIDE]))
        for t in range(NT):
            ins = dve.bn_aggr(m.mv[:, t, :], m.stats[:, t].rearrange("p a b -> p (a b)"))
            if mode == "ln":
                ins.then_inc(s_var, 1)
            else:
                step(ins)
                dve.scalar_tensor_tensor(out=m.ms[:, t:t + 1], in0=m.mv[:, t, 0:1], scalar=m.mv[:, t, 0:1],
                                         in1=m.mv[:, t, 1:2], op0=ALU.mult, op1=ALU.add).then_inc(s_var, 1)
        for t in range(NT):
            dve.wait_ge(s_std, tok0 + t + 1)
            step(dve.reciprocal(m.rstd[:, t:t + 1], m.std[:, t:t + 1]))
            ht = m.h[:, t, :]
            if mode == "ln":
                step(dve.tensor_scalar(ht, ht, m.mv[:, t, 0:1], m.rstd[:, t:t + 1], ALU.subtract, ALU.mult))
                if t == 0:
                    dve.wait_ge(s_rows, rows_in)
                step(dve.tensor_tensor(ht, ht, m.rows[:, 0, :], ALU.mult))
                dve.tensor_tensor(ht, ht, m.rows[:, 1, :], ALU.add).then_inc(s_norm, 1)
            elif not last:
                dve.tensor_scalar(m.unit[:, t, :], ht, m.rstd[:, t:t + 1], None, ALU.mult).then_inc(s_norm, 1)
            else:
                if t == 0:
                    dve.wait_ge(s_rows, rows_in)
                dve.scalar_tensor_tensor(out=ht, in0=ht, scalar=m.rstd[:, t:t + 1], in1=m.rows[:, 0, :],
                                         op0=ALU.mult, op1=ALU.mult).then_inc(s_norm, 1)

    def scalar(act):
        for t in range(NT):
            act.wait_ge(s_var, tok0 + t + 1)
            v = m.mv[:, t, 1:2] if mode == "ln" else m.ms[:, t:t + 1]
            act.activation(m.std[:, t:t + 1], v, ACT.Sqrt, bias=m.eps[eps]).then_inc(s_std, 1)
        if last:
            return
        for n in range(2 * NT):
            t, j = n // 2, n % 2
            act.wait_ge(s_tr, turn0 + n + 1)
            for q in range(4):
                k = 4 * j + q
                dst = m.xT[:, k, t * P:(t + 1) * P]
                ps = kit.psum[:, n % 4, q * P:(q + 1) * P]
                if mode == "ln":
                    ins = act.activation(dst, ps, ACT.Copy)
                else:
                    ins = act.activation(dst, ps, ACT.Copy, scale=m.col(res, k))
            ins.then_inc(s_tf, 1)

    def gpsimd(pool):
        if mode == "ln":
            g, b = m.ln_rows[tag]
            pool.dma_start(m.rows[:, 0, :], g.partition_broadcast(P)).then_inc(s_rows, 16)
            pool.dma_start(m.rows[:, 1, :], b.partition_broadcast(P)).then_inc(s_rows, 16)
        elif last:
            pool.dma_start(m.rows[:, 0, :], m.normf.partition_broadcast(P)).then_inc(s_rows, 16)
            out = final.rearrange("(t p) d -> p t d", p=P)
            for t in range(NT):
                pool.wait_ge(s_norm, tok0 + t + 1)
                pool.dma_start(out[:, t, :], m.h[:, t, :]).then_inc(s_out, 16)
            pool.wait_ge(s_out, 16 * NT)

    return tensor, vector, scalar, gpsimd


def setup(nc, kit, m, a):
    s_base = kit.sem("constant_filled")
    s_sel = kit.sem("constant_cut")
    s_par = kit.sem("parameter_rows_landed")
    s_tr = kit.sem("setup_transposed")
    s_tf = kit.sem("setup_transpose_read")

    def gpsimd(pool):
        base = Chain(pool, s_base)
        fills = [(m.ident, 0.0), (m.ones, 1.0), (m.upper, 1.0), (m.upper_strict, 1.0), (m.lower, 1.0),
                 (m.halves, 0.0), (m.pair_mask[:, 0, :], 0.0), (m.eps_mem[:, 0:1], LN_EPS),
                 (m.eps_mem[:, 1:2], NORM_EPS), (m.eps_mem[:, 2:3], LNX_EPS), (m.eps_mem[:, 3:4], RMS_EPS),
                 (m.eps_mem[:, 4:5], 1.0), (m.pair_mask[:, 1:8, :], 0.0)]
        for ap, v in fills:
            base.mark(pool.memset(ap, v))
        base.wait()
        cut = Chain(pool, s_sel)
        cut.mark(pool.affine_select(out=m.ident[:, :], in_=m.ident[:, :], compare_op=ALU.not_equal, fill=1.0, base=0,
                                    pattern=[[-1, P]], channel_multiplier=1))
        for t, sign, b in ((m.upper, 1, 0), (m.upper_strict, 1, -1), (m.lower, -1, 0)):
            cut.mark(pool.affine_select(out=t[:, :], in_=t[:, :], compare_op=ALU.is_ge, fill=0.0, base=b,
                                        pattern=[[sign, P]], channel_multiplier=-sign))
        cut.wait()
        cut(pool.memset(m.halves[0:64, 0:64], 1.0))
        cut(pool.memset(m.halves[64:P, 64:P], 1.0))
        for n in range(8):
            b = 1 if n == 0 else 2 ** (n - 1)
            half = 1 if n == 0 else 0
            part = m.pair_mask[:, n, :].rearrange("p (q h r) -> p q h r", h=2, r=b)[:, :, half, :]
            lo = 0 if n == 0 else b
            cut(pool.memset(part, 1.0))
            cut(pool.affine_select(out=part, in_=part, compare_op=ALU.is_ge, fill=0.0, base=-lo,
                                   pattern=[[-2 * b, P // (2 * b)], [0, b]], channel_multiplier=1))
            cut(pool.affine_select(out=part, in_=part, compare_op=ALU.is_ge, fill=0.0, base=lo + b - 1,
                                   pattern=[[2 * b, P // (2 * b)], [0, b]], channel_multiplier=-1))

    def scalar(act):
        at = 0
        for name, n in ROWS:
            act.dma_start(m.par_rows[at:at + n, 0, :], a[name].rearrange("(r c) -> r c", c=P)).then_inc(s_par, 16)
            at += n
        act.dma_start(m.par_rows[:, 1, :], a["conv_w"].rearrange("j (r c) -> (j r) c", c=P)).then_inc(s_par, 16)
        for n, ap in enumerate((a["dt_bias"], a["a_log"], a["ssm_d"])):
            act.dma_start(m.head_rows[:, n, :], ap.partition_broadcast(P)).then_inc(s_par, 16)
        for n in range(2 * NT):
            act.wait_ge(s_tr, n + 1)
            t, j = n // 2, n % 2
            act.activation(m.xT[:, 4 * j:4 * j + 4, t * P:(t + 1) * P],
                           kit.psum[:, n % 4, :].rearrange("p (q c) -> p q c", q=4), ACT.Copy).then_inc(s_tf, 1)
        act.wait_ge(s_tr, 2 * NT + 1)
        nrow = sum(n for _, n in ROWS)
        act.activation(m.par_cols[:, 0, 0:nrow], kit.psum[:, 4, 0:nrow], ACT.Copy)
        act.activation(m.par_cols[:, 1, :], kit.psum[:, 4, P:2 * P], ACT.Copy)

    def tensor(pe):
        pe.wait_ge(s_sel, 1)
        for n in range(2 * NT):
            t, j = n // 2, n % 2
            if j == 0:
                pe.wait_ge(m.x_landed[t], 16)
            if n >= 4:
                pe.wait_ge(s_tf, n - 3)
            for q in range(4):
                mm = pe.transpose(kit.psum[:, n % 4, q * P:(q + 1) * P], m.h[:, t, (4 * j + q) * P:(4 * j + q + 1) * P],
                                  m.ident[:, :])
            mm.then_inc(s_tr, 1)
        pe.wait_ge(s_par, 16 * (len(ROWS) + 4))
        nrow = sum(n for _, n in ROWS)
        pe.transpose(kit.psum[:, 4, 0:nrow], m.par_rows[0:nrow, 0, :], m.ident[0:nrow, 0:nrow])
        pe.transpose(kit.psum[:, 4, P:2 * P], m.par_rows[:, 1, :], m.ident[:, :]).then_inc(s_tr, 1)

    def vector(dve):
        pass

    return tensor, vector, scalar, gpsimd


def mamba_in(nc, kit, m, a):
    g = Gemm(kit, a["w_in"], KD, D_INNER, XBC, True)
    gd = Gemm(kit, a["w_in"], KD, D_INNER + XBC, SSM_HEADS, False)
    s_conv = kit.sem("conv_ready")
    s_dt = kit.sem("dt_raw_ready")
    s_abs = kit.sem("dt_abs_ready")
    s_exp = kit.sem("dt_exp_step")

    def tensor(pe):
        g.tensor(pe, m.xT)
        gd.tensor(pe, m.xT)

    def vector(dve):
        step = kit.vector_chain(dve)
        for n in range(XBC_TILES):
            ps = g.wait_tile(dve, n)
            acc = m.xbcF[:, n, :]
            w = [m.par_cols[:, 1, j * XBC_TILES + n:j * XBC_TILES + n + 1] for j in range(D_CONV)]
            step(dve.tensor_scalar(acc, ps, w[3], m.col("conv_b", n), ALU.mult, ALU.add))
            for d in (1, 2):
                step(dve.scalar_tensor_tensor(out=acc[:, d:], in0=ps[:, :SEQ - d], scalar=w[3 - d], in1=acc[:, d:],
                                              op0=ALU.mult, op1=ALU.add))
            dve.scalar_tensor_tensor(out=acc[:, 3:], in0=ps[:, :SEQ - 3], scalar=w[0], in1=acc[:, 3:],
                                     op0=ALU.mult, op1=ALU.add).then_inc(kit.tile_free, 1)
        for t in range(NT):
            ps = gd.wait_tile(dve, t)
            dve.tensor_tensor(m.dt_raw[:, t, :], ps[:, 0:SSM_HEADS], m.head_rows[:, 0, :], ALU.add)\
               .then_inc(kit.tile_free, 1)
        dve.wait_ge(kit.tile_free, gd.tile0 + gd.count)
        dve.scalar_tensor_tensor(out=m.dt_abs[:, :, :], in0=m.dt_raw[:, :, :], scalar=-1.0, in1=m.dt_raw[:, :, :],
                                 op0=ALU.mult, op1=ALU.max).then_inc(s_abs, 1)
        dve.wait_ge(s_exp, 3)
        step(dve.scalar_tensor_tensor(out=m.dt[:, :, :], in0=m.dt_raw[:, :, :], scalar=0.0, in1=m.dt_abs[:, :, :],
                                      op0=ALU.max, op1=ALU.add))
        dve.scalar_tensor_tensor(out=m.da[:, :, :], in0=m.dt[:, :, :], scalar=-1.0,
                                 in1=across(m.head_rows[:, 1, :], NT), op0=ALU.mult, op1=ALU.mult)

    def scalar(act):
        for n in range(XBC_TILES):
            act.wait_ge(kit.tile_free, g.tile0 + n + 1)
            act.activation(m.xbcF[:, n, :], m.xbcF[:, n, :], ACT.Silu)
        act.activation(m.head_rows[:, 1, :], m.head_rows[:, 1, :], ACT.Exp).then_inc(s_exp, 1)
        act.wait_ge(s_abs, 1)
        act.activation(m.dt_abs[:, :, :], m.dt_abs[:, :, :], ACT.Exp, scale=-1.0).then_inc(s_exp, 1)
        act.wait_ge(s_exp, 2)
        act.activation(m.dt_abs[:, :, :], m.dt_abs[:, :, :], ACT.Ln, bias=m.one).then_inc(s_exp, 1)

    return tensor, vector, scalar, None


def mamba_turn(nc, kit, m, a):
    s_tr = kit.sem("xb_transposed")
    s_tf = kit.sem("xb_transpose_read")
    s_cs = kit.sem("decay_sums_ready")
    s_sum = kit.sem("decay_sums_read")
    s_cr = kit.sem("decay_sums_read_by_scalar")
    s_exp = kit.sem("decay_exp_step")
    s_xr = kit.sem("x_tokens_ready")
    GRP = (X_TILES + SSM_GROUPS) // 4

    def tensor(pe):
        for c in range(NT):
            pe.matmul(kit.psum[:, 6, c * 32:c * 32 + 32], m.upper[:, :], m.da[:, c, :], start=True, stop=True)
            mm = pe.matmul(kit.psum[:, 7, c * 32:c * 32 + 32], m.ones[:, :], m.da[:, c, :], start=True, stop=True)
        mm.then_inc(s_cs, 1)
        for n in range(NT * GRP):
            c, j = n // GRP, n % GRP
            if n >= 6:
                pe.wait_ge(s_tf, n - 5)
            for q in range(4):
                mm = pe.transpose(kit.psum[:, n % 6, q * P:(q + 1) * P], m.xbcF[:, 4 * j + q, c * P:(c + 1) * P],
                                  m.ident[:, :])
            mm.then_inc(s_tr, 1)

    def scalar(act):
        act.wait_ge(s_cs, 1)
        cs, end = kit.psum[:, 6, 0:P], kit.psum[:, 7, 0:P]
        act.activation(m.ncs[:, :, :].rearrange("p a b -> p (a b)"), cs, ACT.Copy, scale=-1.0)
        act.activation(m.ecs[:, :, :].rearrange("p a b -> p (a b)"), cs, ACT.Exp)
        act.activation(m.eend[:, :, :].rearrange("p a b -> p (a b)"), end, ACT.Exp).then_inc(s_cr, 1)
        for n in range(NT * GRP):
            c, j = n // GRP, n % GRP
            act.wait_ge(s_tr, n + 1)
            dst = m.xT_tok[:, c, j * WIDE:(j + 1) * WIDE] if j < X_TILES // 4 else \
                m.bTok[:, c, (j - X_TILES // 4) * WIDE:(j - X_TILES // 4 + 1) * WIDE]
            act.activation(dst, kit.psum[:, n % 6, :], ACT.Copy).then_inc(s_tf, 1)
        act.wait_ge(s_sum, 1)
        act.activation(m.wend[:, :, :], m.wend[:, :, :], ACT.Exp)

    def vector(dve):
        step = kit.vector_chain(dve)
        dve.wait_ge(s_cr, 1)
        w = m.wend[:, :, :].rearrange("p a b -> p (a b)")
        step(dve.tensor_copy(w, kit.psum[:, 7, 0:P]))
        dve.tensor_tensor(w, w, kit.psum[:, 6, 0:P], ALU.subtract).then_inc(s_sum, 1)
        dve.wait_ge(s_tf, NT * GRP)
        for c in range(NT):
            x = m.xT_tok[:, c, :].rearrange("p (h d) -> p h d", d=64)
            step(dve.tensor_tensor(m.y[:, c, :].rearrange("p (h d) -> p h d", d=64), x,
                                   over(m.head_rows[:, 2, :], 64), ALU.mult))
            dve.tensor_tensor(x, x, over(m.dt[:, c, :], 64), ALU.mult)

    return tensor, vector, scalar, None


def mamba_scan(nc, kit, m, a):
    s_cb = kit.sem("cb_and_sums_ready")
    s_d = kit.sem("log_decay_ready")
    s_e = kit.sem("decay_matrix_ready")
    s_cut = kit.sem("decay_matrix_causal")
    s_mix = kit.sem("mix_matrix_ready")
    s_xw = kit.sem("x_to_state_ready")
    s_y = kit.sem("chunk_products_ready")
    s_fold = kit.sem("chunk_products_read")
    STEPS = NT * SSM_GROUPS
    GW = HPG * 64

    def tensor(pe):
        def first(i):
            c, g = i // SSM_GROUPS, i % SSM_GROUPS
            blk = slice(c * P, (c + 1) * P)
            if i >= 2:
                pe.wait_ge(s_mix, i - 1)
                pe.wait_ge(s_e, i - 1)
            pe.matmul(kit.psum[:, i % 2, 0:P], m.xbcF[:, X_TILES + g, blk], m.xbcF[:, X_TILES + SSM_GROUPS + g, blk],
                      start=True, stop=True)
            for r in range(HPG):
                h = g * HPG + r
                mm = pe.matmul(kit.psum[:, 2 + i % 2, r * P:(r + 1) * P], m.da[:, c, h:h + 1].broadcast_to([P, P]),
                               m.upper[:, :], start=True, stop=True)
            mm.then_inc(s_cb, 1)

        def second(i):
            c, g = i // SSM_GROUPS, i % SSM_GROUPS
            blk = slice(c * P, (c + 1) * P)
            if i >= 2:
                pe.wait_ge(s_fold, i - 1)
            yb = kit.psum[:, 4 + i % 2, :]
            pe.wait_ge(s_mix, i + 1)
            for r in range(HPG):
                h = g * HPG + r
                mm = pe.matmul(yb[:, r * 64:(r + 1) * 64], m.mix[:, i % 2, r, :],
                               m.xT_tok[:, c, h * 64:(h + 1) * 64], start=True, stop=True)
            if c > 0:
                pe.wait_ge(s_fold, i - SSM_GROUPS + 1)
                mm = pe.matmul(yb[:, GW:2 * GW], m.xbcF[:, X_TILES + SSM_GROUPS + g, blk], m.state[:, g, :],
                               start=True, stop=True)
            if c < NT - 1:
                pe.wait_ge(s_xw, i + 1)
                mm = pe.matmul(kit.psum[:, 6 + i % 2, 0:GW], m.bTok[:, c, g * P:(g + 1) * P], m.xw[:, i % 2, :],
                               start=True, stop=True)
            mm.then_inc(s_y, 1)

        for i in range(STEPS + 1):
            if i < STEPS:
                first(i)
            if i >= 1:
                second(i - 1)

    def scalar(act):
        for i in range(STEPS):
            c, g = i // SSM_GROUPS, i % SSM_GROUPS
            act.wait_ge(s_d, i + 1)
            act.activation(m.decay[:, i % 2], m.decay[:, i % 2], ACT.Exp).then_inc(s_e, 1)

    def gpsimd(pool):
        for i in range(STEPS):
            c, g = i // SSM_GROUPS, i % SSM_GROUPS
            if c < NT - 1:
                if i >= 2:
                    pool.wait_ge(s_y, i - 1)
                pool.tensor_tensor(m.xw[:, i % 2, :].rearrange("p (h d) -> p h d", d=64),
                                   m.xT_tok[:, c, g * GW:(g + 1) * GW].rearrange("p (h d) -> p h d", d=64),
                                   over(m.wend[:, c, g * HPG:(g + 1) * HPG], 64), ALU.mult).then_inc(s_xw, 1)
            pool.wait_ge(s_e, i + 1)
            e = m.decay[:, i % 2]
            pool.affine_select(out=e, in_=e, compare_op=ALU.is_ge, fill=0.0, base=0,
                               pattern=[[0, HPG], [1, P]], channel_multiplier=-1).then_inc(s_cut, 1)

    def vector(dve):
        st = kit.vector_chain(dve)

        def sums(i):
            c, g = i // SSM_GROUPS, i % SSM_GROUPS
            dve.wait_ge(s_cb, i + 1)
            if i >= 2:
                dve.wait_ge(s_y, i - 1)
            for r in range(HPG):
                ins = dve.tensor_scalar(m.decay[:, i % 2, r, :], kit.psum[:, 2 + i % 2, r * P:(r + 1) * P],
                                        m.ncs[:, c, g * HPG + r:g * HPG + r + 1], 0.0, ALU.add, ALU.min)
            ins.then_inc(s_d, 1)

        def mix(i):
            dve.wait_ge(s_cut, i + 1)
            dve.tensor_tensor(m.mix[:, i % 2], m.decay[:, i % 2], across(kit.psum[:, i % 2, 0:P], HPG), ALU.mult)\
               .then_inc(s_mix, 1)

        def fold(i):
            c, g = i // SSM_GROUPS, i % SSM_GROUPS
            dve.wait_ge(s_y, i + 1)
            y = m.y[:, c, g * GW:(g + 1) * GW]
            yb = kit.psum[:, 4 + i % 2, :]
            st(dve.tensor_tensor(y, y, yb[:, 0:GW], ALU.add))
            if c > 0:
                st(dve.tensor_tensor(m.ytmp[:, :].rearrange("p (h d) -> p h d", d=64),
                                     yb[:, GW:2 * GW].rearrange("p (h d) -> p h d", d=64),
                                     over(m.ecs[:, c, g * HPG:(g + 1) * HPG], 64), ALU.mult))
                ins = dve.tensor_tensor(y, y, m.ytmp[:, :], ALU.add)
                if c < NT - 1:
                    st(ins)
                    s = m.state[:, g, :].rearrange("p (h d) -> p h d", d=64)
                    st(dve.tensor_tensor(s, s, over(m.eend[:, c, g * HPG:(g + 1) * HPG], 64), ALU.mult))
                    ins = dve.tensor_tensor(m.state[:, g, :], m.state[:, g, :], kit.psum[:, 6 + i % 2, 0:GW], ALU.add)
            else:
                ins = dve.tensor_copy(m.state[:, g, :], kit.psum[:, 6 + i % 2, 0:GW])
            ins.then_inc(s_fold, 1)

        for i in range(STEPS + 1):
            if i == 0:
                sums(0)
            if i < STEPS:
                mix(i)
            if i >= 1:
                fold(i - 1)
            if i + 1 < STEPS:
                sums(i + 1)

    return tensor, vector, scalar, gpsimd


def mamba_gate(nc, kit, m, a):
    g = Gemm(kit, a["w_in"], KD, 0, D_INNER, False)
    s_silu = kit.sem("silu_z_ready")
    s_gated = kit.sem("gated_ready")
    s_ss = kit.sem("squares_summed")
    s_std = kit.sem("group_deviation_ready")
    s_norm = kit.sem("y_normed")
    s_tr = kit.sem("y_transposed")
    s_tf = kit.sem("y_transpose_read")
    GW = D_INNER // SSM_GROUPS

    def tensor(pe):
        g.tensor(pe, m.xT)
        for n in range(X_TILES):
            if n == 0:
                pe.wait_ge(kit.tile_free, g.tile0 + g.count)
                pe.wait_ge(s_norm, NT)
            if n >= 4:
                pe.wait_ge(s_tf, n - 3)
            for c in range(NT):
                mm = pe.transpose(kit.psum[:, n % 4, c * P:(c + 1) * P], m.y[:, c, n * P:(n + 1) * P], m.ident[:, :])
            mm.then_inc(s_tr, 1)

    def scalar(act):
        for n in range(g.count):
            ps = g.wait_tile(act, n)
            if n >= 2:
                act.wait_ge(s_gated, n - 1)
            act.activation(m.gate_tmp[:, n % 2, :], ps, ACT.Silu).then_inc(kit.tile_free, 1)
        act.wait_ge(s_ss, 1)
        act.activation(m.gstd[:, :, :], m.gss[:, :, :], ACT.Sqrt, bias=m.eps["rms"], scale=1.0 / GW).then_inc(s_std, 1)

    def vector(dve):
        step = kit.vector_chain(dve)
        for n in range(g.count):
            j, t = n // NT, n % NT
            dve.wait_ge(kit.tile_free, g.tile0 + n + 1)
            y = m.y[:, t, j * WIDE:(j + 1) * WIDE]
            dve.tensor_tensor(y, y, m.gate_tmp[:, n % 2, :], ALU.mult).then_inc(s_gated, 1)
            dve.wait_ge(s_gated, n + 1)
            for q in range(2):
                yq = y[:, q * GW:(q + 1) * GW]
                step(dve.tensor_tensor_reduce(out=m.sq_tmp[:, 0:GW], in0=yq, in1=yq, scale=1.0, scalar=0.0,
                                              op0=ALU.mult, op1=ALU.add, accum_out=m.gss[:, t, 2 * j + q:2 * j + q + 1]))
        dve.engine_nop().then_inc(s_ss, 1)
        dve.wait_ge(s_std, 1)
        step(dve.reciprocal(m.gstd[:, :, :], m.gstd[:, :, :]))
        for t in range(NT):
            y = m.y[:, t, :].rearrange("p (g d) -> p g d", d=GW)
            dve.tensor_tensor(y, y, over(m.gstd[:, t, :], GW), ALU.mult).then_inc(s_norm, 1)
        for n in range(X_TILES):
            dve.wait_ge(s_tr, n + 1)
            dve.tensor_scalar(m.yF[:, n, :], kit.psum[:, n % 4, :], m.col("norm_w", n), None, ALU.mult)\
               .then_inc(s_tf, 1)

    def gpsimd(pool):
        pool.dma_start(m.h, a["x"].rearrange("b (t p) d -> (b p) t d", p=P)).then_inc(m.h_landed, 16)

    return tensor, vector, scalar, gpsimd


def mlp_up(nc, kit, m, w, tag):
    g = Gemm(kit, w, KD, 0, D_FF, True)
    s_sq = kit.sem(f"{tag}_squared")

    def tensor(pe):
        g.tensor(pe, m.xT)

    def vector(dve):
        for n in range(g.count):
            ps = g.wait_tile(dve, n)
            dve.tensor_scalar(m.hidden[:, n, :], ps, 0.0, None, ALU.max).then_inc(kit.tile_free, 1)

    def scalar(act):
        for n in range(g.count):
            act.wait_ge(kit.tile_free, g.tile0 + n + 1)
            act.activation(m.hidden[:, n, :], m.hidden[:, n, :], ACT.Square)

    return tensor, vector, scalar, None


def sb_project(nc, kit, m, a):
    gq = Gemm(kit, a["sb_w_q"], KD, 0, D, True)
    gk = Gemm(kit, a["sb_w_k"], KD, 0, D, True)
    gv = Gemm(kit, a["sb_w_v"], KD, 0, D, False)

    def tensor(pe):
        for g in (gq, gk, gv):
            g.tensor(pe, m.xT)

    def scalar(act):
        for g, dst in ((gq, m.qF), (gk, m.kF)):
            for n in range(g.count):
                ps = g.wait_tile(act, n)
                act.activation(dst[:, n, :], ps, ACT.Copy, scale=HD ** -0.5 if g is gq else 1.0)\
                   .then_inc(kit.tile_free, 1)
        for n in range(gv.count):
            ps = gv.wait_tile(act, n)
            act.activation(m.vTok[:, n % NT, (n // NT) * WIDE:(n // NT + 1) * WIDE], ps, ACT.Copy)\
               .then_inc(kit.tile_free, 1)

    return tensor, None, scalar, None


def sb_attend(nc, kit, m, a):
    s_z = kit.sem("sb_logits_ready")
    s_abs = kit.sem("sb_abs_ready")
    s_ln = kit.sem("sb_act_step")
    s_sp = kit.sem("sb_lo_raw")
    s_lo = kit.sem("sb_lo_ready")
    s_x = kit.sem("sb_exponent_ready")
    s_w = kit.sem("sb_weights_raw")
    s_cut = kit.sem("sb_weights_ready")
    s_o = kit.sem("sb_out_ready")
    s_of = kit.sem("sb_out_read")

    def q_from(b):
        return b * P

    def tensor(pe):
        for h in range(SB_HEADS):
            rows = slice((h % 2) * 64, (h % 2) * 64 + 64)
            if h >= 1:
                pe.wait_ge(s_w, NT * h)
            for b in range(NT):
                pe.matmul(kit.psum[:, b, q_from(b):], m.kF[rows, h // 2, b * P:(b + 1) * P],
                          m.qF[rows, h // 2, q_from(b):], start=True, stop=True, skip_group_check=True)\
                    .then_inc(s_z, 1)
            for b in reversed(range(NT)):
                pe.wait_ge(s_lo, NT * h + NT - b)
                for later in range(NT - 1, b, -1):
                    pe.matmul(kit.psum[:, b, q_from(later):], m.ones[:, :], m.lo[:, later, q_from(later):],
                              start=False, stop=False, skip_group_check=True)
                pe.matmul(kit.psum[:, b, q_from(b):], m.lower[:, :], m.lo[:, b, q_from(b):],
                          start=False, stop=True, skip_group_check=True).then_inc(s_x, 1)
            if h >= 2:
                pe.wait_ge(s_of, h - 1)
            o = kit.psum[rows, 4 + h % 2, :]
            pe.wait_ge(s_cut, NT * (h + 1))
            for b in range(NT):
                mm = pe.matmul(o[:, q_from(b):], m.vTok[:, b, h * 64:(h + 1) * 64], m.wt[:, b, q_from(b):],
                               start=(b == 0), stop=(b == NT - 1), skip_group_check=True)
            mm.then_inc(s_o, 1)

    def scalar(act):
        ln = Chain(act, s_ln)
        for h in range(SB_HEADS):
            for i, b in enumerate(reversed(range(NT))):
                n = NT * h + i
                act.wait_ge(s_abs, n + 1)
                t = m.sp[:, b, q_from(b):]
                ln(act.activation(t, t, ACT.Exp, scale=-1.0))
                act.activation(t, t, ACT.Ln, bias=m.one).then_inc(s_sp, 1)
            for i, b in enumerate(reversed(range(NT))):
                n = NT * h + i
                act.wait_ge(s_x, n + 1)
                if h >= 1:
                    act.wait_ge(s_o, h)
                act.activation(m.wt[:, b, q_from(b):], kit.psum[:, b, q_from(b):], ACT.Exp).then_inc(s_w, 1)
            if h >= 1:
                put(act, h - 1)
        put(act, SB_HEADS - 1)

    def put(act, h):
        rows = slice((h % 2) * 64, (h % 2) * 64 + 64)
        act.wait_ge(s_o, h + 1)
        act.activation(m.oF[rows, h // 2, :], kit.psum[rows, 4 + h % 2, :], ACT.Copy).then_inc(s_of, 1)

    def vector(dve):
        step = kit.vector_chain(dve)
        for h in range(SB_HEADS):
            for i, b in enumerate(reversed(range(NT))):
                z = kit.psum[:, b, q_from(b):]
                sp = m.sp[:, b, q_from(b):]
                dve.wait_ge(s_z, NT * h + b + 1)
                step(dve.tensor_scalar(sp, z, -1.0, None, ALU.mult))
                dve.tensor_tensor(sp, sp, z, ALU.max).then_inc(s_abs, 1)
            for i, b in enumerate(reversed(range(NT))):
                n = NT * h + i
                z = kit.psum[:, b, q_from(b):]
                sp = m.sp[:, b, q_from(b):]
                if h >= 1:
                    dve.wait_ge(s_x, NT * h)
                dve.wait_ge(s_sp, n + 1)
                step(dve.scalar_tensor_tensor(out=sp, in0=z, scalar=0.0, in1=sp, op0=ALU.max, op1=ALU.add))
                lo = m.lo[:, b, q_from(b):]
                if b < NT - 1:
                    step(dve.tensor_scalar(lo[:, P:], sp[:, P:], -1.0, None, ALU.mult))
                dve.scalar_tensor_tensor(out=lo[:, 0:P], in0=sp[:, 0:P], scalar=-1.0, in1=m.upper_strict[:, :],
                                         op0=ALU.mult, op1=ALU.mult).then_inc(s_lo, 1)

    def gpsimd(pool):
        for h in range(SB_HEADS):
            for i, b in enumerate(reversed(range(NT))):
                n = NT * h + i
                pool.wait_ge(s_w, n + 1)
                w = m.wt[:, b, q_from(b):q_from(b) + P]
                pool.affine_select(out=w, in_=w, compare_op=ALU.is_gt, fill=0.0, base=0, pattern=[[1, P]],
                                   channel_multiplier=-1).then_inc(s_cut, 1)

    return tensor, vector, scalar, gpsimd


def second_project(nc, kit, m, a):
    gr = Gemm(kit, a["w_in_2"], KD, 0, RW_COLS, True)
    ga = Gemm(kit, a["w_in_2"], KD, RW_COLS, 3 * ATT, False)
    gi = Gemm(kit, a["w_in_2"], KD, RW_COLS + 3 * ATT, IDXW, False)

    def tensor(pe):
        for g in (gr, ga, gi):
            g.tensor(pe, m.xT)

    def vector(dve):
        step = kit.vector_chain(dve)
        for n in range(gr.count):
            dve.wait_ge(kit.tile_free, gr.tile0 + n + 1)
            p, d = m.rwF[:, n, :], m.shift_tmp[:, n % 2, :]
            step(dve.tensor_tensor(d[:, 1:], p[:, :SEQ - 1], p[:, 1:], ALU.subtract))
            step(dve.tensor_scalar(d[:, 0:1], p[:, 0:1], -1.0, None, ALU.mult))
            step(dve.scalar_tensor_tensor(out=p, in0=d, scalar=m.col("mu", n), in1=p, op0=ALU.mult, op1=ALU.add))

    def scalar(act):
        for n in range(gr.count):
            ps = gr.wait_tile(act, n)
            act.activation(m.rwF[:, n, :], ps, ACT.Copy).then_inc(kit.tile_free, 1)
        for g, dst in ((ga, m.attTok), (gi, m.idxTok)):
            for n in range(g.count):
                w = g.parts[n // NT][0]
                ps = g.wait_tile(act, n)
                act.activation(dst[:, n % NT, (n // NT) * WIDE:(n // NT) * WIDE + w], ps[:, 0:w], ACT.Copy)\
                   .then_inc(kit.tile_free, 1)

    return tensor, vector, scalar, None


def rope_turn(nc, kit, m, a):
    s_rot = kit.sem("rotated")
    s_tr = kit.sem("rope_transposed")
    s_tf = kit.sem("rope_transpose_read")
    s_cs = kit.sem("rope_table_landed")
    JOBS = [("att", 0, 2 * NHEAD), ("idx", 0, NHEAD + 1)]

    def gpsimd(pool):
        pool.dma_start(m.rope[:, :, :], a["rope"].rearrange("(t p) c -> p t c", p=P)).then_inc(s_cs, 16)

    def vector(dve):
        step = kit.vector_chain(dve)
        dve.wait_ge(s_cs, 16)
        for t in range(NT):
            for src, n in ((m.attTok[:, t, 0:2 * ATT], 2 * NHEAD), (m.idxTok[:, t, 0:ATT + HD], NHEAD + 1)):
                x = src.rearrange("p (h s d) -> p h s d", s=2, d=HD // 2)
                x1, x2 = x[:, :, 0, :], x[:, :, 1, :]
                cos, sin = (across(m.rope[:, t, q * 32:(q + 1) * 32], n) for q in range(2))
                v = [m.rope_tmp[:, q, 0:n * 32].rearrange("p (h d) -> p h d", d=32) for q in range(2)]
                step(dve.tensor_tensor(v[0], x1, sin, ALU.mult))
                step(dve.tensor_tensor(v[1], x2, sin, ALU.mult))
                step(dve.tensor_tensor(x1, x1, cos, ALU.mult))
                step(dve.tensor_tensor(x2, x2, cos, ALU.mult))
                step(dve.tensor_tensor(x1, x1, v[1], ALU.subtract))
                ins = dve.tensor_tensor(x2, x2, v[0], ALU.add)
                step(ins)
            dve.engine_nop().then_inc(s_rot, 1)

    def tensor(pe):
        n = 0
        for t in range(NT):
            pe.wait_ge(s_rot, t + 1)
            for j in range(4):
                if n >= 4:
                    pe.wait_ge(s_tf, n - 3)
                for q in range(4):
                    k = 4 * j + q
                    if j < 2:
                        mm = pe.transpose(kit.psum[:, n % 4, q * P:(q + 1) * P], m.attTok[:, t, k * P:(k + 1) * P],
                                          m.ident[:, :])
                    elif j == 2:
                        mm = pe.transpose(kit.psum[:, n % 4, q * P:(q + 1) * P], m.idxTok[:, t, q * P:(q + 1) * P],
                                          m.ident[:, :])
                    elif q < 2:
                        if q == 0:
                            mm = pe.matmul(kit.psum[0:HD, n % 4, 0:P], m.idxTok[:, t, ATT:ATT + HD], m.ident[:, :],
                                           start=True, stop=True)
                        else:
                            mm = pe.matmul(kit.psum[64:P, n % 4, P:2 * P], m.idxTok[:, t, ATT:ATT + HD], m.ident[:, :],
                                           start=True, stop=True)
                mm.then_inc(s_tr, 1)
                n += 1

    def scalar(act):
        n = 0
        for t in range(NT):
            blk = slice(t * P, (t + 1) * P)
            for j in range(4):
                act.wait_ge(s_tr, n + 1)
                ps = kit.psum[:, n % 4, :]
                if j < 3:
                    dst = (m.attF[:, 0:4, blk], m.attF[:, 4:8, blk], m.idxF[:, 0:4, blk])[j]
                    act.activation(dst, ps.rearrange("p (q c) -> p q c", q=4), ACT.Copy,
                                   scale=HD ** -0.5 if j == 0 else 1.0).then_inc(s_tf, 1)
                else:
                    act.activation(m.idxF[0:HD, 4, blk], ps[0:HD, 0:P], ACT.Copy)
                    act.activation(m.idxF[64:P, 4, blk], ps[64:P, P:2 * P], ACT.Copy).then_inc(s_tf, 1)
                n += 1

    return tensor, vector, scalar, gpsimd


def sparse_attend(nc, kit, m, a):
    s_ix = kit.sem("index_products_ready")
    s_relu = kit.sem("index_relu_ready")
    s_acc = kit.sem("index_terms_added")
    s_fut = kit.sem("future_filled")
    s_mask = kit.sem("key_bias_ready")
    s_lg = kit.sem("logits_ready")
    s_lb = kit.sem("logits_biased")
    s_max = kit.sem("logit_max_ready")
    s_p = kit.sem("probabilities_ready")
    s_tr = kit.sem("probabilities_transposed")
    s_tc = kit.sem("probabilities_copied")
    s_o = kit.sem("sparse_out_ready")
    s_of = kit.sem("sparse_out_read")
    s_yt = kit.sem("sparse_out_transposed")
    IDX_SCALE = HD ** -0.5 * NHEAD ** -0.5

    def rows(h):
        return slice((h % 2) * 64, (h % 2) * 64 + 64)

    def tensor(pe):
        for t in range(NT):
            n = (t + 1) * P
            blk = slice(t * P, (t + 1) * P)
            for h in range(NHEAD):
                i = t * NHEAD + h
                if i >= 2:
                    pe.wait_ge(s_relu, i - 1)
                pe.matmul(kit.psum[:, i % 2, 0:n], m.idxF[rows(h), h // 2, blk], m.idxF[rows(h), 4, 0:n],
                          start=True, stop=True).then_inc(s_ix, 1)
            for h in range(NHEAD + 1):
                if h < NHEAD:
                    i = t * NHEAD + h
                    if i >= 2:
                        pe.wait_ge(s_lb, i - 1)
                    pe.matmul(kit.psum[:, 2 + i % 2, 0:n], m.attF[rows(h), h // 2, blk], m.attF[rows(h), 4 + h // 2, 0:n],
                              start=True, stop=True).then_inc(s_lg, 1)
                if h >= 1:
                    i = t * NHEAD + h - 1
                    pe.wait_ge(s_p, i + 1)
                    if i >= 2:
                        pe.wait_ge(s_tc, i - 1)
                    for b in range(t + 1):
                        mm = pe.transpose(kit.psum[:, 4 + i % 2, b * P:(b + 1) * P], m.prob[:, i % 2, b * P:(b + 1) * P],
                                          m.ident[:, :])
                    mm.then_inc(s_tr, 1)
                    pe.wait_ge(s_tc, i + 1)
                    if i >= 2:
                        pe.wait_ge(s_of, i - 1)
                    if t >= 1 and h == 1:
                        pe.wait_ge(s_yt, 2 * t)
                    for b in range(t + 1):
                        mm = pe.matmul(kit.psum[:, 6 + i % 2, (h - 1) * 64:h * 64], m.probT[:, i % 2, b * P:(b + 1) * P],
                                       m.attTok[:, b, 2 * ATT + (h - 1) * 64:2 * ATT + h * 64],
                                       start=(b == 0), stop=(b == t))
                    mm.then_inc(s_o, 1)
            pe.wait_ge(s_of, (t + 1) * NHEAD)
            for q in range(NHP):
                mm = pe.transpose(kit.psum[:, 6, q * P:(q + 1) * P], m.ybTok[:, q * P:(q + 1) * P], m.ident[:, :])
            mm.then_inc(s_yt, 1)

    def scalar(act):
        for t in range(NT):
            n = (t + 1) * P
            for h in range(NHEAD):
                i = t * NHEAD + h
                act.wait_ge(s_ix, i + 1)
                if i >= 2:
                    act.wait_ge(s_acc, i - 1)
                act.activation(m.relu[:, i % 2, 0:n], kit.psum[:, i % 2, 0:n], ACT.Relu).then_inc(s_relu, 1)
            for h in range(NHEAD + 1):
                if h < NHEAD:
                    i = t * NHEAD + h
                    act.wait_ge(s_max, i + 1)
                    if i >= 2:
                        act.wait_ge(s_tr, i - 1)
                    act.activation(m.prob[:, i % 2, 0:n], m.lgt[:, i % 2, 0:n], ACT.Exp, bias=m.nmax[:, i % 2, :],
                                   accum_out=m.psum_row[:, i % 2, :]).then_inc(s_p, 1)
                if h >= 1:
                    i = t * NHEAD + h - 1
                    act.wait_ge(s_tr, i + 1)
                    if i >= 2:
                        act.wait_ge(s_o, i - 1)
                    act.activation(m.probT[:, i % 2, 0:n], kit.psum[:, 4 + i % 2, 0:n], ACT.Copy).then_inc(s_tc, 1)
            act.wait_ge(s_yt, 2 * t + 1)
            act.activation(m.ybF[:, :, t * P:(t + 1) * P], kit.psum[:, 6, :].rearrange("p (q c) -> p q c", q=NHP),
                           ACT.Copy).then_inc(s_yt, 1)

    def gpsimd(pool):
        for t in range(NT):
            n = (t + 1) * P
            pool.wait_ge(s_acc, (t + 1) * NHEAD)
            pool.affine_select(out=m.score[:, t * P:n], in_=m.score[:, t * P:n], compare_op=ALU.is_ge, fill=FUTURE,
                               base=0, pattern=[[-1, P]], channel_multiplier=1).then_inc(s_fut, 1)

    def vector(dve):
        step = kit.vector_chain(dve)
        for t in range(NT):
            n = (t + 1) * P
            sc = m.score[:, 0:n]
            for h in range(NHEAD):
                i = t * NHEAD + h
                dve.wait_ge(s_relu, i + 1)
                r, w = m.relu[:, i % 2, 0:n], m.idxTok[:, t, ATT + HD + h:ATT + HD + h + 1]
                if h == 0:
                    dve.tensor_scalar(sc, r, w, 0.0, ALU.mult, ALU.add).then_inc(s_acc, 1)
                else:
                    dve.wait_ge(s_acc, i)
                    dve.scalar_tensor_tensor(out=sc, in0=r, scalar=w, in1=sc, op0=ALU.mult, op1=ALU.add)\
                       .then_inc(s_acc, 1)
            dve.wait_ge(s_fut, t + 1)
            if n > TOPK:
                step(dve.tensor_scalar(m.work[:, 0:n], sc, IDX_SCALE, None, ALU.mult))
                wk = m.work[:, 0:n]
                for _ in range(TOPK // 8):
                    step(dve.max(m.best[:, :], wk))
                    step(dve.match_replace(wk, m.best[:, :], wk, REMOVED))
                step(dve.tensor_scalar(wk, wk, REMOVED, None, ALU.is_equal))
                step(dve.tensor_scalar(sc, sc, FUTURE / 2, None, ALU.is_ge))
                step(dve.tensor_tensor(sc, sc, wk, ALU.mult))
            else:
                step(dve.tensor_scalar(sc, sc, FUTURE / 2, None, ALU.is_ge))
            step(dve.tensor_scalar(sc, sc, -FUTURE, FUTURE, ALU.mult, ALU.add))
            for h in range(NHEAD + 1):
                if h < NHEAD:
                    i = t * NHEAD + h
                    dve.wait_ge(s_lg, i + 1)
                    if i >= 2:
                        dve.wait_ge(s_p, i - 1)
                    lg = m.lgt[:, i % 2, 0:n]
                    dve.tensor_tensor(lg, kit.psum[:, 2 + i % 2, 0:n], sc, ALU.add).then_inc(s_lb, 1)
                    dve.wait_ge(s_lb, i + 1)
                    dve.tensor_reduce(m.nmax[:, i % 2, :], lg, AX_X, ALU.max, negate=True).then_inc(s_max, 1)
                if h >= 1:
                    i = t * NHEAD + h - 1
                    dve.wait_ge(s_p, i + 1)
                    step(dve.reciprocal(m.prec[:, i % 2, :], m.psum_row[:, i % 2, :]))
                    dve.wait_ge(s_o, i + 1)
                    if t >= 1 and h == 1:
                        dve.wait_ge(s_yt, 2 * t - 1)
                    dve.tensor_scalar(m.ybTok[:, (h - 1) * 64:h * 64], kit.psum[:, 6 + i % 2, (h - 1) * 64:h * 64],
                                      m.prec[:, i % 2, :], None, ALU.mult).then_inc(s_of, 1)

    return tensor, vector, scalar, gpsimd


def rwkv_prepare(nc, kit, m, a):
    s_up = kit.sem("lora_weights_landed")
    s_lin = kit.sem("lora_inputs_ready")
    s_lo = kit.sem("lora_products_ready")
    s_act = kit.sem("lora_products_read")
    s_kk = kit.sem("key_squares_ready")
    s_kn = kit.sem("key_norm_sums_ready")
    s_kr = kit.sem("key_norm_root")
    s_bo = kit.sem("bonus_terms_ready")
    s_bp = kit.sem("bonus_sums_ready")
    s_cs = kit.sem("decay_scan_ready")
    s_ex = kit.sem("decay_factors_ready")

    def gpsimd(pool):
        pool.dma_start(m.up_w[0:64, 0, :], a["w_decay_up"]).then_inc(s_up, 16)
        pool.dma_start(m.up_w[64:P, 0, :], a["a_up"]).then_inc(s_up, 16)
        pool.dma_start(m.up_w[:, 1, :], a["g_up"]).then_inc(s_up, 16)

    def tensor(pe):
        pe.wait_ge(s_up, 48)
        pe.wait_ge(s_lin, 2)
        for n in range(3 * NHP):
            kind, t = n // NHP, n % NHP
            if n >= 4:
                pe.wait_ge(s_act, n - 3)
            f = slice(t * P, (t + 1) * P)
            if kind == 0:
                mm = pe.matmul(kit.psum[:, n % 4, :], m.up_w[0:64, 0, f], m.rwF[0:64, 12, :], start=True, stop=True)
            elif kind == 1:
                mm = pe.matmul(kit.psum[:, n % 4, :], m.up_w[64:P, 0, f], m.rwF[64:P, 12, :], start=True, stop=True)
            else:
                mm = pe.matmul(kit.psum[:, n % 4, :], m.up_w[:, 1, f], m.rwF[:, 13, :], start=True, stop=True)
            mm.then_inc(s_lo, 1)
        for t in range(NHP):
            pe.wait_ge(s_kk, t + 1)
            pe.matmul(kit.psum[:, 4 + t, :], m.halves[:, :], m.sqF[:, t, :], start=True, stop=True).then_inc(s_kn, 1)
        for t in range(NHP):
            pe.wait_ge(s_bo, t + 1)
            pe.matmul(kit.psum[:, t, :], m.halves[:, :], m.sqF[:, t, :], start=True, stop=True).then_inc(s_bp, 1)

    def scalar(act):
        act.activation(m.rwF[0:64, 12, :], m.rwF[0:64, 12, :], ACT.Tanh).then_inc(s_lin, 1)
        act.activation(m.rwF[:, 13, :], m.rwF[:, 13, :], ACT.Sigmoid).then_inc(s_lin, 1)
        for n in range(3 * NHP):
            kind, t = n // NHP, n % NHP
            act.wait_ge(s_lo, n + 1)
            ps = kit.psum[:, n % 4, :]
            if kind == 0:
                act.activation(m.sg[:, t, :], ps, ACT.Sigmoid, bias=m.col("w0", t)).then_inc(s_act, 1)
            elif kind == 1:
                act.activation(m.aF[:, t, :], ps, ACT.Sigmoid, bias=m.col("a0", t)).then_inc(s_act, 1)
            else:
                act.activation(m.gF[:, t, :], ps, ACT.Copy).then_inc(s_act, 1)
        for t in range(NHP):
            act.wait_ge(s_kn, t + 1)
            act.activation(m.sqF[:, t, :], kit.psum[:, 4 + t, :], ACT.Sqrt).then_inc(s_kr, 1)
        for t in range(NHP):
            for c in range(NT):
                n = NT * t + c
                act.wait_ge(s_cs, n + 1)
                blk = slice(c * P, (c + 1) * P)
                mid, nmid = m.mid[:, 0, n:n + 1], m.mid[:, 1, n:n + 1]
                act.activation(m.eF[:, 0, n % 2, :], m.prev_cs[:, n % 2, :], ACT.Exp, bias=mid, scale=-DECAY_UNIT)
                act.activation(m.eF[:, 1, n % 2, :], m.cs[:, n % 2, :], ACT.Exp, bias=mid, scale=-DECAY_UNIT)
                act.activation(m.eF[:, 2, n % 2, :], m.cs[:, n % 2, :], ACT.Exp, bias=nmid, scale=DECAY_UNIT)
                act.activation(m.emid[:, c, t:t + 1], nmid, ACT.Exp).then_inc(s_ex, 1)

    def vector(dve):
        step = kit.vector_chain(dve)
        dve.wait_ge(s_act, 2 * NHP)
        for t in range(NHP):
            k, kk = m.rwF[:, 4 + t, :], m.kkF[:, t, :]
            step(dve.tensor_scalar(kk, k, m.col("k_k", t), None, ALU.mult))
            dve.tensor_tensor(m.sqF[:, t, :], kk, kk, ALU.mult).then_inc(s_kk, 1)
        for t in range(NHP):
            k, ae = m.rwF[:, 4 + t, :], m.tmpF[:, 0, :]
            step(dve.tensor_scalar(ae, m.aF[:, t, :], -1.0, m.col("k_a", t), ALU.add, ALU.mult))
            step(dve.scalar_tensor_tensor(out=k, in0=ae, scalar=1.0, in1=k, op0=ALU.add, op1=ALU.mult))
            dve.wait_ge(s_kr, t + 1)
            nrm = m.sqF[:, t, :]
            step(dve.tensor_scalar(nrm, nrm, 1e-12, None, ALU.max))
            step(dve.reciprocal(nrm, nrm))
            step(dve.tensor_tensor(m.kkF[:, t, :], m.kkF[:, t, :], nrm, ALU.mult))
            step(dve.tensor_tensor(m.aF[:, t, :], m.aF[:, t, :], m.kkF[:, t, :], ALU.mult))
            step(dve.tensor_tensor(m.tmpF[:, 0, :], m.rwF[:, t, :], k, ALU.mult))
            dve.tensor_scalar(m.sqF[:, t, :], m.tmpF[:, 0, :], m.col("r_k", t), None, ALU.mult).then_inc(s_bo, 1)
            dve.wait_ge(s_bo, t + 1)
        for t in range(NHP):
            dve.wait_ge(s_bp, t + 1)
            step(dve.tensor_tensor(m.bonus[:, t, :], m.rwF[:, 8 + t, :], kit.psum[:, t, :], ALU.mult))

        def scan(n):
            t, c = n // NT, n % NT
            sg = m.sg[:, t, c * P:(c + 1) * P]
            if n >= 2:
                dve.wait_ge(s_ex, n - 1)
            cs = m.cs[:, n % 2, :]
            step(dve.tensor_tensor_scan(cs, m.ones[:, :], sg, 0.0, ALU.mult, ALU.add))
            step(dve.tensor_tensor(m.prev_cs[:, n % 2, :], cs, sg, ALU.subtract))
            step(dve.tensor_scalar(m.mid[:, 0, n:n + 1], cs[:, P - 1:P], DECAY_UNIT / 2, None, ALU.mult))
            dve.tensor_scalar(m.mid[:, 1, n:n + 1], cs[:, P - 1:P], -DECAY_UNIT / 2, None, ALU.mult).then_inc(s_cs, 1)

        def scale(n):
            t, c = n // NT, n % NT
            blk = slice(c * P, (c + 1) * P)
            dve.wait_ge(s_ex, n + 1)
            e = [m.eF[:, q, n % 2, :] for q in range(3)]
            for x, f in ((m.kkF, e[0]), (m.rwF, e[1]), (m.aF, e[2])):
                step(dve.tensor_tensor(x[:, t, blk], x[:, t, blk], f, ALU.mult))
            k = m.rwF[:, 4 + t, blk]
            step(dve.tensor_tensor(k, k, e[2], ALU.mult))

        for n in range(NT * NHP + 1):
            if n < NT * NHP:
                scan(n)
            if n >= 1:
                scale(n - 1)

    return tensor, vector, scalar, gpsimd


def rwkv_scan(nc, kit, m, a):
    s_tt = kit.sem("chunk_turned")
    s_tr = kit.sem("chunk_turn_read")
    s_pr = kit.sem("pair_products_ready")
    s_pm = kit.sem("pair_products_masked")
    s_lm = kit.sem("level_matrix_ready")
    s_u = kit.sem("level_u_ready")
    s_uc = kit.sem("level_u_copied")
    s_dl = kit.sem("level_change_ready")
    s_xy = kit.sem("inverse_updated")
    s_d = kit.sem("value_mix_ready")
    s_dc = kit.sem("value_mix_copied")
    s_w = kit.sem("wy_products_ready")
    s_wc = kit.sem("wy_products_copied")
    s_z = kit.sem("state_reads_ready")
    s_sa = kit.sem("corrections_ready")
    s_n = kit.sem("new_state_ready")
    s_st = kit.sem("state_scaled")
    s_y = kit.sem("recurrent_out_ready")
    s_yc = kit.sem("recurrent_out_read")
    LEVELS = 7

    def rows(g):
        return slice(g * 64, g * 64 + 64)

    def quad(bank):
        return kit.psum[:, bank, :].rearrange("p (q c) -> p q c", q=NHP)

    kap = lambda g, q, blk: m.kkF[rows(g), q, blk]
    rho = lambda g, q, blk: m.rwF[rows(g), q, blk]
    bet = lambda g, q, blk: m.aF[rows(g), q, blk]
    gam = lambda g, q, blk: m.rwF[rows(g), 4 + q, blk]
    PAIRS = [(kap, bet), (bet, kap), (gam, kap), (bet, rho), (gam, rho)]

    def tensor(pe):
        for c in range(NT):
            blk = slice(c * P, (c + 1) * P)
            if c >= 1:
                pe.wait_ge(s_yc, 2 * c)
            for n, src in enumerate((m.kkF, m.aF, m.rwF, m.rwF)):
                off = (0, 0, 4, 8)[n]
                for q in range(NHP):
                    mm = pe.transpose(kit.psum[:, n, q * P:(q + 1) * P], src[:, off + q, blk], m.ident[:, :])
                mm.then_inc(s_tt, 1)
            if c >= 1:
                pe.wait_ge(s_st, c)
            for n, (left, right) in enumerate(PAIRS):
                for g in range(2):
                    k = 2 * n + g
                    if k >= 4:
                        pe.wait_ge(s_pm, 10 * c + k - 3)
                    for q in range(NHP):
                        mm = pe.matmul(kit.psum[:, 4 + k % 4, q * P:(q + 1) * P], left(g, q, blk), right(g, q, blk),
                                       start=True, stop=True)
                    mm.then_inc(s_pr, 1)
            pe.wait_ge(s_tr, 4 * (c + 1))
            pe.wait_ge(s_pm, 10 * (c + 1))
            for lv in range(1, LEVELS):
                for g in range(2):
                    i = (c * (LEVELS - 1) + lv - 1) * 2 + g
                    pe.wait_ge(s_lm, i + 1)
                    pe.wait_ge(s_xy, (c * LEVELS + lv - 1) * 2 + g + 1)
                    for q in range(NHP):
                        mm = pe.matmul(kit.psum[:, g, q * P:(q + 1) * P], m.level[:, g, q, :], m.X[:, g, q, :],
                                       start=True, stop=True)
                    mm.then_inc(s_u, 1)
                for g in range(2):
                    i = (c * (LEVELS - 1) + lv - 1) * 2 + g
                    pe.wait_ge(s_uc, i + 1)
                    for q in range(NHP):
                        mm = pe.matmul(kit.psum[:, 2 + g, q * P:(q + 1) * P], m.Y[:, g, q, :], m.U[:, g, q, :],
                                       start=True, stop=True)
                    if lv < LEVELS - 1:
                        for q in range(NHP):
                            mm = pe.matmul(kit.psum[:, 4 + g, q * P:(q + 1) * P], m.U[:, g, q, :], m.Y[:, g, q, :],
                                           start=True, stop=True)
                    mm.then_inc(s_dl, 1)
            for g in range(2):
                pe.wait_ge(s_xy, (c * LEVELS + LEVELS - 1) * 2 + g + 1)
            for g in range(2):
                for q in range(NHP):
                    h = 2 * q + g
                    mm = pe.matmul(kit.psum[:, 0, h * 64:(h + 1) * 64], m.gk[:, g, q, :], m.vC[:, h * 64:(h + 1) * 64],
                                   start=True, stop=True)
            mm.then_inc(s_d, 1)
            for g in range(2):
                for q in range(NHP):
                    h = 2 * q + g
                    mm = pe.matmul(kit.psum[rows(g), 1 + g, q * P:(q + 1) * P], m.kapC[:, h * 64:(h + 1) * 64],
                                   m.X[:, g, q, :], start=True, stop=True)
            mm.then_inc(s_w, 1)
            pe.wait_ge(s_dc, c + 1)
            pe.wait_ge(s_wc, c + 1)
            if c >= 1:
                pe.wait_ge(s_st, c)
            for g in range(2):
                for q in range(NHP):
                    h = 2 * q + g
                    z = kit.psum[:, 3 + g, q * 64:(q + 1) * 64]
                    mm = pe.matmul(z, m.X[:, g, q, :], m.D[:, h * 64:(h + 1) * 64], start=True, stop=(c == 0))
                    if c > 0:
                        mm = pe.matmul(z, m.WT[rows(g), q, :], m.S[rows(g), q, :], start=False, stop=True)
            mm.then_inc(s_z, 1)
            pe.wait_ge(s_sa, c + 1)
            if c < NT - 1:
                for g in range(2):
                    for q in range(NHP):
                        h = 2 * q + g
                        n = kit.psum[rows(g), 5, q * 64:(q + 1) * 64]
                        pe.matmul(n, m.betC[:, h * 64:(h + 1) * 64], m.SA[:, h * 64:(h + 1) * 64],
                                  start=True, stop=False)
                        mm = pe.matmul(n, m.gamC[:, h * 64:(h + 1) * 64], m.vC[:, h * 64:(h + 1) * 64],
                                       start=False, stop=True)
                mm.then_inc(s_n, 1)
            for g in range(2):
                for q in range(NHP):
                    h = 2 * q + g
                    y = kit.psum[rows(g), 6 + g, q * P:(q + 1) * P]
                    pe.matmul(y, m.SA[:, h * 64:(h + 1) * 64], m.br[:, g, q, :], start=True, stop=False)
                    mm = pe.matmul(y, m.vC[:, h * 64:(h + 1) * 64], m.gr[:, g, q, :], start=False, stop=(c == 0))
                    if c > 0:
                        mm = pe.matmul(y, m.S[rows(g), q, :], rho(g, q, blk), start=False, stop=True)
            mm.then_inc(s_y, 1)

    def scalar(act):
        for c in range(NT):
            blk = slice(c * P, (c + 1) * P)
            for n, dst in enumerate((m.kapC, m.betC, m.gamC, m.vC)):
                act.wait_ge(s_tt, 4 * c + n + 1)
                if c >= 1 and n == 0:
                    act.wait_ge(s_y, c)
                act.activation(dst[:, :], kit.psum[:, n, :], ACT.Copy).then_inc(s_tr, 1)
            for lv in range(1, LEVELS):
                for g in range(2):
                    i = (c * (LEVELS - 1) + lv - 1) * 2 + g
                    act.wait_ge(s_u, i + 1)
                    act.activation(m.U[:, g], quad(g), ACT.Copy).then_inc(s_uc, 1)
            act.wait_ge(s_d, c + 1)
            act.activation(m.D[:, :], kit.psum[:, 0, :], ACT.Copy).then_inc(s_dc, 1)
            act.wait_ge(s_w, c + 1)
            act.activation(m.WT[0:64], quad(1)[0:64], ACT.Copy)
            act.activation(m.WT[64:P], quad(2)[64:P], ACT.Copy).then_inc(s_wc, 1)
            act.wait_ge(s_z, c + 1)
            sa = m.SA[:, :].rearrange("p (q g d) -> p q g d", g=2, d=64)
            for g in range(2):
                ins = act.activation(sa[:, :, g, :], kit.psum[:, 3 + g, 0:NHP * 64].rearrange("p (q d) -> p q d", d=64),
                                     ACT.Copy, scale=-1.0)
            ins.then_inc(s_sa, 1)
            act.wait_ge(s_y, c + 1)
            for g in range(2):
                act.activation(m.yaF[rows(g), :, blk], quad(6 + g)[rows(g)], ACT.Copy).then_inc(s_yc, 1)

    def gpsimd(pool):
        for c in range(NT):
            for lv in range(1, LEVELS):
                for g in range(2):
                    i = (c * (LEVELS - 1) + lv - 1) * 2 + g
                    pool.wait_ge(s_pm, 10 * c + g + 1)
                    if i >= 2:
                        pool.wait_ge(s_u, i - 1)
                    pool.tensor_tensor(m.level[:, g], m.kb[:, g], across(m.pair_mask[:, 1 + lv, :], NHP), ALU.mult)\
                        .then_inc(s_lm, 1)

    def vector(dve):
        step = kit.vector_chain(dve)
        for c in range(NT):
            if c >= 1:
                dve.wait_ge(s_y, c)
                dve.wait_ge(s_lm, 2 * (LEVELS - 1) * c)
            for n in range(len(PAIRS)):
                for g in range(2):
                    k = 2 * n + g
                    dve.wait_ge(s_pr, 10 * c + k + 1)
                    ps = quad(4 + k % 4)
                    if n == 0:
                        step(dve.tensor_copy(m.kb[:, g], ps))
                        step(dve.tensor_tensor(m.Y[:, g], m.kb[:, g], across(m.pair_mask[:, 1, :], NHP), ALU.mult))
                        dve.tensor_tensor(m.Y[:, g], across(m.ident[:, :], NHP), m.Y[:, g], ALU.subtract)\
                           .then_inc(s_pm, 1)
                    elif n == 1:
                        step(dve.tensor_tensor(m.X[:, g], ps, across(m.pair_mask[:, 0, :], NHP), ALU.mult))
                        dve.tensor_tensor(m.X[:, g], across(m.ident[:, :], NHP), m.X[:, g], ALU.subtract)\
                           .then_inc(s_pm, 1)
                        dve.wait_ge(s_pm, 10 * c + k + 1)
                        dve.engine_nop().then_inc(s_xy, 1)
                    else:
                        dst = (m.gk, m.br, m.gr)[n - 2]
                        mask = m.upper_strict if n == 2 else m.upper
                        dve.tensor_tensor(dst[:, g], ps, across(mask[:, :], NHP), ALU.mult).then_inc(s_pm, 1)
            for lv in range(1, LEVELS):
                for g in range(2):
                    i = (c * (LEVELS - 1) + lv - 1) * 2 + g
                    dve.wait_ge(s_dl, i + 1)
                    if lv < LEVELS - 1:
                        step(dve.tensor_tensor(m.Y[:, g], m.Y[:, g], quad(4 + g), ALU.subtract))
                    dve.tensor_tensor(m.X[:, g], m.X[:, g], quad(2 + g), ALU.subtract).then_inc(s_xy, 1)
            if c < NT - 1:
                dve.wait_ge(s_n, c + 1)
                dve.wait_ge(s_y, c + 1)
                s, new = m.S[:, :, :], kit.psum[:, 5, 0:NHP * 64].rearrange("p (q d) -> p q d", d=64)
                if c > 0:
                    step(dve.tensor_tensor(s, s, new, ALU.add))
                else:
                    step(dve.tensor_copy(s, new))
                step(dve.tensor_tensor(s, s, over(m.emid[:, c, :], 64), ALU.mult))
                dve.tensor_tensor(s, s, over(m.emid[:, c + 1, :], 64), ALU.mult).then_inc(s_st, 1)

    return tensor, vector, scalar, gpsimd


def rwkv_finish(nc, kit, m, a):
    s_mu = kit.sem("head_sums_ready")
    s_sq = kit.sem("head_squares_ready")
    s_cen = kit.sem("head_centred")
    s_var = kit.sem("head_square_sums_ready")
    s_rt = kit.sem("head_root_ready")

    def tensor(pe):
        for t in range(NHP):
            pe.matmul(kit.psum[:, t, :], m.halves[:, :], m.yaF[:, t, :], start=True, stop=True).then_inc(s_mu, 1)
        for t in range(NHP):
            pe.wait_ge(s_sq, t + 1)
            pe.matmul(kit.psum[:, 4 + t, :], m.halves[:, :], m.sqF[:, t, :], start=True, stop=True).then_inc(s_var, 1)

    def scalar(act):
        for t in range(NHP):
            act.wait_ge(s_cen, t + 1)
            act.activation(m.sqF[:, t, :], m.yaF[:, t, :], ACT.Square).then_inc(s_sq, 1)
        for t in range(NHP):
            act.wait_ge(s_var, t + 1)
            act.activation(m.sqF[:, t, :], kit.psum[:, 4 + t, :], ACT.Sqrt, bias=m.eps["lnx"], scale=1.0 / HD)\
               .then_inc(s_rt, 1)

    def vector(dve):
        step = kit.vector_chain(dve)
        for t in range(NHP):
            dve.wait_ge(s_mu, t + 1)
            y = m.yaF[:, t, :]
            dve.scalar_tensor_tensor(out=y, in0=kit.psum[:, t, :], scalar=-1.0 / HD, in1=y, op0=ALU.mult, op1=ALU.add)\
               .then_inc(s_cen, 1)
        for t in range(NHP):
            y, r = m.yaF[:, t, :], m.sqF[:, t, :]
            dve.wait_ge(s_rt, t + 1)
            step(dve.reciprocal(r, r))
            step(dve.tensor_tensor(y, y, r, ALU.mult))
            step(dve.tensor_scalar(y, y, m.col("lnx_g", t), m.col("lnx_b", t), ALU.mult, ALU.add))
            step(dve.tensor_tensor(y, y, m.bonus[:, t, :], ALU.add))
            step(dve.tensor_tensor(y, y, m.gF[:, t, :], ALU.mult))

    return tensor, vector, scalar, None


def merge(nc, kit, m, a):
    gg = Gemm(kit, a["w_in_2"], KD, RW_COLS + 3 * ATT + IDXW, 2 * D, True)
    gr = Gemm(kit, a["w_o_rwkv"], RW // P, 0, D, True)
    gb = Gemm(kit, a["w_o_att"], ATT // P, 0, D, True)
    s_sig = kit.sem("gates_ready")

    def tensor(pe):
        gg.tensor(pe, m.xT)
        gr.tensor(pe, m.yaF)
        gb.tensor(pe, m.ybF)

    def scalar(act):
        for n in range(gg.count):
            ps = gg.wait_tile(act, n)
            act.activation(m.gates[:, n, :], ps, ACT.Sigmoid).then_inc(kit.tile_free, 1)

    def vector(dve):
        step = kit.vector_chain(dve)
        dve.wait_ge(kit.tile_free, gg.tile0 + gg.count)
        for n in range(KD):
            ps = gr.wait_tile(dve, n)
            dve.tensor_tensor(m.gates[:, n, :], m.gates[:, n, :], ps, ALU.mult).then_inc(kit.tile_free, 1)
        for n in range(KD):
            ps = gb.wait_tile(dve, n)
            dve.tensor_tensor(m.gates[:, KD + n, :], m.gates[:, KD + n, :], ps, ALU.mult).then_inc(kit.tile_free, 1)
            dve.wait_ge(kit.tile_free, gb.tile0 + n + 1)
            step(dve.tensor_tensor(m.merged[:, n, :], m.gates[:, n, :], m.gates[:, KD + n, :], ALU.add))

    return tensor, vector, scalar, None


def ffn_up(nc, kit, m, a):
    gg = Gemm(kit, a["w_ffn_in"], KD, 0, D_FF2, True)
    gu = Gemm(kit, a["w_ffn_in"], KD, D_FF2, D_FF2, True)

    def tensor(pe):
        gg.tensor(pe, m.xT)
        gu.tensor(pe, m.xT)

    def scalar(act):
        for n in range(gg.count):
            ps = gg.wait_tile(act, n)
            act.activation(m.hidden[:, n, :], ps, ACT.Silu).then_inc(kit.tile_free, 1)

    def vector(dve):
        dve.wait_ge(kit.tile_free, gg.tile0 + gg.count)
        for n in range(gu.count):
            ps = gu.wait_tile(dve, n)
            dve.tensor_tensor(m.hidden[:, n, :], m.hidden[:, n, :], ps, ALU.mult).then_inc(kit.tile_free, 1)

    return tensor, vector, scalar, None


class Memory:

    def __init__(self, kit):
        self.h = self.own(kit, "residual", NT, D)
        self.xT = self.own(kit, "x_features", KD, SEQ)
        consts = kit.tensor_sb("constants", [P, 6, P])
        self.ident, self.ones, self.upper, self.upper_strict, self.lower, self.halves = (consts[:, n] for n in range(6))
        self.pair_mask = self.own(kit, "pair_masks", 8, P)
        self.par_cols = self.own(kit, "parameter_columns", 2, P)
        self.head_rows = self.own(kit, "head_rows", 3, SSM_HEADS)
        self.eps_mem = kit.tensor_sb("epsilons", [P, 5])
        self.eps = {k: self.eps_mem[:, n:n + 1] for n, k in enumerate(("ln", "norm", "lnx", "rms"))}
        self.one = self.eps_mem[:, 4:5]
        self.stats = kit.tensor_sb("norm_stats", [P, NT, 2, 6])
        self.mv = kit.tensor_sb("mean_variance", [P, NT, 2])
        self.ms, self.std, self.rstd = (self.own(kit, n, NT) for n in ("mean_square", "deviation", "inverse_deviation"))
        self.gss, self.gstd = (kit.tensor_sb(n, [P, NT, SSM_GROUPS]) for n in ("group_squares", "group_deviation"))
        self.best = kit.tensor_sb("best", [P, 8])
        self.nmax, self.psum_row = (kit.tensor_sb(n, [P, 2, 1]) for n in ("neg_max", "prob_sum"))
        self.prec = kit.tensor_sb("prob_inverse", [P, 2, 1])
        self.mid = kit.tensor_sb("half_chunk_decay", [P, 2, NT * NHP])
        self.emid = kit.tensor_sb("exp_half_chunk_decay", [P, NT, NHP])
        self.rows_mem = kit.tensor_sb("gain_rows", [P, 2 * D])
        self.rows = self.part(self.rows_mem, 0, 2, D)
        self.small = kit.tensor_sb("heads_by_token", [P, 8 * P])
        self.big = kit.tensor_sb("big", [P, 26912])
        self.col0, at = {}, 0
        for name, n in ROWS:
            self.col0[name] = at
            at += n
        b, r, s = self.big, self.rows_mem, self.small
        self.par_rows = self.part(b, 0, 2, P)
        self.dt_raw, self.dt_abs, self.dt, self.da, self.ncs, self.ecs, self.eend, self.wend = \
            (self.part(s, n * P, NT, SSM_HEADS) for n in range(8))
        self.ytmp = self.part(s, 0, 256)
        self.xbcF = self.part(b, 0, XBC_TILES, SEQ)
        self.y = self.part(b, 0, NT, D_INNER)
        self.xT_tok = self.part(b, 16384, NT, D_INNER)
        self.yF = self.part(b, 16384, X_TILES, SEQ)
        self.bTok = self.h
        self.state = self.part(r, 0, SSM_GROUPS, HPG * 64)
        self.decay = self.part(b, 24576, 2, HPG, P)
        self.gate_tmp = self.part(b, 24576, 2, WIDE)
        self.mix = self.decay
        self.sq_tmp = self.part(b, 25600, 256)
        self.xw = self.part(b, 25600, 2, HPG * 64)
        self.hidden = self.part(b, 0, D_FF // P, SEQ)
        self.unit = self.part(b, 16384, NT, D)
        self.qF, self.kF = self.part(b, 0, KD, SEQ), self.part(b, 4096, KD, SEQ)
        self.vTok = self.part(b, 8192, NT, D)
        self.oF = self.part(b, 12288, KD, SEQ)
        self.lo, self.wt, self.sp = (self.part(b, 16384 + 2048 * n, NT, SEQ) for n in range(3))
        self.rwF = self.part(b, 0, RW_COLS // P, SEQ)
        self.attTok = self.part(b, 7168, NT, 3 * ATT)
        self.idxTok = self.part(b, 13312, NT, IDXW)
        self.shift_tmp = self.part(b, 15648, 2, SEQ)
        self.attF = self.part(b, 15648, 8, SEQ)
        self.idxF = self.part(b, 19744, 5, SEQ)
        self.rope = self.part(b, 22304, NT, HD)
        self.rope_tmp = self.part(b, 22560, 2, SEQ)
        self.prob, self.probT = self.part(b, 22304, 2, SEQ), self.part(b, 23328, 2, SEQ)
        self.ybTok = self.part(b, 24352, ATT)
        self.ybF = self.part(b, 24864, NHP, SEQ)
        self.relu, self.score, self.work = self.part(r, 0, 2, SEQ), self.part(r, 1024, SEQ), self.part(r, 1536, SEQ)
        self.lgt = self.part(s, 0, 2, SEQ)
        self.sg, self.aF, self.gF, self.kkF, self.bonus, self.sqF = (self.part(b, 7168 + 2048 * n, NHP, SEQ) for n in range(6))
        self.yaF = self.sg
        self.tmpF = self.part(b, 19456, 1, SEQ)
        self.up_w = self.part(b, 19968, 2, RW)
        self.cs, self.prev_cs = self.part(b, 20992, 2, P), self.part(b, 21248, 2, P)
        self.eF = self.part(b, 21504, 3, 2, P)
        at = 17408
        self.kb, self.X, self.Y, self.U, self.level, self.gk, self.br = (self.part(b, at + 1024 * n, 2, NHP, P) for n in range(7))
        self.gr = self.part(s, 0, 2, NHP, P)
        self.kapC, self.betC, self.gamC, self.vC = (self.part(r, 512 * n, WIDE) for n in range(4))
        self.D, self.WT = self.part(b, at + 3 * 1024, WIDE), self.part(b, at + 3 * 1024 + 512, NHP, P)
        self.SA = self.part(b, at + 4 * 1024, WIDE)
        self.S = self.part(b, 6144, NHP, 64)
        self.gates = self.part(b, 9216, 2 * KD, SEQ)
        self.merged = self.part(b, 17408, KD, SEQ)

    def own(self, kit, name, *dims):
        return self.part(kit.tensor_sb(name, [P, int(np.prod(dims))]), 0, *dims)

    def part(self, mem, at, *dims):
        ap = mem[:, at:at + int(np.prod(dims))]
        names = "abcd"[:len(dims)]
        if len(dims) == 1:
            return ap
        return ap.rearrange(f"p ({' '.join(names)}) -> p {' '.join(names)}", **dict(zip(names, dims)))

    def col(self, name, k):
        return self.par_cols[:, 0, self.col0[name] + k:self.col0[name] + k + 1]


def build(nc, a, out, stop=None, dump=None):
    with ExitStack() as ctx:
        kit = Kit(nc, ctx)
        m = Memory(kit)
        m.x_landed = [kit.sem(f"x_landed{t}") for t in range(NT)]
        m.h_landed = kit.sem("residual_landed")
        m.normf = a["normf_g"]
        m.ln_rows = {"mix1": (a["ln_mix_g"][0, :], a["ln_mix_b"][0, :]), "mlp1": (a["ln_mlp_g"][0, :], a["ln_mlp_b"][0, :]),
                     "mix2": (a["ln_mix_g"][1, :], a["ln_mix_b"][1, :]), "mlp2": (a["ln_mlp_g"][1, :], a["ln_mlp_b"][1, :])}

        def normed(w, k_tiles, src, tag, alpha=ALPHA, res=None, mode="ln", eps="ln", late=False, final=None):
            g = Gemm(kit, w, k_tiles, 0, D, False) if w is not None else None
            m.gemm_in, m.h_late = src, late
            t, v, s, p = norm_rows(nc, kit, m, g, alpha, res, mode, eps, tag, final)

            def tensor(pe):
                m.gemm_in = src
                t(pe)

            def vector(dve):
                m.h_late = late
                v(dve)

            return tensor, vector, s, p

        plan = [
            ("setup", lambda: setup(nc, kit, m, a)),
            ("mamba_in", lambda: mamba_in(nc, kit, m, a)),
            ("mamba_turn", lambda: mamba_turn(nc, kit, m, a)),
            ("mamba_scan", lambda: mamba_scan(nc, kit, m, a)),
            ("mamba_gate", lambda: mamba_gate(nc, kit, m, a)),
            ("mix1", lambda: normed(a["w_out"], X_TILES, m.yF, "mix1", late=True)),
            ("mlp1_up", lambda: mlp_up(nc, kit, m, a["mlp_w1"][0], "mlp1_up")),
            ("mlp1", lambda: normed(a["mlp_w2"][0], D_FF // P, m.hidden, "mlp1")),
            ("sb_project", lambda: sb_project(nc, kit, m, a)),
            ("sb_attend", lambda: sb_attend(nc, kit, m, a)),
            ("mix2", lambda: normed(a["sb_w_o"], KD, m.oF, "mix2")),
            ("mlp2_up", lambda: mlp_up(nc, kit, m, a["mlp_w1"][1], "mlp2_up")),
            ("mlp2", lambda: normed(a["mlp_w2"][1], D_FF // P, m.hidden, "mlp2")),
            ("norm1", lambda: normed(None, 0, None, "norm1", res="norm1_g", mode="rms", eps="norm")),
            ("second_project", lambda: second_project(nc, kit, m, a)),
            ("rope", lambda: rope_turn(nc, kit, m, a)),
            ("sparse", lambda: sparse_attend(nc, kit, m, a)),
            ("rwkv_prepare", lambda: rwkv_prepare(nc, kit, m, a)),
            ("rwkv_scan", lambda: rwkv_scan(nc, kit, m, a)),
            ("rwkv_finish", lambda: rwkv_finish(nc, kit, m, a)),
            ("merge", lambda: merge(nc, kit, m, a)),
            ("norm2", lambda: normed(a["w_out_2"], KD, m.merged, "norm2", alpha=1.0, res="norm2_g", mode="rms", eps="norm")),
            ("ffn_up", lambda: ffn_up(nc, kit, m, a)),
            ("last", lambda: normed(a["w_ffn_out"], D_FF2 // P, m.hidden, "last", alpha=1.0, mode="last", eps="norm", final=out)),
        ]
        phases = []
        for name, make in plan:
            phases.append(make())
            if name == stop:
                break
        s_dump = kit.sem("dump_written")
        block = ctx.enter_context(nc.Block())

        def run(eng, which):
            for n, phase in enumerate(phases):
                if phase[which] is not None:
                    phase[which](eng)
                eng.drain().then_inc(kit.phase_done, 1)
                eng.wait_ge(kit.phase_done, 4 * (n + 1))

        @block.sync
        def _(sp):
            x = a["x"].rearrange("b (t p) d -> (b p) t d", p=P)
            for t in range(NT):
                sp.dma_start(m.h[:, t, :], x[:, t, :]).then_inc(m.x_landed[t], 16)
            for i, (w, k, nk, c, n) in enumerate(kit.chunks):
                if i >= RING:
                    sp.wait_ge(*kit.chunk_over[i - RING])
                src = w[k * P:(k + nk) * P, c:c + n].rearrange("(k p) n -> p k n", p=P)
                sp.dma_start(kit.ring[i % RING][:, 0:nk, 0:n], src).then_inc(kit.chunk_landed[i % RING], 16)
            if dump is not None:
                sp.wait_ge(kit.phase_done, 4 * len(phases))
                for n, (name, ap) in enumerate(dump[1](m)):
                    sp.dma_start(dump[0][n], ap).then_inc(s_dump, 16)
                sp.wait_ge(s_dump, 16 * (n + 1))

        @block.tensor
        def _(pe):
            run(pe, 0)

        @block.vector
        def _(dve):
            run(dve, 1)

        @block.scalar
        def _(act):
            run(act, 2)

        @block.gpsimd
        def _(pool):
            run(pool, 3)


_INS = [("x", "x"), ("w_in", "ssm_w_in"), ("conv_w", "ssm_conv_w"), ("conv_b", "ssm_conv_b"), ("dt_bias", "ssm_dt_bias"),
        ("a_log", "ssm_a_log"), ("ssm_d", "ssm_d"), ("norm_w", "ssm_norm_w"), ("w_out", "ssm_w_out"),
        ("sb_w_k", "sb_w_k"), ("sb_w_v", "sb_w_v"), ("sb_w_q", "sb_w_q"), ("sb_w_o", "sb_w_o"),
        ("mlp_w1", "mlp_w1"), ("mlp_w2", "mlp_w2"), ("ln_mix_g", "ln_mix_g"), ("ln_mix_b", "ln_mix_b"),
        ("ln_mlp_g", "ln_mlp_g"), ("ln_mlp_b", "ln_mlp_b"), ("norm1_g", "norm1_g_2"), ("w_in_2", "w_in_2"),
        ("mu", "tshift_mu_2"), ("w_decay_up", "w_decay_up_2"), ("w0", "w0_2"), ("a_up", "a_up_2"), ("a0", "a0_2"),
        ("g_up", "g_up_2"), ("k_k", "k_k_2"), ("k_a", "k_a_2"), ("r_k", "r_k_2"), ("lnx_g", "lnx_g_2"),
        ("lnx_b", "lnx_b_2"), ("w_o_rwkv", "w_o_rwkv_2"), ("w_o_att", "w_o_att_2"), ("w_out_2", "w_out_2"),
        ("norm2_g", "norm2_g_2"), ("w_ffn_in", "w_ffn_in_2"), ("w_ffn_out", "w_ffn_out_2"), ("normf_g", "normf_g_2")]
_ONE_LAYER = ["w_in", "conv_w", "conv_b", "dt_bias", "a_log", "ssm_d", "norm_w", "w_out", "sb_w_q", "sb_w_o"]


def kernel(**inputs):
    import numpy as _np
    import concourse.bacc as _bacc
    from concourse import mybir as _mybir
    from concourse.bass_utils import run_bass_kernel_spmd as _run

    nc = _bacc.Bacc("TRN2", target_bir_lowering=False, num_devices=1)
    arrays, a = {}, {}
    for name, source in _INS:
        v = _np.ascontiguousarray(inputs[source])
        if name in _ONE_LAYER:
            v = v[0]
        if name == "r_k":
            v = v.reshape(-1)
        arrays[f"in_{name}"] = v
        a[name] = nc.dram_tensor(f"in_{name}", v.shape, _mybir.dt.from_np(v.dtype), kind="ExternalInput").ap()
    table = host_rope()
    arrays["in_rope"] = table
    a["rope"] = nc.dram_tensor("in_rope", table.shape, _mybir.dt.from_np(table.dtype), kind="ExternalInput").ap()
    out = nc.dram_tensor("out_dram", (1, SEQ, D), F32, kind="ExternalOutput").ap()
    build(nc, a, out.rearrange("b s d -> (b s) d"))
    r = _run(nc, [arrays], core_ids=[0])
    return r.results[0]["out_dram"]
```

```python
import math
from contextlib import ExitStack

import numpy as np

import concourse.bass as bass
from concourse import mybir

F32 = mybir.dt.float32
F32R = mybir.dt.float32r
ALU = mybir.AluOpType
ACT = mybir.ActivationFunctionType
AX_X = mybir.AxisListType.X

P = 128
SEQ = 512
NT = SEQ // P
D = 1024
KD = D // P
WIDE = 512
RING = 3
SPLIT = 2
KC = 4
BANKS = 8
LN_EPS = 1e-5
RMS_EPS = 1e-5
NORM_EPS = 1e-6
LNX_EPS = 64e-5
ALPHA = (2 * 2) ** 0.25

D_INNER = 2 * D
SSM_HEADS = D_INNER // 64
SSM_GROUPS = 8
HPG = SSM_HEADS // SSM_GROUPS
XBC = D_INNER + 2 * SSM_GROUPS * P
XBC_TILES = XBC // P
X_TILES = D_INNER // P
D_CONV = 4
SB_HEADS = 16
HD = 64
D_FF = 4 * D
RW = 512
RW_COLS = 3 * RW + 64 + 64 + 128
ATT = 512
IDXW = 512 + 64 + 8
D_FF2 = 2816
TOPK = 128
NHEAD = 8
NHP = NHEAD // 2
DECAY_UNIT = math.exp(-0.5)
REMOVED = -3.0e38
FUTURE = -1.0e38
FAR = -1.0e30

ROWS = [("mu", RW_COLS // P), ("w0", 4), ("a0", 4), ("k_k", 4), ("k_a", 4), ("r_k", 4), ("lnx_g", 4), ("lnx_b", 4),
        ("conv_b", XBC_TILES), ("norm_w", X_TILES), ("norm1_g", KD), ("norm2_g", KD)]


def host_rope():
    half = HD // 2
    inv = (np.float32(1.0) / (np.float32(10000.0) ** (np.arange(half, dtype=np.float32) * np.float32(2.0) / np.float32(HD)))).astype(np.float32)
    ang = (np.arange(SEQ, dtype=np.float32)[:, None] * inv[None, :]).astype(np.float32)
    return np.concatenate([np.cos(ang), np.sin(ang)], axis=1).astype(np.float32)


class Split:

    def __init__(self, high, low):
        self.high, self.low = high, low


class Gemm:

    def __init__(self, kit, w, k_tiles, c0, cols, feature, k_from=0, banks=BANKS):
        self.kit, self.feature, self.banks = kit, feature, banks
        self.chunk0, self.tile0, self.phase0 = len(kit.chunks), kit.tiles, kit.phase_tile0
        self.parts = []
        for c in range(c0, c0 + cols, WIDE):
            n = min(WIDE, c0 + cols - c)
            blocks = [(k, min(KC, k_tiles - k)) for k in range(0, k_tiles, KC)]
            kit.tiles += n // P if feature else NT
            for k, nk in blocks:
                kit.chunks.append((w, k_from + k, nk, c, n))
                if k + nk == k_tiles:
                    kit.chunk_over.append((kit.tile_ready, kit.tiles))
                else:
                    kit.parts_used += 1
                    kit.chunk_over.append((kit.part_used, kit.parts_used))
            self.parts.append((n, blocks))
        self.count = kit.tiles - self.tile0
        self.last_chunk = len(kit.chunks)

    def bank(self, n):
        return (self.tile0 - self.phase0 + n) % self.banks

    def tensor(self, pe, x, before=None, after=None):
        kit = self.kit
        i, tile = self.chunk0, self.tile0
        for j, (n, blocks) in enumerate(self.parts):
            tiles = n // P if self.feature else NT
            for b, (k0, nk) in enumerate(blocks):
                if before is not None and j == 0:
                    before(k0 + nk)
                pe.wait_ge(kit.chunk_split, i + 1)
                w = kit.split_ring[i % SPLIT]
                for m in range(tiles):
                    t = tile + m
                    if b == 0 and t - self.phase0 >= self.banks:
                        pe.wait_ge(kit.tile_free, t - self.banks + 1)
                    out = kit.psum[:, (t - self.phase0) % self.banks, 0:WIDE if self.feature else n]
                    for k in range(nk):
                        xk = x(k0 + k)
                        pairs = ((w.high, xk.high), (w.low, xk.high), (w.high, xk.low))
                        for q, (wp, xp) in enumerate(pairs):
                            first = b == 0 and k == 0 and q == 0
                            last = b == len(blocks) - 1 and k == nk - 1 and q == 2
                            if self.feature:
                                mm = pe.matmul(out, wp[:, k, m * P:(m + 1) * P], xp, start=first, stop=last)
                            else:
                                mm = pe.matmul(out, xp[:, m * P:(m + 1) * P], wp[:, k, 0:n], start=first, stop=last)
                    if b == len(blocks) - 1:
                        mm.then_inc(kit.tile_ready, 1)
                    elif m == tiles - 1:
                        mm.then_inc(kit.part_used, 1)
                i += 1
            tile += tiles
            if after is not None:
                after(j)

    def take_over(self, eng):
        if self.tile0:
            eng.wait_ge(self.kit.tile_free, self.tile0)

    def wait_tile(self, eng, n):
        eng.wait_ge(self.kit.tile_ready, self.tile0 + n + 1)
        return self.kit.psum[:, self.bank(n), :]

    def wait_free(self, eng, n):
        eng.wait_ge(self.kit.tile_free, self.tile0 + n + 1)


class Chain:

    def __init__(self, eng, sem):
        self.eng, self.sem, self.n = eng, sem, 0

    def __call__(self, ins):
        self.n += 1
        ins.then_inc(self.sem, 1)
        self.eng.wait_ge(self.sem, self.n)

    def mark(self, ins):
        self.n += 1
        ins.then_inc(self.sem, 1)
        return self.n

    def wait(self):
        self.eng.wait_ge(self.sem, self.n)


class Kit:

    def __init__(self, nc, ctx):
        self.nc, self.ctx = nc, ctx
        self.chunks, self.chunk_over, self.tiles, self.parts_used = [], [], 0, 0
        self.psum = self.tensor_psum("psum", [P, BANKS, WIDE])
        self.ring_mem = self.tensor_sb("weight_ring", [P, RING, KC, WIDE])
        self.ring = [self.ring_mem[:, r] for r in range(RING)]
        self.split_mem = self.tensor_sb("weight_split_ring", [P, SPLIT, 2, KC, WIDE], F32R)
        self.split_ring = [Split(self.split_mem[:, r, 0], self.split_mem[:, r, 1]) for r in range(SPLIT)]
        self.high_made, self.chunk_split, self.split_done = self.sem("chunk_high_made"), self.sem("chunk_split"), 0
        self.phase_tile0 = 0
        self.chunk_landed = [self.sem(f"chunk_landed{r}") for r in range(RING)]
        self.part_used = self.sem("part_used")
        self.tile_ready = self.sem("tile_ready")
        self.tile_free = self.sem("tile_free")
        self.phase_done = self.sem("phase_done")
        self.vector_step, self.chain = self.sem("vector_step"), None
        self.norm_sems = [self.sem(f"norm_{n}") for n in ("variance_ready", "deviation_ready", "normed", "transposed",
                                                          "high_ready", "transpose_read", "rows_landed")]
        self.norms, self.norm_rows = 0, 0
        self.mlp_sems = [self.sem(f"mlp_{n}") for n in ("relu_ready", "square_ready", "high_ready", "split_ready")]
        self.mlp_tiles = 0

    def tensor_sb(self, name, shape, dtype=F32):
        return self.ctx.enter_context(self.nc.sbuf_tensor(name, shape, dtype))

    def split_chunks(self, pool, upto):
        for i in range(self.split_done, min(upto, len(self.chunks))):
            _, _, nk, _, n = self.chunks[i]
            raw, part = self.ring[i % RING][:, 0:nk, 0:n], self.split_ring[i % SPLIT]
            pool.wait_ge(self.chunk_landed[i % RING], 16 * (i // RING + 1))
            if i >= SPLIT:
                pool.wait_ge(*self.chunk_over[i - SPLIT])
            pool.tensor_scalar(part.high[:, 0:nk, 0:n], raw, 1.0, 0.0, ALU.mult, ALU.add).then_inc(self.high_made, 1)
            pool.wait_ge(self.high_made, i + 1)
            pool.tensor_tensor(part.low[:, 0:nk, 0:n], raw, part.high[:, 0:nk, 0:n].bitcast(F32), ALU.subtract)\
                .then_inc(self.chunk_split, 1)
        self.split_done = max(self.split_done, min(upto, len(self.chunks)))

    def tensor_psum(self, name, shape):
        return self.ctx.enter_context(self.nc.psum_tensor(name, shape, F32))

    def vector_chain(self, dve):
        if self.chain is None:
            self.chain = Chain(dve, self.vector_step)
        return self.chain

    def sem(self, name):
        return self.ctx.enter_context(self.nc.semaphore(name))


def over(ap, n):
    return ap.unsqueeze(len(ap.shape)).broadcast_to(list(ap.shape) + [n])


def across(ap, n):
    return ap.unsqueeze(1).broadcast_to([ap.shape[0], n, ap.shape[1]])


def norm_rows(nc, kit, m, alpha, gain, mode, eps, tag, gemms=(), src=None, first=None, final=None):
    s_var, s_std, s_norm, s_tr, s_high, s_tf, s_rows = kit.norm_sems
    s_out = kit.sem("out_written") if final is not None else None
    tok0, turn0 = kit.norms * NT, kit.norms * 2 * NT
    kit.norms += 1
    if mode != "rms":
        kit.norm_rows += 32 if mode == "ln" else 16
    rows_in = kit.norm_rows
    unit = m.h if mode != "rms" else m.unit
    last = final is not None

    def tensor(pe):
        if last:
            return
        for t in range(NT):
            pe.wait_ge(s_norm, tok0 + t + 1)
            if gemms and t == 0:
                gemms[-1].wait_free(pe, gemms[-1].count - 1)
            for j in range(2):
                n = 2 * t + j
                if n >= 4:
                    pe.wait_ge(s_tf, turn0 + n - 3)
                for q in range(4):
                    mm = pe.transpose(kit.psum[:, n % 4, q * P:(q + 1) * P],
                                      unit[:, t, (4 * j + q) * P:(4 * j + q + 1) * P], m.ident[:, :])
                mm.then_inc(s_tr, 1)

    def add_tiles(dve, gemm, scale, stats):
        step = kit.vector_chain(dve)
        for n in range(2):
            for t in range(NT):
                ps = gemm.wait_tile(dve, 4 * n + t)
                hs = m.h[:, t, n * WIDE:(n + 1) * WIDE]
                dve.scalar_tensor_tensor(out=hs, in0=hs, scalar=scale, in1=ps, op0=ALU.mult, op1=ALU.add)\
                   .then_inc(kit.tile_free, 1)
                gemm.wait_free(dve, 4 * n + t)
                if stats:
                    step.mark(dve.bn_stats(m.stats[:, t, n, :], hs))

    def low_parts(dve, t):
        for j in range(2):
            n = 2 * t + j
            dve.wait_ge(s_high, turn0 + n + 1)
            blk = slice(t * P, (t + 1) * P)
            ps = kit.psum[:, n % 4, :].rearrange("p (q c) -> p q c", q=4)
            high, low = (x[:, 4 * j:4 * j + 4, blk] for x in (m.xin.high, m.xin.low))
            if mode == "ln":
                dve.tensor_tensor(low, ps, high.bitcast(F32), ALU.subtract).then_inc(s_tf, 1)
            else:
                for q in range(4):
                    ins = dve.scalar_tensor_tensor(out=low[:, q], in0=ps[:, q], scalar=m.col(gain, 4 * j + q),
                                                   in1=high[:, q].bitcast(F32), op0=ALU.mult, op1=ALU.subtract)
                ins.then_inc(s_tf, 1)

    def vector(dve):
        step = kit.vector_chain(dve)
        if not gemms:
            for t in range(NT):
                for n in range(2):
                    step.mark(dve.bn_stats(m.stats[:, t, n, :], m.h[:, t, n * WIDE:(n + 1) * WIDE]))
        step.wait()
        for t in range(NT):
            step.mark(dve.bn_aggr(m.mv[:, t, :], m.stats[:, t].rearrange("p a b -> p (a b)")))
        step.wait()
        if mode != "ln":
            step(dve.tensor_tensor(m.ms[:, :], m.mv[:, :, 0], m.mv[:, :, 0], ALU.mult))
            step(dve.tensor_tensor(m.mv[:, :, 1], m.mv[:, :, 1], m.ms[:, :], ALU.add))
        dve.tensor_scalar(m.ms[:, :], m.mv[:, :, 1], m.eps[eps], None, ALU.add).then_inc(s_var, 1)
        dve.wait_ge(s_std, tok0 // NT + 1)
        r, w = m.rstd[:, :], m.std[:, :]
        step(dve.reciprocal(r, w))
        step(dve.tensor_tensor(w, r, r, ALU.mult))
        step(dve.tensor_tensor(w, w, m.ms[:, :], ALU.mult))
        step(dve.tensor_scalar(w, w, -0.5, 1.5, ALU.mult, ALU.add))
        step(dve.tensor_tensor(r, r, w, ALU.mult))
        for t in range(NT + 1):
            if t < NT:
                ht, rt = m.h[:, t, :], m.rstd[:, t:t + 1]
                if t == 0 and mode != "rms":
                    dve.wait_ge(s_rows, rows_in)
                if mode == "ln":
                    step(dve.scalar_tensor_tensor(out=ht, in0=ht, scalar=m.mv[:, t, 0:1], in1=m.rows[:, 0, :],
                                                  op0=ALU.subtract, op1=ALU.mult))
                    dve.scalar_tensor_tensor(out=ht, in0=ht, scalar=rt, in1=m.rows[:, 1, :],
                                             op0=ALU.mult, op1=ALU.add).then_inc(s_norm, 1)
                elif not last:
                    dve.tensor_scalar(m.unit[:, t, :], ht, rt, None, ALU.mult).then_inc(s_norm, 1)
                else:
                    dve.scalar_tensor_tensor(out=ht, in0=ht, scalar=rt, in1=m.rows[:, 0, :],
                                             op0=ALU.mult, op1=ALU.mult).then_inc(s_norm, 1)
            if t >= 1 and not last:
                low_parts(dve, t - 1)

    def scalar(act):
        act.wait_ge(s_var, tok0 // NT + 1)
        act.activation(m.std[:, :], m.ms[:, :], ACT.Sqrt).then_inc(s_std, 1)
        if last:
            return
        for n in range(2 * NT):
            t, j = n // 2, n % 2
            act.wait_ge(s_tr, turn0 + n + 1)
            dst = m.xin.high[:, 4 * j:4 * j + 4, t * P:(t + 1) * P]
            ps = kit.psum[:, n % 4, :].rearrange("p (q c) -> p q c", q=4)
            if mode == "ln":
                ins = act.activation(dst, ps, ACT.Copy)
            else:
                for q in range(4):
                    ins = act.activation(dst[:, q], ps[:, q], ACT.Copy, scale=m.col(gain, 4 * j + q))
            ins.then_inc(s_high, 1)

    def rows(pool):
        if mode == "ln":
            g, b = m.ln_rows[tag]
            pool.dma_start(m.rows[:, 0, :], g.partition_broadcast(P)).then_inc(s_rows, 16)
            pool.dma_start(m.rows[:, 1, :], b.partition_broadcast(P)).then_inc(s_rows, 16)
        elif last:
            pool.dma_start(m.rows[:, 0, :], m.normf.partition_broadcast(P)).then_inc(s_rows, 16)

    def gpsimd(pool):
        if last:
            out = final.rearrange("(t p) d -> p t d", p=P)
            for t in range(NT):
                pool.wait_ge(s_norm, tok0 + t + 1)
                pool.dma_start(out[:, t, :], m.h[:, t, :]).then_inc(s_out, 16)
            pool.wait_ge(s_out, 16 * NT)

    return tensor, vector, scalar, gpsimd, rows, add_tiles


def project_norm(nc, kit, m, w, k_tiles, x, alpha, tag, gain=None, mode="ln", eps="ln", late=False):
    g = Gemm(kit, w, k_tiles, 0, D, False)
    t, v, a, p, rows, add = norm_rows(nc, kit, m, alpha, gain, mode, eps, tag, gemms=(g,))

    def tensor(pe):
        g.tensor(pe, x)
        t(pe)

    def vector(dve):
        if late:
            dve.wait_ge(m.h_landed, 16)
        add(dve, g, alpha, True)
        v(dve)

    def gpsimd(pool):
        rows(pool)
        kit.split_chunks(pool, g.last_chunk + SPLIT)

    return tensor, vector, a, gpsimd


def norm_only(nc, kit, m, tag, gain, eps):
    t, v, a, p, rows, add = norm_rows(nc, kit, m, 1.0, gain, "rms", eps, tag)
    return t, v, a, None


def mlp(nc, kit, m, w1, w2, tag):
    HALF = D_FF // P // 2
    up = [None, None]
    down = [None, None]
    for q in range(2):
        up[q] = Gemm(kit, w1, KD, q * HALF * P, HALF * P, True)
        down[q] = Gemm(kit, w2, HALF, 0, D, False, k_from=q * HALF)
    t, v, a, p, rows, add = norm_rows(nc, kit, m, ALPHA, None, "ln", "ln", tag, gemms=(down[1],))
    s_relu, s_sq, s_high, s_hid = kit.mlp_sems
    n0 = kit.mlp_tiles
    kit.mlp_tiles += 2 * HALF

    def tensor(pe):
        for q in range(2):
            up[q].tensor(pe, m.x_tile)
            down[q].tensor(pe, m.hidden_tile, before=lambda k, q=q: pe.wait_ge(s_hid, n0 + q * HALF + k))
        t(pe)

    def scalar(act):
        for n in range(2 * HALF):
            if n % HALF == 0:
                up[n // HALF].take_over(act)
            ps = up[n // HALF].wait_tile(act, n % HALF)
            if n >= 2:
                act.wait_ge(s_hid, n0 + n - 1)
            act.activation(m.relu_tmp[:, n % 2, :], ps, ACT.Relu).then_inc(kit.tile_free, 1)
            up[n // HALF].wait_free(act, n % HALF)
            if n == HALF:
                act.wait_ge(kit.tile_ready, down[0].tile0 + down[0].count)
            act.activation(m.hid.high[:, n % HALF, :], m.relu_tmp[:, n % 2, :], ACT.Square).then_inc(s_high, 1)
        a(act)

    def vector(dve):
        step = kit.vector_chain(dve)
        for q in range(2):
            for n in range(q * HALF, (q + 1) * HALF):
                up[q].wait_free(dve, n % HALF)
                sq = m.sq_tmp2[:, n % 2, :]
                r = m.relu_tmp[:, n % 2, :]
                step(dve.tensor_tensor(sq, r, r, ALU.mult))
                dve.wait_ge(s_high, n0 + n + 1)
                dve.tensor_tensor(m.hid.low[:, n % HALF, :], sq, m.hid.high[:, n % HALF, :].bitcast(F32), ALU.subtract)\
                   .then_inc(s_hid, 1)
            add(dve, down[q], ALPHA if q == 0 else 1.0, q == 1)
        v(dve)

    def gpsimd(pool):
        rows(pool)
        kit.split_chunks(pool, down[1].last_chunk + SPLIT)

    return tensor, vector, scalar, gpsimd


def setup(nc, kit, m, a):
    s_base = kit.sem("constant_filled")
    s_sel = kit.sem("constant_cut")
    s_par = kit.sem("parameter_rows_landed")
    s_tr = kit.sem("setup_transposed")
    s_tf = kit.sem("setup_transpose_read")
    s_high = kit.sem("setup_high_ready")

    def gpsimd(pool):
        base = Chain(pool, s_base)
        fills = [(m.ident, 0.0), (m.ones, 1.0), (m.upper, 1.0), (m.upper_strict, 1.0), 
                 (m.halves, 0.0), (m.pair_mask[:, 0, :], 0.0), (m.eps_mem[:, 0:1], LN_EPS),
                 (m.eps_mem[:, 1:2], NORM_EPS), (m.eps_mem[:, 2:3], LNX_EPS), (m.eps_mem[:, 3:4], RMS_EPS),
                 (m.eps_mem[:, 4:5], 1.0), (m.neg_ones, -1.0), (m.neg_lower, -1.0), (m.pair_mask[:, 1:8, :], 0.0)]
        for ap, v in fills:
            base.mark(pool.memset(ap, v))
        base.wait()
        cut = Chain(pool, s_sel)
        cut.mark(pool.affine_select(out=m.ident[:, :], in_=m.ident[:, :], compare_op=ALU.not_equal, fill=1.0, base=0,
                                    pattern=[[-1, P]], channel_multiplier=1))
        for t, sign, b in ((m.upper, 1, 0), (m.upper_strict, 1, -1), (m.neg_lower, -1, 0)):
            cut.mark(pool.affine_select(out=t[:, :], in_=t[:, :], compare_op=ALU.is_ge, fill=0.0, base=b,
                                        pattern=[[sign, P]], channel_multiplier=-sign))
        cut.wait()
        cut(pool.memset(m.halves[0:64, 0:64], 1.0))
        cut(pool.memset(m.halves[64:P, 64:P], 1.0))
        for n in range(8):
            b = 1 if n == 0 else 2 ** (n - 1)
            half = 1 if n == 0 else 0
            part = m.pair_mask[:, n, :].rearrange("p (q h r) -> p q h r", h=2, r=b)[:, :, half, :]
            lo = 0 if n == 0 else b
            cut(pool.memset(part, 1.0))
            cut(pool.affine_select(out=part, in_=part, compare_op=ALU.is_ge, fill=0.0, base=-lo,
                                   pattern=[[-2 * b, P // (2 * b)], [0, b]], channel_multiplier=1))
            cut(pool.affine_select(out=part, in_=part, compare_op=ALU.is_ge, fill=0.0, base=lo + b - 1,
                                   pattern=[[2 * b, P // (2 * b)], [0, b]], channel_multiplier=-1))
        cut(pool.tensor_scalar(m.ident_r, m.ident, 1.0, 0.0, ALU.mult, ALU.add))
        cut(pool.tensor_scalar(m.past_r, m.upper, -FAR, FAR, ALU.mult, ALU.add))
        kit.split_chunks(pool, SPLIT)

    def scalar(act):
        at = 0
        for name, n in ROWS:
            act.dma_start(m.par_rows[at:at + n, 0, :], a[name].rearrange("(r c) -> r c", c=P)).then_inc(s_par, 16)
            at += n
        act.dma_start(m.par_rows[:, 1, :], a["conv_w"].rearrange("j (r c) -> (j r) c", c=P)).then_inc(s_par, 16)
        for n, ap in enumerate((a["dt_bias"], a["a_log"], a["ssm_d"])):
            act.dma_start(m.head_rows[:, n, :], ap.partition_broadcast(P)).then_inc(s_par, 16)
        for n in range(2 * NT):
            act.wait_ge(s_tr, n + 1)
            t, j = n // 2, n % 2
            act.activation(m.xin.high[:, 4 * j:4 * j + 4, t * P:(t + 1) * P],
                           kit.psum[:, n % 4, :].rearrange("p (q c) -> p q c", q=4), ACT.Copy).then_inc(s_high, 1)
        act.wait_ge(s_tr, 2 * NT + 1)
        nrow = sum(n for _, n in ROWS)
        act.activation(m.par_cols[:, 0, 0:nrow], kit.psum[:, 4, 0:nrow], ACT.Copy)
        act.activation(m.par_cols[:, 1, :], kit.psum[:, 4, P:2 * P], ACT.Copy)

    def tensor(pe):
        pe.wait_ge(s_sel, 1)
        for n in range(2 * NT):
            t, j = n // 2, n % 2
            if j == 0:
                pe.wait_ge(m.x_landed[t], 16)
            if n >= 4:
                pe.wait_ge(s_tf, n - 3)
            for q in range(4):
                mm = pe.transpose(kit.psum[:, n % 4, q * P:(q + 1) * P], m.h[:, t, (4 * j + q) * P:(4 * j + q + 1) * P],
                                  m.ident[:, :])
            mm.then_inc(s_tr, 1)
        pe.wait_ge(s_par, 16 * (len(ROWS) + 4))
        nrow = sum(n for _, n in ROWS)
        pe.transpose(kit.psum[:, 4, 0:nrow], m.par_rows[0:nrow, 0, :], m.ident[0:nrow, 0:nrow])
        pe.transpose(kit.psum[:, 4, P:2 * P], m.par_rows[:, 1, :], m.ident[:, :]).then_inc(s_tr, 1)

    def vector(dve):
        for n in range(2 * NT):
            dve.wait_ge(s_high, n + 1)
            t, j = n // 2, n % 2
            high, low = (x[:, 4 * j:4 * j + 4, t * P:(t + 1) * P] for x in (m.xin.high, m.xin.low))
            dve.tensor_tensor(low, kit.psum[:, n % 4, :].rearrange("p (q c) -> p q c", q=4), high.bitcast(F32),
                              ALU.subtract).then_inc(s_tf, 1)

    return tensor, vector, scalar, gpsimd


def mamba_in(nc, kit, m, a):
    BK = 6
    g = Gemm(kit, a["w_in"], KD, D_INNER, XBC, True, banks=BK)
    gd = Gemm(kit, a["w_in"], KD, D_INNER + XBC, SSM_HEADS, False, banks=BK)
    TURNED = X_TILES + SSM_GROUPS
    s_silu = kit.sem("conv_silu_ready")
    s_tr = kit.sem("xb_transposed")
    s_tf = kit.sem("xb_transpose_read")
    s_abs = kit.sem("dt_abs_ready")
    s_exp = kit.sem("dt_exp_step")
    s_da = kit.sem("da_ready")
    s_cs = kit.sem("decay_sums_ready")
    s_cr = kit.sem("decay_sums_read_by_scalar")
    s_sum = kit.sem("decay_to_end_ready")
    s_we = kit.sem("weight_to_end_ready")

    def tile(n):
        return m.xring[:, n % 8, :] if n < X_TILES else m.bcF[:, n - X_TILES, :]

    def tensor(pe):
        def turn(j):
            for n in range(4 * j, 4 * j + 4):
                if n >= TURNED:
                    return
                pe.wait_ge(s_silu, n + 1)
                if n >= 2:
                    pe.wait_ge(s_tf, n - 1)
                for c in range(NT):
                    mm = pe.transpose(kit.psum[:, BK + n % 2, c * P:(c + 1) * P], tile(n)[:, c * P:(c + 1) * P],
                                      m.ident[:, :])
                mm.then_inc(s_tr, 1)

        g.tensor(pe, m.x_tile, after=lambda j: turn(j - 1) if j >= 1 else None)
        gd.tensor(pe, m.x_tile)
        pe.wait_ge(s_da, 1)
        pe.wait_ge(s_tf, TURNED)
        for c in range(NT):
            pe.matmul(kit.psum[:, 6, c * 32:c * 32 + 32], m.upper[:, :], m.da[:, c, :], start=True, stop=True)
            mm = pe.matmul(kit.psum[:, 7, c * 32:c * 32 + 32], m.ones[:, :], m.da[:, c, :], start=True, stop=True)
        mm.then_inc(s_cs, 1)

    def vector(dve):
        step = kit.vector_chain(dve)
        for n in range(XBC_TILES):
            ps = g.wait_tile(dve, n)
            if 8 <= n < X_TILES:
                dve.wait_ge(s_tr, n - 7)
            acc = tile(n)
            w = [m.par_cols[:, 1, j * XBC_TILES + n:j * XBC_TILES + n + 1] for j in range(D_CONV)]
            step(dve.tensor_scalar(acc, ps, w[3], m.col("conv_b", n), ALU.mult, ALU.add))
            for d in (1, 2):
                step(dve.scalar_tensor_tensor(out=acc[:, d:], in0=ps[:, :SEQ - d], scalar=w[3 - d], in1=acc[:, d:],
                                              op0=ALU.mult, op1=ALU.add))
            dve.scalar_tensor_tensor(out=acc[:, 3:], in0=ps[:, :SEQ - 3], scalar=w[0], in1=acc[:, 3:],
                                     op0=ALU.mult, op1=ALU.add).then_inc(kit.tile_free, 1)
        for t in range(NT):
            ps = gd.wait_tile(dve, t)
            dve.tensor_tensor(m.dt_raw[:, t, :], ps[:, 0:SSM_HEADS], m.head_rows[:, 0, :], ALU.add)\
               .then_inc(kit.tile_free, 1)
        gd.wait_free(dve, NT - 1)
        dve.scalar_tensor_tensor(out=m.dt_abs[:, :, :], in0=m.dt_raw[:, :, :], scalar=-1.0, in1=m.dt_raw[:, :, :],
                                 op0=ALU.mult, op1=ALU.max).then_inc(s_abs, 1)
        dve.wait_ge(s_exp, 3)
        step(dve.scalar_tensor_tensor(out=m.dt[:, :, :], in0=m.dt_raw[:, :, :], scalar=0.0, in1=m.dt_abs[:, :, :],
                                      op0=ALU.max, op1=ALU.add))
        dve.scalar_tensor_tensor(out=m.da[:, :, :], in0=m.dt[:, :, :], scalar=-1.0,
                                 in1=across(m.head_rows[:, 1, :], NT), op0=ALU.mult, op1=ALU.mult).then_inc(s_da, 1)
        dve.wait_ge(s_cr, 1)
        w = m.wend[:, :, :].rearrange("p a b -> p (a b)")
        step(dve.tensor_copy(w, kit.psum[:, 7, 0:P]))
        dve.tensor_tensor(w, w, kit.psum[:, 6, 0:P], ALU.subtract).then_inc(s_sum, 1)
        dve.wait_ge(s_we, 1)
        dve.tensor_tensor(m.wend[:, :, :], m.wend[:, :, :], m.dt[:, :, :], ALU.mult)

    def scalar(act):
        def turned(n):
            act.wait_ge(s_tr, n + 1)
            f = n if n < X_TILES else n - X_TILES
            dst = (m.xT_tok if n < X_TILES else m.bTok)[:, :, f * P:(f + 1) * P]
            act.activation(dst, kit.psum[:, BK + n % 2, :].rearrange("p (c d) -> p c d", c=NT), ACT.Copy).then_inc(s_tf, 1)

        for n in range(XBC_TILES):
            g.wait_free(act, n)
            act.activation(tile(n), tile(n), ACT.Silu).then_inc(s_silu, 1)
            if 4 <= n < TURNED + 4:
                turned(n - 4)
        act.activation(m.head_rows[:, 1, :], m.head_rows[:, 1, :], ACT.Exp).then_inc(s_exp, 1)
        act.wait_ge(s_abs, 1)
        act.activation(m.dt_abs[:, :, :], m.dt_abs[:, :, :], ACT.Exp, scale=-1.0).then_inc(s_exp, 1)
        act.wait_ge(s_exp, 2)
        act.activation(m.dt_abs[:, :, :], m.dt_abs[:, :, :], ACT.Ln, bias=m.one).then_inc(s_exp, 1)
        act.wait_ge(s_cs, 1)
        cs, end = kit.psum[:, 6, 0:P], kit.psum[:, 7, 0:P]
        act.activation(m.ncs[:, :, :].rearrange("p a b -> p (a b)"), cs, ACT.Copy, scale=-1.0)
        act.activation(m.ecs[:, :, :].rearrange("p a b -> p (a b)"), cs, ACT.Exp)
        act.activation(m.eend[:, :, :].rearrange("p a b -> p (a b)"), end, ACT.Exp).then_inc(s_cr, 1)
        act.wait_ge(s_sum, 1)
        act.activation(m.wend[:, :, :], m.wend[:, :, :], ACT.Exp).then_inc(s_we, 1)

    def gpsimd(pool):
        kit.split_chunks(pool, gd.last_chunk + SPLIT)

    return tensor, vector, scalar, gpsimd


def mamba_scan(nc, kit, m, a):
    s_cb = kit.sem("cb_and_sums_ready")
    s_e = kit.sem("decay_matrix_ready")
    s_mix = kit.sem("mix_matrix_ready")
    s_xw = kit.sem("weighted_x_ready")
    s_y = kit.sem("chunk_products_ready")
    s_fold = kit.sem("chunk_products_read")
    s_skip = kit.sem("skip_term_ready")
    STEPS = NT * SSM_GROUPS
    GW = HPG * 64

    def split(i):
        return i // SSM_GROUPS, i % SSM_GROUPS

    def by_head(ap):
        return ap.rearrange("p (h d) -> p h d", d=64)

    def tensor(pe):
        def first(i):
            c, g = split(i)
            blk = slice(c * P, (c + 1) * P)
            if i >= 2:
                pe.wait_ge(s_mix, i - 1)
            pe.matmul(kit.psum[:, i % 2, 0:P], m.bcF[:, g, blk], m.bcF[:, SSM_GROUPS + g, blk],
                      start=True, stop=True)
            bank = kit.psum[:, 2 + i % 2, :]
            pe.matmul(bank.rearrange("p (h l) -> p h l", h=HPG), m.ident_r[:, :], across(m.past_r[:, :], HPG),
                      start=True, stop=True, skip_group_check=True)
            for r in range(HPG):
                h = g * HPG + r
                mm = pe.matmul(bank[:, r * P:(r + 1) * P], m.da[:, c, h:h + 1].broadcast_to([P, P]),
                               m.upper[:, :], start=False, stop=True, skip_group_check=True)
            mm.then_inc(s_cb, 1)

        def second(i):
            c, g = split(i)
            blk = slice(c * P, (c + 1) * P)
            if i >= 2:
                pe.wait_ge(s_fold, i - 1)
            yb = kit.psum[:, 4 + i % 2, :]
            pe.wait_ge(s_xw, i + 1)
            pe.wait_ge(s_mix, i + 1)
            for r in range(HPG):
                mm = pe.matmul(yb[:, r * 64:(r + 1) * 64], m.decay[:, i % 3, r, :], m.xdt[:, i % 2, r * 64:(r + 1) * 64],
                               start=True, stop=True)
            if c > 0:
                pe.wait_ge(s_fold, i - SSM_GROUPS + 1)
                mm = pe.matmul(yb[:, GW:2 * GW], m.bcF[:, SSM_GROUPS + g, blk], m.state[:, g, :],
                               start=True, stop=True)
            if c < NT - 1:
                mm = pe.matmul(kit.psum[:, 6 + i % 2, 0:GW], m.bTok[:, c, g * P:(g + 1) * P], m.xw[:, i % 2, :],
                               start=True, stop=True)
            mm.then_inc(s_y, 1)

        for i in range(STEPS + 2):
            if i < STEPS:
                first(i)
            if i >= 2:
                second(i - 2)

    def scalar(act):
        for i in range(STEPS):
            c, g = split(i)
            act.wait_ge(s_cb, i + 1)
            if i >= 3:
                act.wait_ge(s_y, i - 2)
            for r in range(HPG):
                h = g * HPG + r
                ins = act.activation(m.decay[:, i % 3, r, :], kit.psum[:, 2 + i % 2, r * P:(r + 1) * P], ACT.Exp,
                                     bias=m.ncs[:, c, h:h + 1])
            ins.then_inc(s_e, 1)

    def gpsimd(pool):
        def weigh(i):
            c, g = split(i)
            heads = slice(g * HPG, (g + 1) * HPG)
            x = by_head(m.y[:, c, g * GW:(g + 1) * GW])
            if i >= 2:
                pool.wait_ge(s_y, i - 1)
            ins = pool.tensor_tensor(by_head(m.xdt[:, i % 2, :]), x, over(m.dt[:, c, heads], 64), ALU.mult)
            if c < NT - 1:
                ins = pool.tensor_tensor(by_head(m.xw[:, i % 2, :]), x, over(m.wend[:, c, heads], 64), ALU.mult)
            ins.then_inc(s_xw, 1)

        def skip(i):
            c, g = split(i)
            pool.wait_ge(s_xw, i + 1)
            y = by_head(m.y[:, c, g * GW:(g + 1) * GW])
            pool.tensor_tensor(y, y, over(m.head_rows[:, 2, g * HPG:(g + 1) * HPG], 64), ALU.mult).then_inc(s_skip, 1)

        for i in range(STEPS):
            weigh(i)
            skip(i)

    def vector(dve):
        st = kit.vector_chain(dve)

        def mix(i):
            dve.wait_ge(s_e, i + 1)
            e = m.decay[:, i % 3]
            dve.tensor_tensor(e, e, across(kit.psum[:, i % 2, 0:P], HPG), ALU.mult).then_inc(s_mix, 1)

        def fold(i):
            c, g = split(i)
            y, s = m.y[:, c, g * GW:(g + 1) * GW], m.state[:, g, :]
            yb, new = kit.psum[:, 4 + i % 2, :], kit.psum[:, 6 + i % 2, 0:GW]
            dve.wait_ge(s_skip, i + 1)
            dve.wait_ge(s_y, i + 1)
            st.mark(dve.tensor_tensor(y, y, yb[:, 0:GW], ALU.add))
            if c == 0:
                ins = dve.tensor_copy(s, new)
            else:
                dve.wait_ge(s_fold, i - 1)
                tmp = m.ytmp[:, i % 2, :]
                st.mark(dve.tensor_tensor(by_head(tmp), by_head(yb[:, GW:2 * GW]),
                                          over(m.ecs[:, c, g * HPG:(g + 1) * HPG], 64), ALU.mult))
                if c < NT - 1:
                    st.mark(dve.tensor_tensor(by_head(s), by_head(s), over(m.eend[:, c, g * HPG:(g + 1) * HPG], 64),
                                              ALU.mult))
                st.wait()
                ins = dve.tensor_tensor(y, y, tmp, ALU.add)
                if c < NT - 1:
                    ins = dve.tensor_tensor(s, s, new, ALU.add)
            ins.then_inc(s_fold, 1)

        for i in range(STEPS + 1):
            if i < STEPS:
                mix(i)
            if i >= 1:
                fold(i - 1)

    return tensor, vector, scalar, gpsimd


def mamba_gate(nc, kit, m, a):
    g = Gemm(kit, a["w_in"], KD, 0, D_INNER, False)
    s_yhigh = kit.sem("y_high_ready")
    s_gated = kit.sem("gated_ready")
    s_ss = kit.sem("squares_summed")
    s_std = kit.sem("group_deviation_ready")
    s_norm = kit.sem("y_normed")
    s_tr = kit.sem("y_transposed")
    s_tf = kit.sem("y_transpose_read")
    GW = D_INNER // SSM_GROUPS

    def tensor(pe):
        g.tensor(pe, m.x_tile)
        for n in range(X_TILES):
            if n == 0:
                pe.wait_ge(kit.tile_free, g.tile0 + g.count)
                pe.wait_ge(s_norm, NT)
            if n >= 4:
                pe.wait_ge(s_tf, n - 3)
            for c in range(NT):
                mm = pe.transpose(kit.psum[:, n % 4, c * P:(c + 1) * P], m.y[:, c, n * P:(n + 1) * P], m.ident[:, :])
            mm.then_inc(s_tr, 1)

    def scalar(act):
        for n in range(g.count):
            ps = g.wait_tile(act, n)
            if n >= 2:
                act.wait_ge(s_gated, n - 1)
            act.activation(m.gate_tmp[:, n % 2, :], ps, ACT.Silu).then_inc(kit.tile_free, 1)
        act.wait_ge(s_ss, 1)
        act.activation(m.gstd[:, :, :], m.gss[:, :, :], ACT.Sqrt, bias=m.eps["rms"], scale=1.0 / GW).then_inc(s_std, 1)
        for n in range(X_TILES):
            act.wait_ge(s_tr, n + 1)
            act.activation(m.y_tile(n).high, kit.psum[:, n % 4, :], ACT.Copy, scale=m.col("norm_w", n))\
               .then_inc(s_yhigh, 1)

    def vector(dve):
        step = kit.vector_chain(dve)
        for n in range(g.count):
            j, t = n // NT, n % NT
            dve.wait_ge(kit.tile_free, g.tile0 + n + 1)
            y = m.y[:, t, j * WIDE:(j + 1) * WIDE]
            dve.tensor_tensor(y, y, m.gate_tmp[:, n % 2, :], ALU.mult).then_inc(s_gated, 1)
            dve.wait_ge(s_gated, n + 1)
            for q in range(2):
                yq = y[:, q * GW:(q + 1) * GW]
                step(dve.tensor_tensor_reduce(out=m.sq_tmp[:, 0:GW], in0=yq, in1=yq, scale=1.0, scalar=0.0,
                                              op0=ALU.mult, op1=ALU.add, accum_out=m.gss[:, t, 2 * j + q:2 * j + q + 1]))
        dve.engine_nop().then_inc(s_ss, 1)
        dve.wait_ge(s_std, 1)
        step(dve.reciprocal(m.gstd[:, :, :], m.gstd[:, :, :]))
        for t in range(NT):
            y = m.y[:, t, :].rearrange("p (g d) -> p g d", d=GW)
            dve.tensor_tensor(y, y, over(m.gstd[:, t, :], GW), ALU.mult).then_inc(s_norm, 1)
        for n in range(X_TILES):
            dve.wait_ge(s_yhigh, n + 1)
            dve.scalar_tensor_tensor(out=m.y_tile(n).low, in0=kit.psum[:, n % 4, :], scalar=m.col("norm_w", n),
                                     in1=m.y_tile(n).high.bitcast(F32), op0=ALU.mult, op1=ALU.subtract)\
               .then_inc(s_tf, 1)

    def gpsimd(pool):
        pool.dma_start(m.h, a["x"].rearrange("b (t p) d -> (b p) t d", p=P)).then_inc(m.h_landed, 16)
        kit.split_chunks(pool, g.last_chunk + SPLIT)

    return tensor, vector, scalar, gpsimd


def sb_project(nc, kit, m, a):
    gq = Gemm(kit, a["sb_w_q"], KD, 0, D, True)
    gk = Gemm(kit, a["sb_w_k"], KD, 0, D, True)
    gv = Gemm(kit, a["sb_w_v"], KD, 0, D, False)

    def tensor(pe):
        for g in (gq, gk, gv):
            g.tensor(pe, m.x_tile)

    def scalar(act):
        for g, dst in ((gq, m.qF), (gk, m.kF)):
            for n in range(g.count):
                ps = g.wait_tile(act, n)
                act.activation(dst[:, n, :], ps, ACT.Copy, scale=HD ** -0.5 if g is gq else 1.0)\
                   .then_inc(kit.tile_free, 1)
        for n in range(gv.count):
            ps = gv.wait_tile(act, n)
            act.activation(m.vTok[:, n % NT, (n // NT) * WIDE:(n // NT + 1) * WIDE], ps, ACT.Copy)\
               .then_inc(kit.tile_free, 1)

    def gpsimd(pool):
        kit.split_chunks(pool, gv.last_chunk + SPLIT)

    return tensor, None, scalar, gpsimd


def sb_attend(nc, kit, m, a):
    s_z = kit.sem("sb_logits_ready")
    s_abs = kit.sem("sb_abs_ready")
    s_exp = kit.sem("sb_exp_ready")
    s_ln = kit.sem("sb_ln_ready")
    s_sp = kit.sem("sb_softplus_raw")
    s_lo = kit.sem("sb_softplus_ready")
    s_x = kit.sem("sb_exponent_ready")
    s_w = kit.sem("sb_weights_raw")
    s_cut = kit.sem("sb_weights_ready")
    s_o = kit.sem("sb_out_ready")
    s_oh = kit.sem("sb_out_high_ready")
    s_of = kit.sem("sb_out_read")

    START = [0, 512, 896, 1152]
    BANK = [(0, 0), (1, 0), (2, 0), (2, 256)]
    SPANS = [(0, 512), (512, 384), (896, 384)]

    def bank(h, b, q=None):
        n, c = BANK[b]
        c += (0 if q is None else q - b * P)
        return kit.psum[:, 3 * (h % 2) + n, c:BANK[b][1] + SEQ - b * P]

    def packed(buf, h, b, q=None):
        c = START[b] + (0 if q is None else q - b * P)
        return buf[:, h % 2, c:START[b] + SEQ - b * P]

    def rows(h):
        return slice((h % 2) * 64, (h % 2) * 64 + 64)

    def tensor(pe):
        def logits(h):
            if h >= 2:
                pe.wait_ge(s_w, h - 1)
            for b in range(NT):
                mm = pe.matmul(bank(h, b), m.kF[rows(h), h // 2, b * P:(b + 1) * P], m.qF[rows(h), h // 2, b * P:],
                               start=(b != 3), stop=True, skip_group_check=True)
            mm.then_inc(s_z, 1)

        def exponents(h):
            pe.wait_ge(s_lo, h + 1)
            for b in reversed(range(NT)):
                for later in range(NT - 1, b, -1):
                    pe.matmul(bank(h, b, later * P), m.neg_ones[:, :], packed(m.sp, h, later),
                              start=False, stop=True, skip_group_check=True)
                mm = pe.matmul(bank(h, b), m.neg_lower[:, :], packed(m.sp, h, b),
                               start=False, stop=True, skip_group_check=True)
            mm.then_inc(s_x, 1)

        def out(h):
            if h >= 2:
                pe.wait_ge(s_of, h - 1)
            pe.wait_ge(s_cut, h + 1)
            o = kit.psum[rows(h), 6 + h % 2, :]
            for b in range(NT):
                mm = pe.matmul(o[:, b * P:], m.vTok[:, b, h * 64:(h + 1) * 64], packed(m.wt, h, b),
                               start=(b == 0), stop=(b == NT - 1), skip_group_check=True)
            mm.then_inc(s_o, 1)

        logits(0)
        for h in range(SB_HEADS + 1):
            if h + 1 < SB_HEADS:
                logits(h + 1)
            if h < SB_HEADS:
                exponents(h)
            if h >= 1:
                out(h - 1)

    def scalar(act):
        act.preload_act_table_set("natural_log_exp_and_others")

        def ln(h):
            act.wait_ge(s_abs, h + 1)
            t = m.sp[:, h % 2, :]
            act.activation(t, t, ACT.Exp).then_inc(s_exp, 1)
            act.wait_ge(s_exp, h + 1)
            act.activation(t, t, ACT.Ln, bias=m.one).then_inc(s_ln, 1)

        ln(0)
        for h in range(SB_HEADS + 1):
            if h + 1 < SB_HEADS:
                ln(h + 1)
            if h < SB_HEADS:
                act.wait_ge(s_x, h + 1)
                if h >= 2:
                    act.wait_ge(s_o, h - 1)
                for n, (c, w) in enumerate(SPANS):
                    ins = act.activation(m.wt[:, h % 2, c:c + w], kit.psum[:, 3 * (h % 2) + n, 0:w], ACT.Exp)
                ins.then_inc(s_w, 1)
            if h >= 1:
                act.wait_ge(s_o, h)
                act.activation(m.xin.high[rows(h - 1), (h - 1) // 2, :], kit.psum[rows(h - 1), 6 + (h - 1) % 2, :], ACT.Copy)\
                   .then_inc(s_oh, 1)

    def vector(dve):
        step = kit.vector_chain(dve)

        def softplus(h):
            dve.wait_ge(s_z, h + 1)
            if h >= 2:
                dve.wait_ge(s_x, h - 1)
            for n, (c, w) in enumerate(SPANS):
                ins = dve.tensor_scalar(m.sp[:, h % 2, c:c + w], kit.psum[:, 3 * (h % 2) + n, 0:w], 0.0, None, ALU.min)
            step(ins)
            for n, (c, w) in enumerate(SPANS):
                sp = m.sp[:, h % 2, c:c + w]
                ins = dve.scalar_tensor_tensor(out=sp, in0=sp, scalar=2.0, in1=kit.psum[:, 3 * (h % 2) + n, 0:w],
                                               op0=ALU.mult, op1=ALU.subtract)
            ins.then_inc(s_abs, 1)

        def add(h):
            dve.wait_ge(s_ln, h + 1)
            for n, (c, w) in enumerate(SPANS):
                sp = m.sp[:, h % 2, c:c + w]
                ins = dve.scalar_tensor_tensor(out=sp, in0=kit.psum[:, 3 * (h % 2) + n, 0:w], scalar=0.0, in1=sp,
                                               op0=ALU.max, op1=ALU.add)
            ins.then_inc(s_sp, 1)

        def low(h):
            dve.wait_ge(s_oh, h + 1)
            dve.tensor_tensor(m.xin.low[rows(h), h // 2, :], kit.psum[rows(h), 6 + h % 2, :],
                              m.xin.high[rows(h), h // 2, :].bitcast(F32), ALU.subtract).then_inc(s_of, 1)

        softplus(0)
        add(0)
        for h in range(SB_HEADS + 1):
            if h + 1 < SB_HEADS:
                softplus(h + 1)
                add(h + 1)
            if h >= 1:
                low(h - 1)

    def gpsimd(pool):
        def mask(h):
            pool.wait_ge(s_sp, h + 1)
            for b in range(NT):
                sp = packed(m.sp, h, b)[:, 0:P]
                ins = pool.tensor_tensor(sp, sp, m.upper_strict[:, :], ALU.mult)
            ins.then_inc(s_lo, 1)

        mask(0)
        for h in range(SB_HEADS):
            if h + 1 < SB_HEADS:
                mask(h + 1)
            pool.wait_ge(s_w, h + 1)
            for b in range(NT):
                w = packed(m.wt, h, b)[:, 0:P]
                ins = pool.affine_select(out=w, in_=w, compare_op=ALU.is_gt, fill=0.0, base=0, pattern=[[1, P]],
                                         channel_multiplier=-1)
            ins.then_inc(s_cut, 1)

    return tensor, vector, scalar, gpsimd


def second_project(nc, kit, m, a):
    gr = Gemm(kit, a["w_in_2"], KD, 0, RW_COLS, True)
    ga = Gemm(kit, a["w_in_2"], KD, RW_COLS, 3 * ATT, False)
    gi = Gemm(kit, a["w_in_2"], KD, RW_COLS + 3 * ATT, IDXW, False)
    s_rot = kit.sem("rotated")
    s_tr = kit.sem("rope_transposed")
    s_tf = kit.sem("rope_transpose_read")
    s_cs = kit.sem("rope_table_landed")

    def tensor(pe):
        for g in (gr, ga, gi):
            g.tensor(pe, m.x_tile)
        gi.wait_free(pe, gi.count - 1)
        n = 0
        for t in range(NT):
            pe.wait_ge(s_rot, t + 1)
            for j in range(4):
                if n >= 4:
                    pe.wait_ge(s_tf, n - 3)
                for q in range(4):
                    k = 4 * j + q
                    if j < 2:
                        mm = pe.transpose(kit.psum[:, n % 4, q * P:(q + 1) * P], m.qkTok[:, t, k * P:(k + 1) * P],
                                          m.ident[:, :])
                    elif j == 2:
                        mm = pe.transpose(kit.psum[:, n % 4, q * P:(q + 1) * P], m.idxTok[:, t, q * P:(q + 1) * P],
                                          m.ident[:, :])
                    elif q < 2:
                        if q == 0:
                            mm = pe.matmul(kit.psum[0:HD, n % 4, 0:P], m.idxTok[:, t, ATT:ATT + HD], m.ident[:, :],
                                           start=True, stop=True)
                        else:
                            mm = pe.matmul(kit.psum[64:P, n % 4, P:2 * P], m.idxTok[:, t, ATT:ATT + HD], m.ident[:, :],
                                           start=True, stop=True)
                mm.then_inc(s_tr, 1)
                n += 1

    def vector(dve):
        step = kit.vector_chain(dve)
        for n in range(gr.count):
            dve.wait_ge(kit.tile_free, gr.tile0 + n + 1)
            p, d = m.rwF[:, n, :], m.shift_tmp[:, n % 2, :]
            step(dve.tensor_tensor(d[:, 1:], p[:, :SEQ - 1], p[:, 1:], ALU.subtract))
            step(dve.tensor_scalar(d[:, 0:1], p[:, 0:1], -1.0, None, ALU.mult))
            step(dve.scalar_tensor_tensor(out=p, in0=d, scalar=m.col("mu", n), in1=p, op0=ALU.mult, op1=ALU.add))
        dve.wait_ge(s_cs, 16)

        def rotate(t, x, n):
            x = x.rearrange("p (h s d) -> p h s d", s=2, d=HD // 2)
            x1, x2 = x[:, :, 0, :], x[:, :, 1, :]
            cos, sin = (across(m.rope[:, t, q * 32:(q + 1) * 32], n) for q in range(2))
            v = [m.rope_tmp[:, q, 0:n * 32].rearrange("p (h d) -> p h d", d=32) for q in range(2)]
            step.mark(dve.tensor_tensor(v[0], x1, sin, ALU.mult))
            step(dve.tensor_tensor(v[1], x2, sin, ALU.mult))
            step.mark(dve.tensor_tensor(x1, x1, cos, ALU.mult))
            step(dve.tensor_tensor(x2, x2, cos, ALU.mult))
            step.mark(dve.tensor_tensor(x1, x1, v[1], ALU.subtract))
            step(dve.tensor_tensor(x2, x2, v[0], ALU.add))

        for t in range(NT):
            ga.wait_free(dve, NT + t)
            rotate(t, m.qkTok[:, t, :], 2 * NHEAD)
        for t in range(NT):
            gi.wait_free(dve, (gi.count // NT - 1) * NT + t)
            rotate(t, m.idxTok[:, t, 0:ATT + HD], NHEAD + 1)
            dve.tensor_copy(m.widx[:, t, :], m.idxTok[:, t, ATT + HD:IDXW]).then_inc(s_rot, 1)

    def scalar(act):
        for n in range(gr.count):
            ps = gr.wait_tile(act, n)
            act.activation(m.rwF[:, n, :], ps, ACT.Copy).then_inc(kit.tile_free, 1)
        for g in (ga, gi):
            for n in range(g.count):
                j, t, w = n // NT, n % NT, g.parts[n // NT][0]
                dst = m.idxTok[:, t, j * WIDE:j * WIDE + w] if g is gi else \
                    m.qkTok[:, t, j * WIDE:(j + 1) * WIDE] if j < 2 else m.vT[:, t, :]
                ps = g.wait_tile(act, n)
                act.activation(dst, ps[:, 0:w], ACT.Copy).then_inc(kit.tile_free, 1)
        n = 0
        for t in range(NT):
            blk = slice(t * P, (t + 1) * P)
            for j in range(4):
                act.wait_ge(s_tr, n + 1)
                ps = kit.psum[:, n % 4, :]
                if j < 3:
                    dst = (m.attF[:, 0:4, blk], m.attF[:, 4:8, blk], m.idxF[:, 0:4, blk])[j]
                    act.activation(dst, ps.rearrange("p (q c) -> p q c", q=4), ACT.Copy,
                                   scale=HD ** -0.5 if j == 0 else 1.0).then_inc(s_tf, 1)
                else:
                    act.activation(m.kidxF[0:HD, blk], ps[0:HD, 0:P], ACT.Copy)
                    act.activation(m.kidxF[64:P, blk], ps[64:P, P:2 * P], ACT.Copy).then_inc(s_tf, 1)
                n += 1

    def gpsimd(pool):
        pool.dma_start(m.rope[:, :, :], a["rope"].rearrange("(t p) c -> p t c", p=P)).then_inc(s_cs, 16)
        kit.split_chunks(pool, gi.last_chunk + SPLIT)

    return tensor, vector, scalar, gpsimd


def sparse_attend(nc, kit, m, a):
    s_ix = kit.sem("index_products_ready")
    s_relu = kit.sem("index_relu_ready")
    s_acc = kit.sem("index_terms_added")
    s_fut = kit.sem("future_filled")
    s_lg = kit.sem("logits_ready")
    s_bias = kit.sem("key_bias_ready")
    s_max = kit.sem("logit_max_ready")
    s_p = kit.sem("probabilities_ready")
    s_tr = kit.sem("probabilities_transposed")
    s_tc = kit.sem("probabilities_copied")
    s_o = kit.sem("sparse_out_ready")
    s_of = kit.sem("sparse_out_read")
    s_yt = kit.sem("sparse_out_transposed")
    s_yc = kit.sem("sparse_out_copied")
    IDX_SCALE = HD ** -0.5 * NHEAD ** -0.5
    STEPS = NT * NHEAD
    ROUNDS = TOPK // 8

    def rows(h):
        return slice((h % 2) * 64, (h % 2) * 64 + 64)

    def split(i):
        t, h = i // NHEAD, i % NHEAD
        return t, h, (t + 1) * P, slice(t * P, (t + 1) * P)

    def score(t):
        at = t * (t + 1) // 2 * P
        return m.score[:, at:at + (t + 1) * P]

    def bias(t):
        at = t * (t + 1) // 2 * P
        return m.bias_r[:, at:at + (t + 1) * P]

    def tensor(pe):
        for i in range(STEPS):
            t, h, n, blk = split(i)
            if i >= 4:
                pe.wait_ge(s_relu, i - 3)
            pe.matmul(kit.psum[:, i % 4, 0:n], m.idxF[rows(h), h // 2, blk], m.kidxF[rows(h), 0:n],
                      start=True, stop=True).then_inc(s_ix, 1)

        def logits(i):
            t, h, n, blk = split(i)
            if i < 3:
                pe.wait_ge(s_relu, STEPS)
            else:
                pe.wait_ge(s_p, i - 2)
            out = kit.psum[:, 1 + i % 3, 0:n]
            pe.matmul(out, m.attF[rows(h), h // 2, blk], m.attF[rows(h), 4 + h // 2, 0:n], start=True, stop=False)
            if h == 0:
                pe.wait_ge(s_bias, t + 1)
            pe.matmul(out, m.ident_r[:, :], bias(t), start=False, stop=True).then_inc(s_lg, 1)

        def turn(i):
            t, h, n, blk = split(i)
            pe.wait_ge(s_p, i + 1)
            if i >= 2:
                pe.wait_ge(s_tc, i - 1)
            for b in range(t + 1):
                mm = pe.transpose(kit.psum[:, 4 + i % 2, b * P:(b + 1) * P], m.prob[:, i % 2, b * P:(b + 1) * P],
                                  m.ident[:, :])
            mm.then_inc(s_tr, 1)

        def out(i):
            t, h, n, blk = split(i)
            pe.wait_ge(s_tc, i + 1)
            if i >= 2:
                pe.wait_ge(s_of, i - 1)
            for b in range(t + 1):
                mm = pe.matmul(kit.psum[:, 6 + i % 2, h * 64:(h + 1) * 64], m.probT[:, i % 2, b * P:(b + 1) * P],
                               m.vT[:, b, h * 64:(h + 1) * 64], start=(b == 0), stop=(b == t))
            mm.then_inc(s_o, 1)

        def turn_out(t):
            pe.wait_ge(s_of, (t + 1) * NHEAD)
            if t >= 1:
                pe.wait_ge(s_yc, t)
            for q in range(NHP):
                mm = pe.transpose(kit.psum[:, 0, q * P:(q + 1) * P], m.ybTok[:, t % 2, q * P:(q + 1) * P], m.ident[:, :])
            mm.then_inc(s_yt, 1)

        for k in range(STEPS + 5):
            if k < STEPS:
                logits(k)
            if 2 <= k < STEPS + 2:
                turn(k - 2)
            if 3 <= k < STEPS + 3:
                out(k - 3)
            if k >= 5 and (k - 4) % NHEAD == 0:
                turn_out((k - 4) // NHEAD - 1)

    def scalar(act):
        for i in range(STEPS):
            t, h, n, blk = split(i)
            act.wait_ge(s_ix, i + 1)
            if i >= 2:
                act.wait_ge(s_acc, i - 1)
            act.activation(m.relu[:, i % 2, 0:n], kit.psum[:, i % 4, 0:n], ACT.Relu).then_inc(s_relu, 1)

        def exp(i):
            n = split(i)[2]
            act.wait_ge(s_max, i + 1)
            if i >= 2:
                act.wait_ge(s_tr, i - 1)
            act.activation(m.prob[:, i % 2, 0:n], kit.psum[:, 1 + i % 3, 0:n], ACT.Exp, bias=m.nmax[:, i % 4, :],
                           accum_out=m.psum_row[:, i % 4, :]).then_inc(s_p, 1)

        def copy(i):
            n = split(i)[2]
            act.wait_ge(s_tr, i + 1)
            if i >= 2:
                act.wait_ge(s_o, i - 1)
            else:
                act.wait_ge(s_acc, STEPS)
            act.activation(m.probT[:, i % 2, 0:n], kit.psum[:, 4 + i % 2, 0:n], ACT.Copy).then_inc(s_tc, 1)

        for k in range(STEPS + 5):
            if k < STEPS:
                exp(k)
            if 2 <= k < STEPS + 2:
                copy(k - 2)
            if k >= 5 and (k - 4) % NHEAD == 0:
                t = (k - 4) // NHEAD - 1
                act.wait_ge(s_yt, t + 1)
                act.activation(m.ybF[:, :, t * P:(t + 1) * P], kit.psum[:, 0, :].rearrange("p (q c) -> p q c", q=NHP),
                               ACT.Copy).then_inc(s_yc, 1)

    def gpsimd(pool):
        for t in range(NT):
            pool.wait_ge(s_acc, (t + 1) * NHEAD)
            last = score(t)[:, t * P:]
            pool.affine_select(out=last, in_=last, compare_op=ALU.is_ge, fill=FUTURE,
                               base=0, pattern=[[-1, P]], channel_multiplier=1).then_inc(s_fut, 1)

    def vector(dve):
        step = kit.vector_chain(dve)
        for i in range(STEPS):
            t, h, n, blk = split(i)
            dve.wait_ge(s_relu, i + 1)
            r, w, sc = m.relu[:, i % 2, 0:n], m.widx[:, t, h:h + 1], score(t)
            if h == 0:
                dve.tensor_scalar(sc, r, w, 0.0, ALU.mult, ALU.add).then_inc(s_acc, 1)
            else:
                dve.wait_ge(s_acc, i)
                dve.scalar_tensor_tensor(out=sc, in0=r, scalar=w, in1=sc, op0=ALU.mult, op1=ALU.add).then_inc(s_acc, 1)

        def choose(t, part):
            sc, wk = score(t), m.work[:, 0:(t + 1) * P]
            if t == 0:
                step(dve.tensor_scalar(sc, sc, FUTURE / 2, None, ALU.is_ge))
            else:
                if part == 0:
                    step(dve.tensor_scalar(wk, sc, IDX_SCALE, None, ALU.mult))
                for _ in range(ROUNDS // NHEAD):
                    step(dve.max(m.best[:, :], wk))
                    step(dve.match_replace(wk, m.best[:, :], wk, REMOVED))
                if part < NHEAD - 1:
                    return
                step(dve.tensor_scalar(wk, wk, REMOVED, None, ALU.is_equal))
                step(dve.scalar_tensor_tensor(out=sc, in0=sc, scalar=FUTURE / 2, in1=wk, op0=ALU.is_ge, op1=ALU.mult))
            dve.tensor_scalar(bias(t), sc, -FAR, FAR, ALU.mult, ALU.add).then_inc(s_bias, 1)

        def peak(i):
            t, h, n, blk = split(i)
            dve.wait_ge(s_lg, i + 1)
            dve.tensor_reduce(m.nmax[:, i % 4, :], kit.psum[:, 1 + i % 3, 0:n], AX_X, ALU.max, negate=True)\
               .then_inc(s_max, 1)

        def finish(i):
            t, h, n, blk = split(i)
            dve.wait_ge(s_p, i + 1)
            step(dve.reciprocal(m.prec[:, i % 2, :], m.psum_row[:, i % 4, :]))
            dve.wait_ge(s_o, i + 1)
            if t >= 2 and h == 0:
                dve.wait_ge(s_yt, t - 1)
            dve.tensor_scalar(m.ybTok[:, t % 2, h * 64:(h + 1) * 64], kit.psum[:, 6 + i % 2, h * 64:(h + 1) * 64],
                              m.prec[:, i % 2, :], None, ALU.mult).then_inc(s_of, 1)

        dve.wait_ge(s_fut, NT)
        choose(0, 0)
        for k in range(STEPS + 3):
            if k < STEPS:
                peak(k)
            if k >= 3:
                finish(k - 3)
            if k < STEPS and k // NHEAD + 1 < NT:
                choose(k // NHEAD + 1, k % NHEAD)

    return tensor, vector, scalar, gpsimd


def rwkv_prepare(nc, kit, m, a):
    s_up = kit.sem("lora_weights_landed")
    s_lin = kit.sem("lora_inputs_ready")
    s_lo = kit.sem("lora_products_ready")
    s_act = kit.sem("lora_products_read")
    s_kk = kit.sem("key_squares_ready")
    s_kn = kit.sem("key_norm_sums_ready")
    s_kr = kit.sem("key_norm_root")
    s_cs = kit.sem("decay_scan_ready")
    s_ex = kit.sem("decay_factors_ready")

    def gpsimd(pool):
        pool.dma_start(m.up_w[0:64, :], a["w_decay_up"]).then_inc(s_up, 16)
        pool.dma_start(m.up_w[64:P, :], a["a_up"]).then_inc(s_up, 16)

    def tensor(pe):
        pe.wait_ge(s_up, 32)
        pe.wait_ge(s_lin, 1)
        for n in range(2 * NHP):
            kind, t = n // NHP, n % NHP
            if n >= 4:
                pe.wait_ge(s_act, n - 3)
            f = slice(t * P, (t + 1) * P)
            if kind == 0:
                mm = pe.matmul(kit.psum[:, n % 4, :], m.up_w[0:64, f], m.rwF[0:64, 12, :], start=True, stop=True)
            else:
                mm = pe.matmul(kit.psum[:, n % 4, :], m.up_w[64:P, f], m.rwF[64:P, 12, :], start=True, stop=True)
            mm.then_inc(s_lo, 1)
        for t in range(NHP):
            pe.wait_ge(s_kk, t + 1)
            pe.matmul(kit.psum[:, 4 + t, :], m.halves[:, :], m.sqF[:, t, :], start=True, stop=True).then_inc(s_kn, 1)

    def scalar(act):
        act.activation(m.rwF[0:64, 12, :], m.rwF[0:64, 12, :], ACT.Tanh).then_inc(s_lin, 1)
        act.activation(m.rwF[:, 13, :], m.rwF[:, 13, :], ACT.Sigmoid).then_inc(s_lin, 1)
        for n in range(2 * NHP):
            kind, t = n // NHP, n % NHP
            act.wait_ge(s_lo, n + 1)
            ps = kit.psum[:, n % 4, :]
            if kind == 0:
                act.activation(m.sg[:, t, :], ps, ACT.Sigmoid, bias=m.col("w0", t)).then_inc(s_act, 1)
            else:
                act.activation(m.aF[:, t, :], ps, ACT.Sigmoid, bias=m.col("a0", t)).then_inc(s_act, 1)
        for t in range(NHP):
            act.wait_ge(s_kn, t + 1)
            act.activation(m.sqF[:, t, :], kit.psum[:, 4 + t, :], ACT.Sqrt).then_inc(s_kr, 1)
        for t in range(NHP):
            for c in range(NT):
                n = NT * t + c
                act.wait_ge(s_cs, n + 1)
                blk = slice(c * P, (c + 1) * P)
                mid, nmid = m.mid[:, 0, n:n + 1], m.mid[:, 1, n:n + 1]
                act.activation(m.eF[:, 0, n % 2, :], m.prev_cs[:, n % 2, :], ACT.Exp, bias=mid, scale=-DECAY_UNIT)
                act.activation(m.eF[:, 1, n % 2, :], m.cs[:, n % 2, :], ACT.Exp, bias=mid, scale=-DECAY_UNIT)
                act.activation(m.eF[:, 2, n % 2, :], m.cs[:, n % 2, :], ACT.Exp, bias=nmid, scale=DECAY_UNIT)
                act.activation(m.emid[:, c, t:t + 1], nmid, ACT.Exp).then_inc(s_ex, 1)

    def vector(dve):
        step = kit.vector_chain(dve)
        dve.wait_ge(s_act, 2 * NHP)
        for t in range(NHP):
            k, kk = m.rwF[:, 4 + t, :], m.kkF[:, t, :]
            step(dve.tensor_scalar(kk, k, m.col("k_k", t), None, ALU.mult))
            dve.tensor_tensor(m.sqF[:, t, :], kk, kk, ALU.mult).then_inc(s_kk, 1)
        for t in range(NHP):
            k, ae = m.rwF[:, 4 + t, :], m.tmpF[:, 0, :]
            step(dve.tensor_scalar(ae, m.aF[:, t, :], -1.0, m.col("k_a", t), ALU.add, ALU.mult))
            step(dve.scalar_tensor_tensor(out=k, in0=ae, scalar=1.0, in1=k, op0=ALU.add, op1=ALU.mult))
            dve.wait_ge(s_kr, t + 1)
            nrm = m.sqF[:, t, :]
            step(dve.tensor_scalar(nrm, nrm, 1e-12, None, ALU.max))
            step(dve.reciprocal(nrm, nrm))
            step(dve.tensor_tensor(m.kkF[:, t, :], m.kkF[:, t, :], nrm, ALU.mult))
            step(dve.tensor_tensor(m.aF[:, t, :], m.aF[:, t, :], m.kkF[:, t, :], ALU.mult))

        def scan(n):
            t, c = n // NT, n % NT
            sg = m.sg[:, t, c * P:(c + 1) * P]
            if n >= 2:
                dve.wait_ge(s_ex, n - 1)
            cs = m.cs[:, n % 2, :]
            step(dve.tensor_tensor_scan(cs, m.ones[:, :], sg, 0.0, ALU.mult, ALU.add))
            step(dve.tensor_tensor(m.prev_cs[:, n % 2, :], cs, sg, ALU.subtract))
            step(dve.tensor_scalar(m.mid[:, 0, n:n + 1], cs[:, P - 1:P], DECAY_UNIT / 2, None, ALU.mult))
            dve.tensor_scalar(m.mid[:, 1, n:n + 1], cs[:, P - 1:P], -DECAY_UNIT / 2, None, ALU.mult).then_inc(s_cs, 1)

        def scale(n):
            t, c = n // NT, n % NT
            blk = slice(c * P, (c + 1) * P)
            dve.wait_ge(s_ex, n + 1)
            e = [m.eF[:, q, n % 2, :] for q in range(3)]
            for x, f in ((m.kkF, e[0]), (m.rwF, e[1]), (m.aF, e[2])):
                step(dve.tensor_tensor(x[:, t, blk], x[:, t, blk], f, ALU.mult))
            k = m.rwF[:, 4 + t, blk]
            step(dve.tensor_tensor(k, k, e[2], ALU.mult))

        for n in range(NT * NHP + 1):
            if n < NT * NHP:
                scan(n)
            if n >= 1:
                scale(n - 1)

    return tensor, vector, scalar, gpsimd


def rwkv_scan(nc, kit, m, a):
    s_tt = kit.sem("chunk_turned")
    s_tr = kit.sem("chunk_turn_read")
    s_pr = kit.sem("pair_products_ready")
    s_pm = kit.sem("pair_products_masked")
    s_lm = kit.sem("level_matrix_ready")
    s_u = kit.sem("level_u_ready")
    s_uc = kit.sem("level_u_copied")
    s_dl = kit.sem("level_change_ready")
    s_xy = kit.sem("inverse_updated")
    s_d = kit.sem("value_mix_ready")
    s_dc = kit.sem("value_mix_copied")
    s_w = kit.sem("wy_products_ready")
    s_wc = kit.sem("wy_products_copied")
    s_z = kit.sem("state_reads_ready")
    s_sa = kit.sem("corrections_ready")
    s_n = kit.sem("new_state_ready")
    s_st = kit.sem("state_scaled")
    s_y = kit.sem("recurrent_out_ready")
    s_yc = kit.sem("recurrent_out_read")
    LEVELS = 7

    def rows(g):
        return slice(g * 64, g * 64 + 64)

    def quad(bank):
        return kit.psum[:, bank, :].rearrange("p (q c) -> p q c", q=NHP)

    kap = lambda g, q, blk: m.kkF[rows(g), q, blk]
    rho = lambda g, q, blk: m.rwF[rows(g), q, blk]
    bet = lambda g, q, blk: m.aF[rows(g), q, blk]
    gam = lambda g, q, blk: m.rwF[rows(g), 4 + q, blk]
    PAIRS = [(kap, bet), (bet, kap), (gam, kap), (bet, rho), (gam, rho)]

    def tensor(pe):
        for c in range(NT):
            blk = slice(c * P, (c + 1) * P)
            if c >= 1:
                pe.wait_ge(s_yc, 2 * c)
            for n, src in enumerate((m.kkF, m.aF, m.rwF, m.rwF)):
                off = (0, 0, 4, 8)[n]
                for q in range(NHP):
                    mm = pe.transpose(kit.psum[:, n, q * P:(q + 1) * P], src[:, off + q, blk], m.ident[:, :])
                mm.then_inc(s_tt, 1)
            if c >= 1:
                pe.wait_ge(s_st, c)
            for n, (left, right) in enumerate(PAIRS):
                for g in range(2):
                    k = 2 * n + g
                    if k >= 4:
                        pe.wait_ge(s_pm, 10 * c + k - 3)
                    for q in range(NHP):
                        mm = pe.matmul(kit.psum[:, 4 + k % 4, q * P:(q + 1) * P], left(g, q, blk), right(g, q, blk),
                                       start=True, stop=True)
                    mm.then_inc(s_pr, 1)
            pe.wait_ge(s_tr, 4 * (c + 1))
            pe.wait_ge(s_pm, 10 * (c + 1))
            for lv in range(1, LEVELS):
                for g in range(2):
                    i = (c * (LEVELS - 1) + lv - 1) * 2 + g
                    pe.wait_ge(s_lm, i + 1)
                    pe.wait_ge(s_xy, (c * LEVELS + lv - 1) * 2 + g + 1)
                    for q in range(NHP):
                        mm = pe.matmul(kit.psum[:, g, q * P:(q + 1) * P], m.level[:, g, q, :], m.X[:, g, q, :],
                                       start=True, stop=True)
                    mm.then_inc(s_u, 1)
                for g in range(2):
                    i = (c * (LEVELS - 1) + lv - 1) * 2 + g
                    pe.wait_ge(s_uc, i + 1)
                    for q in range(NHP):
                        mm = pe.matmul(kit.psum[:, 2 + g, q * P:(q + 1) * P], m.Y[:, g, q, :], m.U[:, g, q, :],
                                       start=True, stop=True)
                    if lv < LEVELS - 1:
                        for q in range(NHP):
                            mm = pe.matmul(kit.psum[:, 4 + g, q * P:(q + 1) * P], m.U[:, g, q, :], m.Y[:, g, q, :],
                                           start=True, stop=True)
                    mm.then_inc(s_dl, 1)
            for g in range(2):
                pe.wait_ge(s_xy, (c * LEVELS + LEVELS - 1) * 2 + g + 1)
            for g in range(2):
                for q in range(NHP):
                    h = 2 * q + g
                    mm = pe.matmul(kit.psum[:, 0, h * 64:(h + 1) * 64], m.gk[:, g, q, :], m.vC[:, h * 64:(h + 1) * 64],
                                   start=True, stop=True)
            mm.then_inc(s_d, 1)
            for g in range(2):
                for q in range(NHP):
                    h = 2 * q + g
                    mm = pe.matmul(kit.psum[rows(g), 1 + g, q * P:(q + 1) * P], m.kapC[:, h * 64:(h + 1) * 64],
                                   m.X[:, g, q, :], start=True, stop=True)
            mm.then_inc(s_w, 1)
            pe.wait_ge(s_dc, c + 1)
            pe.wait_ge(s_wc, c + 1)
            if c >= 1:
                pe.wait_ge(s_st, c)
            for g in range(2):
                for q in range(NHP):
                    h = 2 * q + g
                    z = kit.psum[:, 3 + g, q * 64:(q + 1) * 64]
                    mm = pe.matmul(z, m.X[:, g, q, :], m.D[:, h * 64:(h + 1) * 64], start=True, stop=(c == 0))
                    if c > 0:
                        mm = pe.matmul(z, m.WT[rows(g), q, :], m.S[rows(g), q, :], start=False, stop=True)
            mm.then_inc(s_z, 1)
            pe.wait_ge(s_sa, c + 1)
            if c < NT - 1:
                for g in range(2):
                    for q in range(NHP):
                        h = 2 * q + g
                        n = kit.psum[rows(g), 5, q * 64:(q + 1) * 64]
                        pe.matmul(n, m.betC[:, h * 64:(h + 1) * 64], m.SA[:, h * 64:(h + 1) * 64],
                                  start=True, stop=False)
                        mm = pe.matmul(n, m.gamC[:, h * 64:(h + 1) * 64], m.vC[:, h * 64:(h + 1) * 64],
                                       start=False, stop=True)
                mm.then_inc(s_n, 1)
            for g in range(2):
                for q in range(NHP):
                    h = 2 * q + g
                    y = kit.psum[rows(g), 6 + g, q * P:(q + 1) * P]
                    pe.matmul(y, m.SA[:, h * 64:(h + 1) * 64], m.br[:, g, q, :], start=True, stop=False)
                    mm = pe.matmul(y, m.vC[:, h * 64:(h + 1) * 64], m.gr[:, g, q, :], start=False, stop=(c == 0))
                    if c > 0:
                        mm = pe.matmul(y, m.S[rows(g), q, :], rho(g, q, blk), start=False, stop=True)
            mm.then_inc(s_y, 1)

    def scalar(act):
        for c in range(NT):
            blk = slice(c * P, (c + 1) * P)
            for n, dst in enumerate((m.kapC, m.betC, m.gamC, m.vC)):
                act.wait_ge(s_tt, 4 * c + n + 1)
                if c >= 1 and n == 0:
                    act.wait_ge(s_y, c)
                act.activation(dst[:, :], kit.psum[:, n, :], ACT.Copy).then_inc(s_tr, 1)
            for lv in range(1, LEVELS):
                for g in range(2):
                    i = (c * (LEVELS - 1) + lv - 1) * 2 + g
                    act.wait_ge(s_u, i + 1)
                    act.activation(m.U[:, g], quad(g), ACT.Copy).then_inc(s_uc, 1)
            act.wait_ge(s_d, c + 1)
            act.activation(m.D[:, :], kit.psum[:, 0, :], ACT.Copy).then_inc(s_dc, 1)
            act.wait_ge(s_w, c + 1)
            act.activation(m.WT[0:64], quad(1)[0:64], ACT.Copy)
            act.activation(m.WT[64:P], quad(2)[64:P], ACT.Copy).then_inc(s_wc, 1)
            act.wait_ge(s_z, c + 1)
            sa = m.SA[:, :].rearrange("p (q g d) -> p q g d", g=2, d=64)
            for g in range(2):
                ins = act.activation(sa[:, :, g, :], kit.psum[:, 3 + g, 0:NHP * 64].rearrange("p (q d) -> p q d", d=64),
                                     ACT.Copy, scale=-1.0)
            ins.then_inc(s_sa, 1)
            act.wait_ge(s_y, c + 1)
            for g in range(2):
                act.activation(m.yaF[rows(g), :, blk], quad(6 + g)[rows(g)], ACT.Copy).then_inc(s_yc, 1)

    def gpsimd(pool):
        for c in range(NT):
            for lv in range(1, LEVELS):
                for g in range(2):
                    i = (c * (LEVELS - 1) + lv - 1) * 2 + g
                    pool.wait_ge(s_pm, 10 * c + g + 1)
                    if i >= 2:
                        pool.wait_ge(s_u, i - 1)
                    pool.tensor_tensor(m.level[:, g], m.kb[:, g], across(m.pair_mask[:, 1 + lv, :], NHP), ALU.mult)\
                        .then_inc(s_lm, 1)

    def vector(dve):
        step = kit.vector_chain(dve)
        for c in range(NT):
            if c >= 1:
                dve.wait_ge(s_y, c)
                dve.wait_ge(s_lm, 2 * (LEVELS - 1) * c)
            for n in range(len(PAIRS)):
                for g in range(2):
                    k = 2 * n + g
                    dve.wait_ge(s_pr, 10 * c + k + 1)
                    ps = quad(4 + k % 4)
                    if n == 0:
                        step(dve.tensor_copy(m.kb[:, g], ps))
                        step(dve.tensor_tensor(m.Y[:, g], m.kb[:, g], across(m.pair_mask[:, 1, :], NHP), ALU.mult))
                        dve.tensor_tensor(m.Y[:, g], across(m.ident[:, :], NHP), m.Y[:, g], ALU.subtract)\
                           .then_inc(s_pm, 1)
                    elif n == 1:
                        step(dve.tensor_tensor(m.X[:, g], ps, across(m.pair_mask[:, 0, :], NHP), ALU.mult))
                        dve.tensor_tensor(m.X[:, g], across(m.ident[:, :], NHP), m.X[:, g], ALU.subtract)\
                           .then_inc(s_pm, 1)
                        dve.wait_ge(s_pm, 10 * c + k + 1)
                        dve.engine_nop().then_inc(s_xy, 1)
                    else:
                        dst = (m.gk, m.br, m.gr)[n - 2]
                        mask = m.upper_strict if n == 2 else m.upper
                        dve.tensor_tensor(dst[:, g], ps, across(mask[:, :], NHP), ALU.mult).then_inc(s_pm, 1)
            for lv in range(1, LEVELS):
                for g in range(2):
                    i = (c * (LEVELS - 1) + lv - 1) * 2 + g
                    dve.wait_ge(s_dl, i + 1)
                    if lv < LEVELS - 1:
                        step(dve.tensor_tensor(m.Y[:, g], m.Y[:, g], quad(4 + g), ALU.subtract))
                    dve.tensor_tensor(m.X[:, g], m.X[:, g], quad(2 + g), ALU.subtract).then_inc(s_xy, 1)
            if c < NT - 1:
                dve.wait_ge(s_n, c + 1)
                dve.wait_ge(s_y, c + 1)
                s, new = m.S[:, :, :], kit.psum[:, 5, 0:NHP * 64].rearrange("p (q d) -> p q d", d=64)
                if c > 0:
                    step(dve.tensor_tensor(s, s, new, ALU.add))
                else:
                    step(dve.tensor_copy(s, new))
                step(dve.tensor_tensor(s, s, over(m.emid[:, c, :], 64), ALU.mult))
                dve.tensor_tensor(s, s, over(m.emid[:, c + 1, :], 64), ALU.mult).then_inc(s_st, 1)

    return tensor, vector, scalar, gpsimd


def rwkv_finish(nc, kit, m, a):
    s_up = kit.sem("gate_weights_landed")
    s_gl = kit.sem("gate_products_ready")
    s_gr = kit.sem("gate_products_read")
    s_mu = kit.sem("head_sums_ready")
    s_cen = kit.sem("head_centred")
    s_sq = kit.sem("head_squares_ready")
    s_var = kit.sem("head_square_sums_ready")
    s_rt = kit.sem("head_root_ready")
    s_bo = kit.sem("bonus_terms_ready")
    s_bp = kit.sem("bonus_sums_ready")
    s_yb = kit.sem("sparse_out_high")
    s_done = kit.sem("recurrent_out_gated")
    s_high = kit.sem("recurrent_out_high")

    def gpsimd(pool):
        pool.dma_start(m.g_up[:, :], a["g_up"]).then_inc(s_up, 16)

    def tensor(pe):
        for t in range(NHP):
            pe.matmul(kit.psum[:, t, :], m.halves[:, :], m.yaF[:, t, :], start=True, stop=True).then_inc(s_mu, 1)
        for t in range(NHP):
            pe.wait_ge(s_bo, t + 1)
            pe.matmul(kit.psum[:, 4 + t, :], m.halves[:, :], m.bonus[:, t, :], start=True, stop=True).then_inc(s_bp, 1)
        for t in range(NHP):
            pe.wait_ge(s_sq, t + 1)
            pe.matmul(kit.psum[:, t, :], m.halves[:, :], m.sqF[:, t, :], start=True, stop=True).then_inc(s_var, 1)
        pe.wait_ge(s_up, 16)
        for t in range(NHP):
            pe.wait_ge(s_gr, t + 1)
            pe.matmul(kit.psum[:, 4 + t, :], m.g_up[:, t * P:(t + 1) * P], m.rwF[:, 13, :], start=True, stop=True)\
              .then_inc(s_gl, 1)

    def scalar(act):
        for t in range(NHP):
            act.wait_ge(s_cen, t + 1)
            act.activation(m.sqF[:, t, :], m.yaF[:, t, :], ACT.Square).then_inc(s_sq, 1)
        for t in range(NHP):
            act.wait_ge(s_var, t + 1)
            act.activation(m.sqF[:, t, :], kit.psum[:, t, :], ACT.Sqrt, bias=m.eps["lnx"], scale=1.0 / HD)\
               .then_inc(s_rt, 1)
        for t in range(NHP):
            act.wait_ge(s_done, t + 1)
            if t == 0:
                act.wait_ge(s_bp, NHP)
            act.activation(m.yaR.high[:, t, :], m.yaF[:, t, :], ACT.Copy).then_inc(s_high, 1)
        for t in range(NHP):
            act.activation(m.ybR.high[:, t, :], m.ybF[:, t, :], ACT.Copy).then_inc(s_yb, 1)

    def vector(dve):
        step = kit.vector_chain(dve)
        for t in range(NHP):
            dve.wait_ge(s_mu, t + 1)
            y = m.yaF[:, t, :]
            dve.scalar_tensor_tensor(out=y, in0=kit.psum[:, t, :], scalar=-1.0 / HD, in1=y, op0=ALU.mult, op1=ALU.add)\
               .then_inc(s_cen, 1)
        for t in range(NHP):
            dve.scalar_tensor_tensor(out=m.bonus[:, t, :], in0=m.rwF[:, t, :], scalar=m.col("r_k", t),
                                     in1=m.rwF[:, 4 + t, :], op0=ALU.mult, op1=ALU.mult).then_inc(s_bo, 1)
        for t in range(NHP):
            dve.wait_ge(s_bp, t + 1)
            dve.tensor_tensor(m.bonus[:, t, :], m.rwF[:, 8 + t, :], kit.psum[:, 4 + t, :], ALU.mult).then_inc(s_gr, 1)
        for t in range(NHP):
            y, r = m.yaF[:, t, :], m.sqF[:, t, :]
            dve.wait_ge(s_rt, t + 1)
            step(dve.reciprocal(r, r))
            step(dve.tensor_tensor(y, y, r, ALU.mult))
            step(dve.tensor_scalar(y, y, m.col("lnx_g", t), m.col("lnx_b", t), ALU.mult, ALU.add))
            step(dve.tensor_tensor(y, y, m.bonus[:, t, :], ALU.add))
            dve.wait_ge(s_gl, t + 1)
            dve.tensor_tensor(y, y, kit.psum[:, 4 + t, :], ALU.mult).then_inc(s_done, 1)
        for t in range(NHP):
            dve.wait_ge(s_high, t + 1)
            step.mark(dve.tensor_tensor(m.yaR.low[:, t, :], m.yaF[:, t, :], m.yaR.high[:, t, :].bitcast(F32), ALU.subtract))
        step.wait()
        for t in range(NHP):
            dve.wait_ge(s_yb, t + 1)
            dve.tensor_tensor(m.ybR.low[:, t, :], m.ybF[:, t, :], m.ybR.high[:, t, :].bitcast(F32), ALU.subtract)

    return tensor, vector, scalar, gpsimd


def merge(nc, kit, m, a):
    PARTS = D // WIDE
    gate0 = RW_COLS + 3 * ATT + IDXW
    plan = []
    for j in range(PARTS):
        plan.append((Gemm(kit, a["w_in_2"], KD, gate0 + j * WIDE, WIDE, True),
                     Gemm(kit, a["w_in_2"], KD, gate0 + D + j * WIDE, WIDE, True),
                     Gemm(kit, a["w_o_rwkv"], RW // P, j * WIDE, WIDE, True),
                     Gemm(kit, a["w_o_att"], ATT // P, j * WIDE, WIDE, True)))
    s_used = kit.sem("gates_used")
    s_sum = kit.sem("merged_ready")
    s_high = kit.sem("merged_high_ready")

    def tensor(pe):
        for ga, gb, ya, yb in plan:
            ga.tensor(pe, m.x_tile)
            gb.tensor(pe, m.x_tile)
            ya.tensor(pe, lambda k: Split(m.yaR.high[:, k, :], m.yaR.low[:, k, :]))
            yb.tensor(pe, lambda k: Split(m.ybR.high[:, k, :], m.ybR.low[:, k, :]))

    def scalar(act):
        for j, (ga, gb, ya, yb) in enumerate(plan):
            ga.take_over(act)
            for g, dst in ((ga, m.gate_a), (gb, m.gate_b)):
                for n in range(4):
                    ps = g.wait_tile(act, n)
                    if j >= 1:
                        act.wait_ge(s_used, 4 * (j - 1) + n + 1)
                    act.activation(dst[:, n, :], ps, ACT.Sigmoid).then_inc(kit.tile_free, 1)
            for n in range(4):
                act.wait_ge(s_sum, 4 * j + n + 1)
                act.activation(m.mergedR.high[:, 4 * j + n, :], m.gate_a[:, n, :], ACT.Copy).then_inc(s_high, 1)

    def vector(dve):
        step = kit.vector_chain(dve)
        for j, (ga, gb, ya, yb) in enumerate(plan):
            gb.wait_free(dve, 3)
            for g, gate in ((ya, m.gate_a), (yb, m.gate_b)):
                for n in range(4):
                    ps = g.wait_tile(dve, n)
                    dve.tensor_tensor(gate[:, n, :], gate[:, n, :], ps, ALU.mult).then_inc(kit.tile_free, 1)
            yb.wait_free(dve, 3)
            for n in range(4):
                dve.tensor_tensor(m.gate_a[:, n, :], m.gate_a[:, n, :], m.gate_b[:, n, :], ALU.add).then_inc(s_sum, 1)
            for n in range(4):
                dve.wait_ge(s_high, 4 * j + n + 1)
                dve.tensor_tensor(m.mergedR.low[:, 4 * j + n, :], m.gate_a[:, n, :],
                                  m.mergedR.high[:, 4 * j + n, :].bitcast(F32), ALU.subtract).then_inc(s_used, 1)

    def gpsimd(pool):
        kit.split_chunks(pool, plan[-1][-1].last_chunk + SPLIT)

    return tensor, vector, scalar, gpsimd


def ffn(nc, kit, m, a, final):
    PARTS = [(0, 12), (12, 10)]
    plan, down = [], []
    for f0, nf in PARTS:
        sub = []
        for c in range(0, nf * P, WIDE):
            n = min(WIDE, nf * P - c)
            sub.append((Gemm(kit, a["w_ffn_in"], KD, f0 * P + c, n, True),
                        Gemm(kit, a["w_ffn_in"], KD, D_FF2 + f0 * P + c, n, True)))
        plan.append(sub)
        down.append(Gemm(kit, a["w_ffn_out"], nf, 0, D, False, k_from=f0))
    t, v, act_norm, pool_out, rows, add = norm_rows(nc, kit, m, 1.0, None, "last", "norm", "last", gemms=(down[1],),
                                                    final=final)
    s_mul = kit.sem("ffn_hidden_ready")
    s_high = kit.sem("ffn_high_ready")
    s_hid = kit.sem("ffn_split_ready")
    HALF = [0, 12]

    def tensor(pe):
        for q, sub in enumerate(plan):
            for gg, gu in sub:
                gg.tensor(pe, m.x_tile)
                gu.tensor(pe, m.x_tile)
            down[q].tensor(pe, m.hidden_tile, before=lambda k, q=q: pe.wait_ge(s_hid, HALF[q] + k))

    def scalar(act):
        n = 0
        for q, sub in enumerate(plan):
            for gg, gu in sub:
                gg.take_over(act)
                for i in range(gg.count):
                    ps = gg.wait_tile(act, i)
                    if n + i >= 4:
                        act.wait_ge(s_hid, n + i - 3)
                    act.activation(m.gate_a[:, (n + i) % 4, :], ps, ACT.Silu).then_inc(kit.tile_free, 1)
                for i in range(gu.count):
                    act.wait_ge(s_mul, n + i + 1)
                    if q == 1 and n + i == HALF[1]:
                        act.wait_ge(kit.tile_ready, down[0].tile0 + down[0].count)
                    act.activation(m.hid.high[:, n + i - HALF[q], :], m.gate_a[:, (n + i) % 4, :], ACT.Copy)\
                       .then_inc(s_high, 1)
                n += gu.count
        act_norm(act)

    def vector(dve):
        n = 0
        for q, sub in enumerate(plan):
            for gg, gu in sub:
                gu.take_over(dve)
                for i in range(gu.count):
                    ps = gu.wait_tile(dve, i)
                    gt = m.gate_a[:, (n + i) % 4, :]
                    dve.tensor_tensor(gt, gt, ps, ALU.mult).then_inc(kit.tile_free, 1)
                    gu.wait_free(dve, i)
                    dve.engine_nop().then_inc(s_mul, 1)
                for i in range(gu.count):
                    dve.wait_ge(s_high, n + i + 1)
                    k = n + i - HALF[q]
                    dve.tensor_tensor(m.hid.low[:, k, :], m.gate_a[:, (n + i) % 4, :],
                                      m.hid.high[:, k, :].bitcast(F32), ALU.subtract).then_inc(s_hid, 1)
                n += gu.count
            add(dve, down[q], 1.0, q == 1)
        v(dve)

    def gpsimd(pool):
        rows(pool)
        kit.split_chunks(pool, down[1].last_chunk + SPLIT)
        pool_out(pool)

    return tensor, vector, scalar, gpsimd


HID = 16
BIG = 20768


class Memory:

    def __init__(self, kit):
        self.h = self.own(kit, "residual", NT, D)
        xin = kit.tensor_sb("x_split", [P, 2, KD, SEQ], F32R)
        self.xin = Split(xin[:, 0], xin[:, 1])
        consts = kit.tensor_sb("constants", [P, 7, P])
        self.ident, self.ones, self.upper, self.upper_strict, self.halves, self.neg_ones, self.neg_lower = \
            (consts[:, n] for n in range(7))
        self.ident_r = kit.tensor_sb("exact_identity", [P, P], F32R)[:, :]
        self.pair_mask = self.own(kit, "pair_masks", 8, P)
        self.par_cols = self.own(kit, "parameter_columns", 2, P)
        self.head_rows = self.own(kit, "head_rows", 3, SSM_HEADS)
        self.eps_mem = kit.tensor_sb("epsilons", [P, 5])
        self.eps = {k: self.eps_mem[:, n:n + 1] for n, k in enumerate(("ln", "norm", "lnx", "rms"))}
        self.one = self.eps_mem[:, 4:5]
        self.stats = kit.tensor_sb("norm_stats", [P, NT, 2, 6])
        self.mv = kit.tensor_sb("mean_variance", [P, NT, 2])
        self.ms, self.std, self.rstd = (self.own(kit, n, NT) for n in ("mean_square", "deviation", "inverse_deviation"))
        self.gss, self.gstd = (kit.tensor_sb(n, [P, NT, SSM_GROUPS]) for n in ("group_squares", "group_deviation"))
        self.best = kit.tensor_sb("best", [P, 8])
        self.widx = kit.tensor_sb("index_weights", [P, NT, 8])
        self.nmax, self.psum_row = (kit.tensor_sb(n, [P, 4, 1]) for n in ("neg_max", "prob_sum"))
        self.prec = kit.tensor_sb("prob_inverse", [P, 2, 1])
        self.mid = kit.tensor_sb("half_chunk_decay", [P, 2, NT * NHP])
        self.emid = kit.tensor_sb("exp_half_chunk_decay", [P, NT, NHP])
        self.rows_mem = kit.tensor_sb("gain_rows", [P, 2 * D])
        self.rows = self.part(self.rows_mem, 0, 2, D)
        self.small = kit.tensor_sb("heads_by_token", [P, 8 * P])
        big_at = kit.nc.sbuf_base
        self.big = kit.tensor_sb("big", [P, BIG])
        hid = kit.nc.alloc_sbuf_tensor_at("hidden_split", [P, 2, HID, SEQ], F32R, offset=big_at)
        self.hid = Split(hid[:, 0], hid[:, 1])
        self.col0, at = {}, 0
        for name, n in ROWS:
            self.col0[name] = at
            at += n
        b, r, s = self.big, self.rows_mem, self.small
        self.par_rows = self.part(b, 0, 2, P)
        self.dt_raw, self.dt_abs, self.dt, self.da, self.ncs, self.ecs, self.eend, self.wend = \
            (self.part(s, n * P, NT, SSM_HEADS) for n in range(8))
        self.ytmp = self.part(b, 10752, 2, HPG * 64)
        self.bcF = self.part(b, 0, 2 * SSM_GROUPS, SEQ)
        self.past_r = self.hid.low[:, 8, 0:P]
        self.xring = self.part(b, 8192, 8, SEQ)
        self.decay = self.part(b, 8192, 3, HPG, P)
        self.xdt = self.part(b, 10240, 2, HPG * 64)
        self.xw = self.part(b, 9728, 2, HPG * 64)
        self.xT_tok = self.part(b, BIG - 8192, NT, D_INNER)
        self.y = self.xT_tok
        self.bTok = self.h
        self.state = self.part(r, 0, SSM_GROUPS, HPG * 64)
        self.gate_tmp = self.part(b, 0, 2, WIDE)
        self.sq_tmp = self.part(b, 1024, 256)
        self.relu_tmp, self.sq_tmp2 = self.part(b, 16384, 2, SEQ), self.part(b, 17408, 2, SEQ)
        self.unit = self.part(b, 16384, NT, D)
        self.qF, self.kF = self.part(b, 0, KD, SEQ), self.part(b, 4096, KD, SEQ)
        self.vTok = self.part(b, 8192, NT, D)
        self.sp, self.wt = self.part(b, 12288, 2, 1280), self.part(b, 14848, 2, 1280)
        self.rwF = self.part(b, 0, RW_COLS // P, SEQ)
        self.qkTok = self.part(b, 7168, NT, 2 * ATT)
        self.vT = self.part(b, 11264, NT, ATT)
        self.idxTok = self.part(b, 13312, NT, IDXW)
        self.shift_tmp = self.part(b, 15648, 2, SEQ)
        self.attF = self.part(b, 15648, 8, SEQ)
        self.rope_tmp = self.part(b, 19744, 2, SEQ)
        self.idxF, self.kidxF = self.part(r, 0, 4, SEQ), self.part(s, 0, SEQ)
        self.rope = self.part(s, 512, NT, HD)
        self.relu, self.score, self.work = self.part(b, 7168, 2, SEQ), self.part(b, 8192, 1280), self.part(b, 9472, SEQ)
        self.bias_r = self.hid.low[:, 0:3, :].rearrange("p a b -> p (a b)")
        self.prob, self.probT = self.part(b, 9984, 2, SEQ), self.part(b, 7168, 2, SEQ)
        self.ybTok = self.part(b, 19744, 2, ATT)
        self.ybF = self.part(b, 13312, NHP, SEQ)
        self.kkF, self.aF, self.sg = (self.part(b, 7168 + 2048 * n, NHP, SEQ) for n in range(3))
        self.yaF = self.kkF
        self.sqF = self.part(b, 15360, NHP, SEQ)
        self.tmpF = self.part(b, 17408, 1, SEQ)
        self.eF = self.part(b, 17920, 3, 2, P)
        self.cs, self.prev_cs = self.part(b, 18688, 2, P), self.part(b, 18944, 2, P)
        self.up_w = self.part(r, 0, RW)
        places = [self.part(b, 11264, 2, NHP, P), self.part(b, 12288, 2, NHP, P)] + \
            [self.part(b, 15360 + 1024 * n, 2, NHP, P) for n in range(5)]
        self.kb, self.X, self.Y, self.U, self.level, self.gk, self.br = places
        self.gr = self.part(s, 0, 2, NHP, P)
        self.kapC, self.betC, self.gamC, self.vC = (self.part(r, 512 * n, WIDE) for n in range(4))
        u, lv = places[3], places[4]
        flat = lambda x: x.rearrange("p g q c -> p (g q c)")
        self.D = flat(u)[:, 0:WIDE]
        self.WT = flat(u)[:, WIDE:2 * WIDE].rearrange("p (q c) -> p q c", q=NHP)
        self.SA = flat(lv)[:, 0:WIDE]
        self.S = self.part(b, 6144, NHP, 64)
        self.bonus = self.part(b, 17408, NHP, SEQ)
        self.g_up = self.part(r, 0, RW)
        self.yaR = Split(self.hid.high[:, 0:4], self.hid.high[:, 4:8])
        self.ybR = Split(self.hid.high[:, 8:12], self.hid.high[:, 12:16])
        self.mergedR = Split(self.hid.low[:, 0:8], self.hid.low[:, 8:16])
        self.gate_a, self.gate_b = self.part(b, 16384, 4, SEQ), self.part(b, 18432, 4, SEQ)

    def x_tile(self, k):
        return Split(self.xin.high[:, k, :], self.xin.low[:, k, :])

    def hidden_tile(self, k):
        return Split(self.hid.high[:, k, :], self.hid.low[:, k, :])

    def merged_tile(self, k):
        return Split(self.mergedR.high[:, k, :], self.mergedR.low[:, k, :])

    def y_tile(self, k):
        if k < KD:
            return self.x_tile(k)
        return Split(self.hid.high[:, k - KD, :], self.hid.high[:, k, :])

    def own(self, kit, name, *dims):
        return self.part(kit.tensor_sb(name, [P, int(np.prod(dims))]), 0, *dims)

    def part(self, mem, at, *dims):
        ap = mem[:, at:at + int(np.prod(dims))]
        names = "abcd"[:len(dims)]
        if len(dims) == 1:
            return ap
        return ap.rearrange(f"p ({' '.join(names)}) -> p {' '.join(names)}", **dict(zip(names, dims)))

    def col(self, name, k):
        return self.par_cols[:, 0, self.col0[name] + k:self.col0[name] + k + 1]


PHASE_NAMES = []


def build(nc, a, out, stop=None, dump=None):
    with ExitStack() as ctx:
        kit = Kit(nc, ctx)
        m = Memory(kit)
        m.x_landed = [kit.sem(f"x_landed{t}") for t in range(NT)]
        m.h_landed = kit.sem("residual_landed")
        m.normf = a["normf_g"]
        m.ln_rows = {"mix1": (a["ln_mix_g"][0, :], a["ln_mix_b"][0, :]), "mlp1": (a["ln_mlp_g"][0, :], a["ln_mlp_b"][0, :]),
                     "mix2": (a["ln_mix_g"][1, :], a["ln_mix_b"][1, :]), "mlp2": (a["ln_mlp_g"][1, :], a["ln_mlp_b"][1, :])}

        plan = [
            ("setup", lambda: setup(nc, kit, m, a)),
            ("mamba_in", lambda: mamba_in(nc, kit, m, a)),
            ("mamba_scan", lambda: mamba_scan(nc, kit, m, a)),
            ("mamba_gate", lambda: mamba_gate(nc, kit, m, a)),
            ("mix1", lambda: project_norm(nc, kit, m, a["w_out"], X_TILES, m.y_tile, ALPHA, "mix1", late=True)),
            ("mlp1", lambda: mlp(nc, kit, m, a["mlp_w1"][0], a["mlp_w2"][0], "mlp1")),
            ("sb_project", lambda: sb_project(nc, kit, m, a)),
            ("sb_attend", lambda: sb_attend(nc, kit, m, a)),
            ("mix2", lambda: project_norm(nc, kit, m, a["sb_w_o"], KD, m.x_tile, ALPHA, "mix2")),
            ("mlp2", lambda: mlp(nc, kit, m, a["mlp_w1"][1], a["mlp_w2"][1], "mlp2")),
            ("norm1", lambda: norm_only(nc, kit, m, "norm1", "norm1_g", "norm")),
            ("second_project", lambda: second_project(nc, kit, m, a)),

            ("sparse", lambda: sparse_attend(nc, kit, m, a)),
            ("rwkv_prepare", lambda: rwkv_prepare(nc, kit, m, a)),
            ("rwkv_scan", lambda: rwkv_scan(nc, kit, m, a)),
            ("rwkv_finish", lambda: rwkv_finish(nc, kit, m, a)),
            ("merge", lambda: merge(nc, kit, m, a)),
            ("norm2", lambda: project_norm(nc, kit, m, a["w_out_2"], KD, m.merged_tile, 1.0, "norm2", gain="norm2_g",
                                           mode="rms", eps="norm")),
            ("last", lambda: ffn(nc, kit, m, a, out)),
        ]
        PHASE_NAMES[:] = []
        phases = []
        for name, make in plan:
            kit.phase_tile0 = kit.tiles
            phases.append(make())
            PHASE_NAMES.append(name)
            if name == stop:
                break
        s_dump = kit.sem("dump_written")
        block = ctx.enter_context(nc.Block())

        def run(eng, which):
            for n, phase in enumerate(phases):
                if phase[which] is not None:
                    phase[which](eng)
                eng.drain().then_inc(kit.phase_done, 1)
                eng.wait_ge(kit.phase_done, 4 * (n + 1))

        @block.sync
        def _(sp):
            x = a["x"].rearrange("b (t p) d -> (b p) t d", p=P)
            for t in range(NT):
                sp.dma_start(m.h[:, t, :], x[:, t, :]).then_inc(m.x_landed[t], 16)
            for i, (w, k, nk, c, n) in enumerate(kit.chunks):
                if i >= RING:
                    sp.wait_ge(kit.chunk_split, i - RING + 1)
                src = w[k * P:(k + nk) * P, c:c + n].rearrange("(k p) n -> p k n", p=P)
                sp.dma_start(kit.ring[i % RING][:, 0:nk, 0:n], src).then_inc(kit.chunk_landed[i % RING], 16)
            if dump is not None:
                sp.wait_ge(kit.phase_done, 4 * len(phases))
                for n, (name, ap) in enumerate(dump[1](m)):
                    sp.dma_start(dump[0][n], ap).then_inc(s_dump, 16)
                sp.wait_ge(s_dump, 16 * (n + 1))

        @block.tensor
        def _(pe):
            run(pe, 0)

        @block.vector
        def _(dve):
            run(dve, 1)

        @block.scalar
        def _(act):
            run(act, 2)

        @block.gpsimd
        def _(pool):
            run(pool, 3)


_INS = [("x", "x"), ("w_in", "ssm_w_in"), ("conv_w", "ssm_conv_w"), ("conv_b", "ssm_conv_b"), ("dt_bias", "ssm_dt_bias"),
        ("a_log", "ssm_a_log"), ("ssm_d", "ssm_d"), ("norm_w", "ssm_norm_w"), ("w_out", "ssm_w_out"),
        ("sb_w_k", "sb_w_k"), ("sb_w_v", "sb_w_v"), ("sb_w_q", "sb_w_q"), ("sb_w_o", "sb_w_o"),
        ("mlp_w1", "mlp_w1"), ("mlp_w2", "mlp_w2"), ("ln_mix_g", "ln_mix_g"), ("ln_mix_b", "ln_mix_b"),
        ("ln_mlp_g", "ln_mlp_g"), ("ln_mlp_b", "ln_mlp_b"), ("norm1_g", "norm1_g_2"), ("w_in_2", "w_in_2"),
        ("mu", "tshift_mu_2"), ("w_decay_up", "w_decay_up_2"), ("w0", "w0_2"), ("a_up", "a_up_2"), ("a0", "a0_2"),
        ("g_up", "g_up_2"), ("k_k", "k_k_2"), ("k_a", "k_a_2"), ("r_k", "r_k_2"), ("lnx_g", "lnx_g_2"),
        ("lnx_b", "lnx_b_2"), ("w_o_rwkv", "w_o_rwkv_2"), ("w_o_att", "w_o_att_2"), ("w_out_2", "w_out_2"),
        ("norm2_g", "norm2_g_2"), ("w_ffn_in", "w_ffn_in_2"), ("w_ffn_out", "w_ffn_out_2"), ("normf_g", "normf_g_2")]
_ONE_LAYER = ["w_in", "conv_w", "conv_b", "dt_bias", "a_log", "ssm_d", "norm_w", "w_out", "sb_w_q", "sb_w_o"]


def kernel(**inputs):
    import numpy as _np
    import concourse.bacc as _bacc
    from concourse import mybir as _mybir
    from concourse.bass_utils import run_bass_kernel_spmd as _run

    nc = _bacc.Bacc("TRN2", target_bir_lowering=False, num_devices=1)
    arrays, a = {}, {}
    for name, source in _INS:
        v = _np.ascontiguousarray(inputs[source])
        if name in _ONE_LAYER:
            v = v[0]
        if name == "r_k":
            v = v.reshape(-1)
        arrays[f"in_{name}"] = v
        a[name] = nc.dram_tensor(f"in_{name}", v.shape, _mybir.dt.from_np(v.dtype), kind="ExternalInput").ap()
    table = host_rope()
    arrays["in_rope"] = table
    a["rope"] = nc.dram_tensor("in_rope", table.shape, _mybir.dt.from_np(table.dtype), kind="ExternalInput").ap()
    out = nc.dram_tensor("out_dram", (1, SEQ, D), F32, kind="ExternalOutput").ap()
    build(nc, a, out.rearrange("b s d -> (b s) d"))
    r = _run(nc, [arrays], core_ids=[0])
    return r.results[0]["out_dram"]
```

```python
import math
from contextlib import ExitStack

import numpy as np

import concourse.bass as bass
from concourse import mybir

F32 = mybir.dt.float32
F32R = mybir.dt.float32r
ALU = mybir.AluOpType
ACT = mybir.ActivationFunctionType
AX_X = mybir.AxisListType.X

P = 128
SEQ = 512
NT = SEQ // P
D = 1024
KD = D // P
WIDE = 512
RING = 3
SPLIT = 2
KC = 4
BANKS = 8
LN_EPS = 1e-5
RMS_EPS = 1e-5
NORM_EPS = 1e-6
LNX_EPS = 64e-5
ALPHA = (2 * 2) ** 0.25

D_INNER = 2 * D
SSM_HEADS = D_INNER // 64
SSM_GROUPS = 8
HPG = SSM_HEADS // SSM_GROUPS
XBC = D_INNER + 2 * SSM_GROUPS * P
XBC_TILES = XBC // P
X_TILES = D_INNER // P
D_CONV = 4
SB_HEADS = 16
HD = 64
D_FF = 4 * D
RW = 512
RW_COLS = 3 * RW + 64 + 64 + 128
ATT = 512
IDXW = 512 + 64 + 8
D_FF2 = 2816
TOPK = 128
NHEAD = 8
NHP = NHEAD // 2
DECAY_UNIT = math.exp(-0.5)
REMOVED = -3.0e38
FUTURE = -1.0e38
FAR = -1.0e30

ROWS = [("mu", RW_COLS // P), ("w0", 4), ("a0", 4), ("k_k", 4), ("k_a", 4), ("r_k", 4), ("lnx_g", 4), ("lnx_b", 4),
        ("conv_b", XBC_TILES), ("norm_w", X_TILES), ("norm1_g", KD), ("norm2_g", KD)]


def host_rope():
    half = HD // 2
    inv = (np.float32(1.0) / (np.float32(10000.0) ** (np.arange(half, dtype=np.float32) * np.float32(2.0) / np.float32(HD)))).astype(np.float32)
    ang = (np.arange(SEQ, dtype=np.float32)[:, None] * inv[None, :]).astype(np.float32)
    return np.concatenate([np.cos(ang), np.sin(ang)], axis=1).astype(np.float32)


class Split:

    def __init__(self, high, low):
        self.high, self.low = high, low


class Gemm:

    def __init__(self, kit, w, k_tiles, c0, cols, feature, k_from=0, banks=BANKS):
        self.kit, self.feature, self.banks = kit, feature, banks
        self.chunk0, self.tile0, self.phase0 = len(kit.chunks), kit.tiles, kit.phase_tile0
        self.parts = []
        for c in range(c0, c0 + cols, WIDE):
            n = min(WIDE, c0 + cols - c)
            blocks = [(k, min(KC, k_tiles - k)) for k in range(0, k_tiles, KC)]
            kit.tiles += n // P if feature else NT
            for k, nk in blocks:
                kit.chunks.append((w, k_from + k, nk, c, n))
                if k + nk == k_tiles:
                    kit.chunk_over.append((kit.tile_ready, kit.tiles))
                else:
                    kit.parts_used += 1
                    kit.chunk_over.append((kit.part_used, kit.parts_used))
            self.parts.append((n, blocks))
        self.count = kit.tiles - self.tile0
        self.last_chunk = len(kit.chunks)

    def bank(self, n):
        return (self.tile0 - self.phase0 + n) % self.banks

    def tensor(self, pe, x, before=None, after=None):
        kit = self.kit
        i, tile = self.chunk0, self.tile0
        for j, (n, blocks) in enumerate(self.parts):
            tiles = n // P if self.feature else NT
            for b, (k0, nk) in enumerate(blocks):
                if before is not None and j == 0:
                    before(k0 + nk)
                pe.wait_ge(kit.chunk_split, i + 1)
                w = kit.split_ring[i % SPLIT]
                for m in range(tiles):
                    t = tile + m
                    if b == 0 and t - self.phase0 >= self.banks:
                        pe.wait_ge(kit.tile_free, t - self.banks + 1)
                    out = kit.psum[:, (t - self.phase0) % self.banks, 0:WIDE if self.feature else n]
                    for k in range(nk):
                        xk = x(k0 + k)
                        pairs = ((w.high, xk.high), (w.low, xk.high), (w.high, xk.low))
                        for q, (wp, xp) in enumerate(pairs):
                            first = b == 0 and k == 0 and q == 0
                            last = b == len(blocks) - 1 and k == nk - 1 and q == 2
                            if self.feature:
                                mm = pe.matmul(out, wp[:, k, m * P:(m + 1) * P], xp, start=first, stop=last)
                            else:
                                mm = pe.matmul(out, xp[:, m * P:(m + 1) * P], wp[:, k, 0:n], start=first, stop=last)
                    if b == len(blocks) - 1:
                        mm.then_inc(kit.tile_ready, 1)
                    elif m == tiles - 1:
                        mm.then_inc(kit.part_used, 1)
                i += 1
            tile += tiles
            if after is not None:
                after(j)

    def take_over(self, eng):
        if self.tile0:
            eng.wait_ge(self.kit.tile_free, self.tile0)

    def wait_tile(self, eng, n):
        eng.wait_ge(self.kit.tile_ready, self.tile0 + n + 1)
        return self.kit.psum[:, self.bank(n), :]

    def wait_free(self, eng, n):
        eng.wait_ge(self.kit.tile_free, self.tile0 + n + 1)


class Chain:

    def __init__(self, eng, sem):
        self.eng, self.sem, self.n = eng, sem, 0

    def __call__(self, ins):
        self.n += 1
        ins.then_inc(self.sem, 1)
        self.eng.wait_ge(self.sem, self.n)

    def mark(self, ins):
        self.n += 1
        ins.then_inc(self.sem, 1)
        return self.n

    def wait(self):
        self.eng.wait_ge(self.sem, self.n)


class Kit:

    def __init__(self, nc, ctx):
        self.nc, self.ctx = nc, ctx
        self.chunks, self.chunk_over, self.tiles, self.parts_used = [], [], 0, 0
        self.psum = self.tensor_psum("psum", [P, BANKS, WIDE])
        self.ring_mem = self.tensor_sb("weight_ring", [P, RING, KC, WIDE])
        self.ring = [self.ring_mem[:, r] for r in range(RING)]
        self.split_at = nc.sbuf_base
        self.split_mem = self.tensor_sb("weight_split_ring", [P, SPLIT, 2, KC, WIDE], F32R)
        self.split_ring = [Split(self.split_mem[:, r, 0], self.split_mem[:, r, 1]) for r in range(SPLIT)]
        self.high_made, self.chunk_split, self.split_done = self.sem("chunk_high_made"), self.sem("chunk_split"), 0
        self.phase_tile0 = 0
        self.chunk_landed = [self.sem(f"chunk_landed{r}") for r in range(RING)]
        self.part_used = self.sem("part_used")
        self.tile_ready = self.sem("tile_ready")
        self.tile_free = self.sem("tile_free")
        self.phase_done = self.sem("phase_done")
        self.vector_step, self.chain = self.sem("vector_step"), None
        self.norm_sems = [self.sem(f"norm_{n}") for n in ("variance_ready", "deviation_ready", "normed", "transposed",
                                                          "high_ready", "transpose_read", "rows_landed")]
        self.norms, self.norm_rows = 0, 0
        self.mlp_sems = [self.sem(f"mlp_{n}") for n in ("high_ready", "split_ready")]
        self.mlp_tiles = 0

    def tensor_sb(self, name, shape, dtype=F32):
        return self.ctx.enter_context(self.nc.sbuf_tensor(name, shape, dtype))

    def split_chunks(self, pool, upto):
        for i in range(self.split_done, min(upto, len(self.chunks))):
            _, _, nk, _, n = self.chunks[i]
            raw, part = self.ring[i % RING][:, 0:nk, 0:n], self.split_ring[i % SPLIT]
            pool.wait_ge(self.chunk_landed[i % RING], 16 * (i // RING + 1))
            if i >= SPLIT:
                pool.wait_ge(*self.chunk_over[i - SPLIT])
            pool.tensor_scalar(part.high[:, 0:nk, 0:n], raw, 1.0, 0.0, ALU.mult, ALU.add).then_inc(self.high_made, 1)
            pool.wait_ge(self.high_made, i + 1)
            pool.tensor_tensor(part.low[:, 0:nk, 0:n], raw, part.high[:, 0:nk, 0:n].bitcast(F32), ALU.subtract)\
                .then_inc(self.chunk_split, 1)
        self.split_done = max(self.split_done, min(upto, len(self.chunks)))

    def tensor_psum(self, name, shape):
        return self.ctx.enter_context(self.nc.psum_tensor(name, shape, F32))

    def vector_chain(self, dve):
        if self.chain is None:
            self.chain = Chain(dve, self.vector_step)
        return self.chain

    def sem(self, name):
        return self.ctx.enter_context(self.nc.semaphore(name))


def over(ap, n):
    return ap.unsqueeze(len(ap.shape)).broadcast_to(list(ap.shape) + [n])


def across(ap, n):
    return ap.unsqueeze(1).broadcast_to([ap.shape[0], n, ap.shape[1]])


def norm_rows(nc, kit, m, alpha, gain, mode, eps, tag, gemms=(), src=None, first=None, final=None):
    s_var, s_std, s_norm, s_tr, s_high, s_tf, s_rows = kit.norm_sems
    s_out = kit.sem("out_written") if final is not None else None
    tok0, turn0 = kit.norms * NT, kit.norms * 2 * NT
    kit.norms += 1
    if mode != "rms":
        kit.norm_rows += 32 if mode == "ln" else 16
    rows_in = kit.norm_rows
    unit = m.h if mode != "rms" else m.unit
    last = final is not None

    def tensor(pe):
        if last:
            return
        for t in range(NT):
            pe.wait_ge(s_norm, tok0 + t + 1)
            if gemms and t == 0:
                gemms[-1].wait_free(pe, gemms[-1].count - 1)
            for j in range(2):
                n = 2 * t + j
                if n >= 4:
                    pe.wait_ge(s_tf, turn0 + n - 3)
                for q in range(4):
                    mm = pe.transpose(kit.psum[:, n % 4, q * P:(q + 1) * P],
                                      unit[:, t, (4 * j + q) * P:(4 * j + q + 1) * P], m.ident[:, :])
                mm.then_inc(s_tr, 1)

    def add_tiles(dve, gemm, scale, stats):
        step = kit.vector_chain(dve)
        for n in range(2):
            for t in range(NT):
                ps = gemm.wait_tile(dve, 4 * n + t)
                hs = m.h[:, t, n * WIDE:(n + 1) * WIDE]
                dve.scalar_tensor_tensor(out=hs, in0=hs, scalar=scale, in1=ps, op0=ALU.mult, op1=ALU.add)\
                   .then_inc(kit.tile_free, 1)
                gemm.wait_free(dve, 4 * n + t)
                if stats:
                    step.mark(dve.bn_stats(m.stats[:, t, n, :], hs))

    def low_parts(dve, t):
        for j in range(2):
            n = 2 * t + j
            dve.wait_ge(s_high, turn0 + n + 1)
            blk = slice(t * P, (t + 1) * P)
            ps = kit.psum[:, n % 4, :].rearrange("p (q c) -> p q c", q=4)
            high, low = (x[:, 4 * j:4 * j + 4, blk] for x in (m.xin.high, m.xin.low))
            if mode == "ln":
                dve.tensor_tensor(low, ps, high.bitcast(F32), ALU.subtract).then_inc(s_tf, 1)
            else:
                for q in range(4):
                    ins = dve.scalar_tensor_tensor(out=low[:, q], in0=ps[:, q], scalar=m.col(gain, 4 * j + q),
                                                   in1=high[:, q].bitcast(F32), op0=ALU.mult, op1=ALU.subtract)
                ins.then_inc(s_tf, 1)

    def vector(dve):
        step = kit.vector_chain(dve)
        if not gemms:
            for t in range(NT):
                for n in range(2):
                    step.mark(dve.bn_stats(m.stats[:, t, n, :], m.h[:, t, n * WIDE:(n + 1) * WIDE]))
        step.wait()
        for t in range(NT):
            step.mark(dve.bn_aggr(m.mv[:, t, :], m.stats[:, t].rearrange("p a b -> p (a b)")))
        step.wait()
        if mode != "ln":
            step(dve.tensor_tensor(m.ms[:, :], m.mv[:, :, 0], m.mv[:, :, 0], ALU.mult))
            step(dve.tensor_tensor(m.mv[:, :, 1], m.mv[:, :, 1], m.ms[:, :], ALU.add))
        dve.tensor_scalar(m.ms[:, :], m.mv[:, :, 1], m.eps[eps], None, ALU.add).then_inc(s_var, 1)
        dve.wait_ge(s_std, tok0 // NT + 1)
        r, w = m.rstd[:, :], m.std[:, :]
        step(dve.reciprocal(r, w))
        step(dve.tensor_tensor(w, r, r, ALU.mult))
        step(dve.tensor_tensor(w, w, m.ms[:, :], ALU.mult))
        step(dve.tensor_scalar(w, w, -0.5, 1.5, ALU.mult, ALU.add))
        step(dve.tensor_tensor(r, r, w, ALU.mult))
        for t in range(NT + 1):
            if t < NT:
                ht, rt = m.h[:, t, :], m.rstd[:, t:t + 1]
                if t == 0 and mode != "rms":
                    dve.wait_ge(s_rows, rows_in)
                if mode == "ln":
                    step(dve.scalar_tensor_tensor(out=ht, in0=ht, scalar=m.mv[:, t, 0:1], in1=m.rows[:, 0, :],
                                                  op0=ALU.subtract, op1=ALU.mult))
                    dve.scalar_tensor_tensor(out=ht, in0=ht, scalar=rt, in1=m.rows[:, 1, :],
                                             op0=ALU.mult, op1=ALU.add).then_inc(s_norm, 1)
                elif not last:
                    dve.tensor_scalar(m.unit[:, t, :], ht, rt, None, ALU.mult).then_inc(s_norm, 1)
                else:
                    dve.scalar_tensor_tensor(out=ht, in0=ht, scalar=rt, in1=m.rows[:, 0, :],
                                             op0=ALU.mult, op1=ALU.mult).then_inc(s_norm, 1)
            if t >= 1 and not last:
                low_parts(dve, t - 1)

    def scalar(act):
        act.wait_ge(s_var, tok0 // NT + 1)
        act.activation(m.std[:, :], m.ms[:, :], ACT.Sqrt).then_inc(s_std, 1)
        if last:
            return
        for n in range(2 * NT):
            t, j = n // 2, n % 2
            act.wait_ge(s_tr, turn0 + n + 1)
            dst = m.xin.high[:, 4 * j:4 * j + 4, t * P:(t + 1) * P]
            ps = kit.psum[:, n % 4, :].rearrange("p (q c) -> p q c", q=4)
            if mode == "ln":
                ins = act.activation(dst, ps, ACT.Copy)
            else:
                for q in range(4):
                    ins = act.activation(dst[:, q], ps[:, q], ACT.Copy, scale=m.col(gain, 4 * j + q))
            ins.then_inc(s_high, 1)

    def rows(pool):
        if mode == "ln":
            g, b = m.ln_rows[tag]
            pool.dma_start(m.rows[:, 0, :], g.partition_broadcast(P)).then_inc(s_rows, 16)
            pool.dma_start(m.rows[:, 1, :], b.partition_broadcast(P)).then_inc(s_rows, 16)
        elif last:
            pool.dma_start(m.rows[:, 0, :], m.normf.partition_broadcast(P)).then_inc(s_rows, 16)

    def gpsimd(pool):
        if last:
            out = final.rearrange("(t p) d -> p t d", p=P)
            for t in range(NT):
                pool.wait_ge(s_norm, tok0 + t + 1)
                pool.dma_start(out[:, t, :], m.h[:, t, :]).then_inc(s_out, 16)
            pool.wait_ge(s_out, 16 * NT)

    return tensor, vector, scalar, gpsimd, rows, add_tiles


def project_norm(nc, kit, m, w, k_tiles, x, alpha, tag, gain=None, mode="ln", eps="ln", late=False):
    g = Gemm(kit, w, k_tiles, 0, D, False)
    t, v, a, p, rows, add = norm_rows(nc, kit, m, alpha, gain, mode, eps, tag, gemms=(g,))

    def tensor(pe):
        g.tensor(pe, x)
        t(pe)

    def vector(dve):
        if late:
            dve.wait_ge(m.h_landed, 16)
        add(dve, g, alpha, True)
        v(dve)

    def gpsimd(pool):
        rows(pool)
        kit.split_chunks(pool, g.last_chunk + SPLIT)

    return tensor, vector, a, gpsimd


def norm_only(nc, kit, m, tag, gain, eps):
    t, v, a, p, rows, add = norm_rows(nc, kit, m, 1.0, gain, "rms", eps, tag)
    s_mask = kit.sem("pair_mask_cut")

    def gpsimd(pool):
        cut = Chain(pool, s_mask)
        cut(pool.memset(m.pair_mask[:, :, :], 0.0))
        for n in range(8):
            b = 1 if n == 0 else 2 ** (n - 1)
            half = 1 if n == 0 else 0
            part = m.pair_mask[:, n, :].rearrange("p (q h r) -> p q h r", h=2, r=b)[:, :, half, :]
            lo = 0 if n == 0 else b
            cut(pool.memset(part, 1.0))
            cut(pool.affine_select(out=part, in_=part, compare_op=ALU.is_ge, fill=0.0, base=-lo,
                                   pattern=[[-2 * b, P // (2 * b)], [0, b]], channel_multiplier=1))
            cut(pool.affine_select(out=part, in_=part, compare_op=ALU.is_ge, fill=0.0, base=lo + b - 1,
                                   pattern=[[2 * b, P // (2 * b)], [0, b]], channel_multiplier=-1))

    return t, v, a, gpsimd


def mlp(nc, kit, m, w1, w2, tag):
    HALF = D_FF // P // 2
    up = [None, None]
    down = [None, None]
    for q in range(2):
        up[q] = Gemm(kit, w1, KD, q * HALF * P, HALF * P, True)
        down[q] = Gemm(kit, w2, HALF, 0, D, False, k_from=q * HALF)
    t, v, a, p, rows, add = norm_rows(nc, kit, m, ALPHA, None, "ln", "ln", tag, gemms=(down[1],))
    s_high, s_hid = kit.mlp_sems
    n0 = kit.mlp_tiles
    kit.mlp_tiles += 2 * HALF

    def tensor(pe):
        for q in range(2):
            up[q].tensor(pe, m.x_tile)
            down[q].tensor(pe, m.hidden_tile, before=lambda k, q=q: pe.wait_ge(s_hid, n0 + q * HALF + k))
        t(pe)

    def scalar(act):
        for n in range(2 * HALF):
            if n % HALF == 0:
                up[n // HALF].take_over(act)
            ps = up[n // HALF].wait_tile(act, n % HALF)
            if n >= 2:
                act.wait_ge(s_hid, n0 + n - 1)
            act.activation(m.relu_tmp[:, n % 2, :], ps, ACT.Relu).then_inc(kit.tile_free, 1)
            up[n // HALF].wait_free(act, n % HALF)
            if n == HALF:
                act.wait_ge(kit.tile_ready, down[0].tile0 + down[0].count)
            act.activation(m.hid.high[:, n % HALF, :], m.relu_tmp[:, n % 2, :], ACT.Square).then_inc(s_high, 1)
        a(act)

    def vector(dve):
        step = kit.vector_chain(dve)
        for q in range(2):
            for n in range(q * HALF, (q + 1) * HALF):
                up[q].wait_free(dve, n % HALF)
                sq = m.sq_tmp2[:, n % 2, :]
                r = m.relu_tmp[:, n % 2, :]
                step(dve.tensor_tensor(sq, r, r, ALU.mult))
                dve.wait_ge(s_high, n0 + n + 1)
                dve.tensor_tensor(m.hid.low[:, n % HALF, :], sq, m.hid.high[:, n % HALF, :].bitcast(F32), ALU.subtract)\
                   .then_inc(s_hid, 1)
            add(dve, down[q], ALPHA if q == 0 else 1.0, q == 1)
        v(dve)

    def gpsimd(pool):
        rows(pool)
        kit.split_chunks(pool, down[1].last_chunk + SPLIT)

    return tensor, vector, scalar, gpsimd


def load_parameters(m, a, sp):
    at = 0
    for name, n in ROWS:
        sp.dma_start(m.par_rows[at:at + n, 0, :], a[name].rearrange("(r c) -> r c", c=P)).then_inc(m.parameter_rows_landed, 16)
        at += n
    sp.dma_start(m.par_rows[:, 1, :], a["conv_w"].rearrange("j (r c) -> (j r) c", c=P)).then_inc(m.parameter_rows_landed, 16)
    for n, ap in enumerate((a["dt_bias"], a["a_log"], a["ssm_d"])):
        sp.dma_start(m.head_rows[:, n, :], ap.partition_broadcast(P)).then_inc(m.parameter_rows_landed, 16)


def setup(nc, kit, m, a):
    s_base = kit.sem("constant_filled")
    s_sel = kit.sem("constant_cut")
    s_par = m.parameter_rows_landed
    s_tr = kit.sem("setup_transposed")
    s_tf = kit.sem("setup_transpose_read")
    s_high = kit.sem("setup_high_ready")

    def gpsimd(pool):
        base = Chain(pool, s_base)
        fills = [(m.ident, 0.0), (m.ones, 1.0), (m.upper, 1.0), (m.upper_strict, 1.0), 
                 (m.halves, 0.0), (m.eps_mem[:, 0:1], LN_EPS),
                 (m.eps_mem[:, 1:2], NORM_EPS), (m.eps_mem[:, 2:3], LNX_EPS), (m.eps_mem[:, 3:4], RMS_EPS),
                 (m.eps_mem[:, 4:5], 1.0), (m.neg_ones, -1.0), (m.neg_lower, -1.0)]
        for ap, v in fills:
            base.mark(pool.memset(ap, v))
        base.wait()
        cut = Chain(pool, s_sel)
        cut.mark(pool.affine_select(out=m.ident[:, :], in_=m.ident[:, :], compare_op=ALU.not_equal, fill=1.0, base=0,
                                    pattern=[[-1, P]], channel_multiplier=1))
        cut.wait()
        kit.split_chunks(pool, 1)

    def scalar(act):
        for n in range(2 * NT):
            act.wait_ge(s_tr, n + 1)
            t, j = n // 2, n % 2
            act.activation(m.xin.high[:, 4 * j:4 * j + 4, t * P:(t + 1) * P],
                           kit.psum[:, n % 4, :].rearrange("p (q c) -> p q c", q=4), ACT.Copy).then_inc(s_high, 1)
        act.wait_ge(s_tr, 2 * NT + 1)
        nrow = sum(n for _, n in ROWS)
        act.activation(m.par_cols[:, 0, 0:nrow], kit.psum[:, 4, 0:nrow], ACT.Copy)
        act.activation(m.par_cols[:, 1, :], kit.psum[:, 4, P:2 * P], ACT.Copy)

    def tensor(pe):
        pe.wait_ge(s_sel, 1)
        for n in range(2 * NT):
            t, j = n // 2, n % 2
            if j == 0:
                pe.wait_ge(m.x_landed[t], 16)
            if n >= 4:
                pe.wait_ge(s_tf, n - 3)
            for q in range(4):
                mm = pe.transpose(kit.psum[:, n % 4, q * P:(q + 1) * P], m.h[:, t, (4 * j + q) * P:(4 * j + q + 1) * P],
                                  m.ident[:, :])
            mm.then_inc(s_tr, 1)
        pe.wait_ge(s_par, 16 * (len(ROWS) + 4))
        nrow = sum(n for _, n in ROWS)
        pe.transpose(kit.psum[:, 4, 0:nrow], m.par_rows[0:nrow, 0, :], m.ident[0:nrow, 0:nrow])
        pe.transpose(kit.psum[:, 4, P:2 * P], m.par_rows[:, 1, :], m.ident[:, :]).then_inc(s_tr, 1)

    def vector(dve):
        for n in range(2 * NT):
            dve.wait_ge(s_high, n + 1)
            t, j = n // 2, n % 2
            high, low = (x[:, 4 * j:4 * j + 4, t * P:(t + 1) * P] for x in (m.xin.high, m.xin.low))
            dve.tensor_tensor(low, kit.psum[:, n % 4, :].rearrange("p (q c) -> p q c", q=4), high.bitcast(F32),
                              ALU.subtract).then_inc(s_tf, 1)

    return tensor, vector, scalar, gpsimd


CONSTANT_STEPS = 7


def more_constants(kit, m, pool):
    cut = Chain(pool, m.constants_cut)
    for t, sign, b in ((m.upper, 1, 0), (m.upper_strict, 1, -1), (m.neg_lower, -1, 0)):
        cut.mark(pool.affine_select(out=t[:, :], in_=t[:, :], compare_op=ALU.is_ge, fill=0.0, base=b,
                                    pattern=[[sign, P]], channel_multiplier=-sign))
    cut(pool.tensor_scalar(m.ident_r, m.ident, 1.0, 0.0, ALU.mult, ALU.add))
    cut(pool.tensor_scalar(m.past_r, m.upper, -FAR, FAR, ALU.mult, ALU.add))
    cut(pool.memset(m.halves[0:64, 0:64], 1.0))
    cut(pool.memset(m.halves[64:P, 64:P], 1.0))
    assert cut.n == CONSTANT_STEPS


def mamba_in(nc, kit, m, a):
    BK = 6
    g = Gemm(kit, a["w_in"], KD, D_INNER, XBC, True, banks=BK)
    gd = Gemm(kit, a["w_in"], KD, D_INNER + XBC, SSM_HEADS, False, banks=BK)
    TURNED = X_TILES + SSM_GROUPS
    s_silu = kit.sem("conv_silu_ready")
    s_tr = kit.sem("xb_transposed")
    s_tf = kit.sem("xb_transpose_read")
    s_abs = kit.sem("dt_abs_ready")
    s_exp = kit.sem("dt_exp_step")
    s_da = kit.sem("da_ready")
    s_cs = kit.sem("decay_sums_ready")
    s_cr = kit.sem("decay_sums_read_by_scalar")
    s_sum = kit.sem("decay_to_end_ready")
    s_we = kit.sem("weight_to_end_ready")

    def tile(n):
        return m.xring[:, n % 8, :] if n < X_TILES else m.bcF[:, n - X_TILES, :]

    def tensor(pe):
        def turn(j):
            for n in range(4 * j, 4 * j + 4):
                if n >= TURNED:
                    return
                pe.wait_ge(s_silu, n + 1)
                if n >= 2:
                    pe.wait_ge(s_tf, n - 1)
                for c in range(NT):
                    mm = pe.transpose(kit.psum[:, BK + n % 2, c * P:(c + 1) * P], tile(n)[:, c * P:(c + 1) * P],
                                      m.ident[:, :])
                mm.then_inc(s_tr, 1)

        g.tensor(pe, m.x_tile, after=lambda j: turn(j - 1) if j >= 1 else None)
        gd.tensor(pe, m.x_tile)
        pe.wait_ge(s_da, 1)
        pe.wait_ge(s_tf, TURNED)
        pe.wait_ge(m.constants_cut, CONSTANT_STEPS)
        for c in range(NT):
            pe.matmul(kit.psum[:, 6, c * 32:c * 32 + 32], m.upper[:, :], m.da[:, c, :], start=True, stop=True)
            mm = pe.matmul(kit.psum[:, 7, c * 32:c * 32 + 32], m.ones[:, :], m.da[:, c, :], start=True, stop=True)
        mm.then_inc(s_cs, 1)

    def vector(dve):
        step = kit.vector_chain(dve)
        for n in range(XBC_TILES):
            ps = g.wait_tile(dve, n)
            if 8 <= n < X_TILES:
                dve.wait_ge(s_tr, n - 7)
            acc = tile(n)
            w = [m.par_cols[:, 1, j * XBC_TILES + n:j * XBC_TILES + n + 1] for j in range(D_CONV)]
            step(dve.tensor_scalar(acc, ps, w[3], m.col("conv_b", n), ALU.mult, ALU.add))
            for d in (1, 2):
                step(dve.scalar_tensor_tensor(out=acc[:, d:], in0=ps[:, :SEQ - d], scalar=w[3 - d], in1=acc[:, d:],
                                              op0=ALU.mult, op1=ALU.add))
            dve.scalar_tensor_tensor(out=acc[:, 3:], in0=ps[:, :SEQ - 3], scalar=w[0], in1=acc[:, 3:],
                                     op0=ALU.mult, op1=ALU.add).then_inc(kit.tile_free, 1)
        for t in range(NT):
            ps = gd.wait_tile(dve, t)
            dve.tensor_tensor(m.dt_raw[:, t, :], ps[:, 0:SSM_HEADS], m.head_rows[:, 0, :], ALU.add)\
               .then_inc(kit.tile_free, 1)
        gd.wait_free(dve, NT - 1)
        dve.scalar_tensor_tensor(out=m.dt_abs[:, :, :], in0=m.dt_raw[:, :, :], scalar=-1.0, in1=m.dt_raw[:, :, :],
                                 op0=ALU.mult, op1=ALU.max).then_inc(s_abs, 1)
        dve.wait_ge(s_exp, 3)
        step(dve.scalar_tensor_tensor(out=m.dt[:, :, :], in0=m.dt_raw[:, :, :], scalar=0.0, in1=m.dt_abs[:, :, :],
                                      op0=ALU.max, op1=ALU.add))
        dve.scalar_tensor_tensor(out=m.da[:, :, :], in0=m.dt[:, :, :], scalar=-1.0,
                                 in1=across(m.head_rows[:, 1, :], NT), op0=ALU.mult, op1=ALU.mult).then_inc(s_da, 1)
        dve.wait_ge(s_cr, 1)
        w = m.wend[:, :, :].rearrange("p a b -> p (a b)")
        step(dve.tensor_copy(w, kit.psum[:, 7, 0:P]))
        dve.tensor_tensor(w, w, kit.psum[:, 6, 0:P], ALU.subtract).then_inc(s_sum, 1)
        dve.wait_ge(s_we, 1)
        dve.tensor_tensor(m.wend[:, :, :], m.wend[:, :, :], m.dt[:, :, :], ALU.mult)

    def scalar(act):
        def turned(n):
            act.wait_ge(s_tr, n + 1)
            f = n if n < X_TILES else n - X_TILES
            dst = (m.xT_tok if n < X_TILES else m.bTok)[:, :, f * P:(f + 1) * P]
            act.activation(dst, kit.psum[:, BK + n % 2, :].rearrange("p (c d) -> p c d", c=NT), ACT.Copy).then_inc(s_tf, 1)

        for n in range(XBC_TILES):
            g.wait_free(act, n)
            act.activation(tile(n), tile(n), ACT.Silu).then_inc(s_silu, 1)
            if 4 <= n < TURNED + 4:
                turned(n - 4)
        act.activation(m.head_rows[:, 1, :], m.head_rows[:, 1, :], ACT.Exp).then_inc(s_exp, 1)
        act.wait_ge(s_abs, 1)
        act.activation(m.dt_abs[:, :, :], m.dt_abs[:, :, :], ACT.Exp, scale=-1.0).then_inc(s_exp, 1)
        act.wait_ge(s_exp, 2)
        act.activation(m.dt_abs[:, :, :], m.dt_abs[:, :, :], ACT.Ln, bias=m.one).then_inc(s_exp, 1)
        act.wait_ge(s_cs, 1)
        cs, end = kit.psum[:, 6, 0:P], kit.psum[:, 7, 0:P]
        act.activation(m.ncs[:, :, :].rearrange("p a b -> p (a b)"), cs, ACT.Copy, scale=-1.0)
        act.activation(m.ecs[:, :, :].rearrange("p a b -> p (a b)"), cs, ACT.Exp)
        act.activation(m.eend[:, :, :].rearrange("p a b -> p (a b)"), end, ACT.Exp).then_inc(s_cr, 1)
        act.wait_ge(s_sum, 1)
        act.activation(m.wend[:, :, :], m.wend[:, :, :], ACT.Exp).then_inc(s_we, 1)

    def gpsimd(pool):
        kit.split_chunks(pool, 3)
        more_constants(kit, m, pool)
        kit.split_chunks(pool, gd.last_chunk + SPLIT)

    return tensor, vector, scalar, gpsimd


def mamba_scan(nc, kit, m, a):
    s_cb = kit.sem("cb_and_sums_ready")
    s_e = kit.sem("decay_matrix_ready")
    s_mix = kit.sem("mix_matrix_ready")
    s_xw = kit.sem("weighted_x_ready")
    s_y = kit.sem("chunk_products_ready")
    s_fold = kit.sem("chunk_products_read")
    s_skip = kit.sem("skip_term_ready")
    STEPS = NT * SSM_GROUPS
    GW = HPG * 64

    def split(i):
        return i // SSM_GROUPS, i % SSM_GROUPS

    def by_head(ap):
        return ap.rearrange("p (h d) -> p h d", d=64)

    def tensor(pe):
        def first(i):
            c, g = split(i)
            blk = slice(c * P, (c + 1) * P)
            if i >= 2:
                pe.wait_ge(s_mix, i - 1)
            pe.matmul(kit.psum[:, i % 2, 0:P], m.bcF[:, g, blk], m.bcF[:, SSM_GROUPS + g, blk],
                      start=True, stop=True)
            bank = kit.psum[:, 2 + i % 2, :]
            pe.matmul(bank.rearrange("p (h l) -> p h l", h=HPG), m.ident_r[:, :], across(m.past_r[:, :], HPG),
                      start=True, stop=True, skip_group_check=True)
            for r in range(HPG):
                h = g * HPG + r
                mm = pe.matmul(bank[:, r * P:(r + 1) * P], m.da[:, c, h:h + 1].broadcast_to([P, P]),
                               m.upper[:, :], start=False, stop=True, skip_group_check=True)
            mm.then_inc(s_cb, 1)

        def second(i):
            c, g = split(i)
            blk = slice(c * P, (c + 1) * P)
            if i >= 2:
                pe.wait_ge(s_fold, i - 1)
            yb = kit.psum[:, 4 + i % 2, :]
            pe.wait_ge(s_xw, i + 1)
            pe.wait_ge(s_mix, i + 1)
            for r in range(HPG):
                mm = pe.matmul(yb[:, r * 64:(r + 1) * 64], m.decay[:, i % 3, r, :], m.xdt[:, i % 2, r * 64:(r + 1) * 64],
                               start=True, stop=True)
            if c > 0:
                pe.wait_ge(s_fold, i - SSM_GROUPS + 1)
                mm = pe.matmul(yb[:, GW:2 * GW], m.bcF[:, SSM_GROUPS + g, blk], m.state[:, g, :],
                               start=True, stop=True)
            if c < NT - 1:
                mm = pe.matmul(kit.psum[:, 6 + i % 2, 0:GW], m.bTok[:, c, g * P:(g + 1) * P], m.xw[:, i % 2, :],
                               start=True, stop=True)
            mm.then_inc(s_y, 1)

        for i in range(STEPS + 2):
            if i < STEPS:
                first(i)
            if i >= 2:
                second(i - 2)

    def scalar(act):
        for i in range(STEPS):
            c, g = split(i)
            act.wait_ge(s_cb, i + 1)
            if i >= 3:
                act.wait_ge(s_y, i - 2)
            for r in range(HPG):
                h = g * HPG + r
                ins = act.activation(m.decay[:, i % 3, r, :], kit.psum[:, 2 + i % 2, r * P:(r + 1) * P], ACT.Exp,
                                     bias=m.ncs[:, c, h:h + 1])
            ins.then_inc(s_e, 1)

    def gpsimd(pool):
        def weigh(i):
            c, g = split(i)
            heads = slice(g * HPG, (g + 1) * HPG)
            x = by_head(m.y[:, c, g * GW:(g + 1) * GW])
            if i >= 2:
                pool.wait_ge(s_y, i - 1)
            ins = pool.tensor_tensor(by_head(m.xdt[:, i % 2, :]), x, over(m.dt[:, c, heads], 64), ALU.mult)
            if c < NT - 1:
                ins = pool.tensor_tensor(by_head(m.xw[:, i % 2, :]), x, over(m.wend[:, c, heads], 64), ALU.mult)
            ins.then_inc(s_xw, 1)

        def skip(i):
            c, g = split(i)
            pool.wait_ge(s_xw, i + 1)
            y = by_head(m.y[:, c, g * GW:(g + 1) * GW])
            pool.tensor_tensor(y, y, over(m.head_rows[:, 2, g * HPG:(g + 1) * HPG], 64), ALU.mult).then_inc(s_skip, 1)

        for i in range(STEPS):
            weigh(i)
            skip(i)

    def vector(dve):
        st = kit.vector_chain(dve)

        def mix(i):
            dve.wait_ge(s_e, i + 1)
            e = m.decay[:, i % 3]
            dve.tensor_tensor(e, e, across(kit.psum[:, i % 2, 0:P], HPG), ALU.mult).then_inc(s_mix, 1)

        def fold(i):
            c, g = split(i)
            y, s = m.y[:, c, g * GW:(g + 1) * GW], m.state[:, g, :]
            yb, new = kit.psum[:, 4 + i % 2, :], kit.psum[:, 6 + i % 2, 0:GW]
            dve.wait_ge(s_skip, i + 1)
            dve.wait_ge(s_y, i + 1)
            st.mark(dve.tensor_tensor(y, y, yb[:, 0:GW], ALU.add))
            if c == 0:
                ins = dve.tensor_copy(s, new)
            else:
                dve.wait_ge(s_fold, i - 1)
                tmp = m.ytmp[:, i % 2, :]
                st.mark(dve.tensor_tensor(by_head(tmp), by_head(yb[:, GW:2 * GW]),
                                          over(m.ecs[:, c, g * HPG:(g + 1) * HPG], 64), ALU.mult))
                if c < NT - 1:
                    st.mark(dve.tensor_tensor(by_head(s), by_head(s), over(m.eend[:, c, g * HPG:(g + 1) * HPG], 64),
                                              ALU.mult))
                st.wait()
                ins = dve.tensor_tensor(y, y, tmp, ALU.add)
                if c < NT - 1:
                    ins = dve.tensor_tensor(s, s, new, ALU.add)
            ins.then_inc(s_fold, 1)

        for i in range(STEPS + 1):
            if i < STEPS:
                mix(i)
            if i >= 1:
                fold(i - 1)

    return tensor, vector, scalar, gpsimd


def mamba_gate(nc, kit, m, a):
    g = Gemm(kit, a["w_in"], KD, 0, D_INNER, False)
    s_yhigh = kit.sem("y_high_ready")
    s_gated = kit.sem("gated_ready")
    s_ss = kit.sem("squares_summed")
    s_std = kit.sem("group_deviation_ready")
    s_norm = kit.sem("y_normed")
    s_tr = kit.sem("y_transposed")
    s_tf = kit.sem("y_transpose_read")
    GW = D_INNER // SSM_GROUPS

    def tensor(pe):
        g.tensor(pe, m.x_tile)
        for n in range(X_TILES):
            if n == 0:
                pe.wait_ge(kit.tile_free, g.tile0 + g.count)
            if n % NT == 0:
                pe.wait_ge(s_norm, n + NT)
            if n >= 4:
                pe.wait_ge(s_tf, n - 3)
            for c in range(NT):
                mm = pe.transpose(kit.psum[:, n % 4, c * P:(c + 1) * P], m.y[:, c, n * P:(n + 1) * P], m.ident[:, :])
            mm.then_inc(s_tr, 1)

    def scalar(act):
        for n in range(g.count):
            ps = g.wait_tile(act, n)
            if n >= 2:
                act.wait_ge(s_gated, n - 1)
            act.activation(m.gate_tmp[:, n % 2, :], ps, ACT.Silu).then_inc(kit.tile_free, 1)
            if n % NT == NT - 1:
                j = n // NT
                act.wait_ge(s_ss, j + 1)
                act.activation(m.gstd[:, :, 2 * j:2 * j + 2], m.gss[:, :, 2 * j:2 * j + 2], ACT.Sqrt, bias=m.eps["rms"],
                               scale=1.0 / GW).then_inc(s_std, 1)
        for n in range(X_TILES):
            act.wait_ge(s_tr, n + 1)
            act.activation(m.y_tile(n).high, kit.psum[:, n % 4, :], ACT.Copy, scale=m.col("norm_w", n))\
               .then_inc(s_yhigh, 1)

    def vector(dve):
        step = kit.vector_chain(dve)

        def norm(j):
            dve.wait_ge(s_std, j + 1)
            r = m.gstd[:, :, 2 * j:2 * j + 2]
            step(dve.reciprocal(r, r))
            for t in range(NT):
                y = m.y[:, t, j * WIDE:(j + 1) * WIDE].rearrange("p (g d) -> p g d", d=GW)
                dve.tensor_tensor(y, y, over(m.gstd[:, t, 2 * j:2 * j + 2], GW), ALU.mult).then_inc(s_norm, 1)

        for n in range(g.count):
            j, t = n // NT, n % NT
            if t == 2 and j >= 1:
                norm(j - 1)
            dve.wait_ge(kit.tile_free, g.tile0 + n + 1)
            y = m.y[:, t, j * WIDE:(j + 1) * WIDE]
            dve.tensor_tensor(y, y, m.gate_tmp[:, n % 2, :], ALU.mult).then_inc(s_gated, 1)
            dve.wait_ge(s_gated, n + 1)
            for q in range(2):
                yq = y[:, q * GW:(q + 1) * GW]
                step(dve.tensor_tensor_reduce(out=m.sq_tmp[:, 0:GW], in0=yq, in1=yq, scale=1.0, scalar=0.0,
                                              op0=ALU.mult, op1=ALU.add, accum_out=m.gss[:, t, 2 * j + q:2 * j + q + 1]))
            if t == NT - 1:
                dve.engine_nop().then_inc(s_ss, 1)
        norm(g.count // NT - 1)
        for n in range(X_TILES):
            dve.wait_ge(s_yhigh, n + 1)
            dve.scalar_tensor_tensor(out=m.y_tile(n).low, in0=kit.psum[:, n % 4, :], scalar=m.col("norm_w", n),
                                     in1=m.y_tile(n).high.bitcast(F32), op0=ALU.mult, op1=ALU.subtract)\
               .then_inc(s_tf, 1)

    def gpsimd(pool):
        pool.dma_start(m.h, a["x"].rearrange("b (t p) d -> (b p) t d", p=P)).then_inc(m.h_landed, 16)
        kit.split_chunks(pool, g.last_chunk + SPLIT)

    return tensor, vector, scalar, gpsimd


def sb_project(nc, kit, m, a):
    gq = Gemm(kit, a["sb_w_q"], KD, 0, D, True)
    gk = Gemm(kit, a["sb_w_k"], KD, 0, D, True)
    gv = Gemm(kit, a["sb_w_v"], KD, 0, D, False)

    def tensor(pe):
        for g in (gq, gk, gv):
            g.tensor(pe, m.x_tile)

    def scalar(act):
        for g, dst in ((gq, m.qF), (gk, m.kF)):
            for n in range(g.count):
                ps = g.wait_tile(act, n)
                act.activation(dst[:, n, :], ps, ACT.Copy, scale=HD ** -0.5 if g is gq else 1.0)\
                   .then_inc(kit.tile_free, 1)
        for n in range(gv.count):
            ps = gv.wait_tile(act, n)
            act.activation(m.vTok[:, n % NT, (n // NT) * WIDE:(n // NT + 1) * WIDE], ps, ACT.Copy)\
               .then_inc(kit.tile_free, 1)

    def gpsimd(pool):
        kit.split_chunks(pool, gv.last_chunk + SPLIT)

    return tensor, None, scalar, gpsimd


def sb_attend(nc, kit, m, a):
    s_z = kit.sem("sb_logits_ready")
    s_abs = kit.sem("sb_abs_ready")
    s_exp = kit.sem("sb_exp_ready")
    s_ln = kit.sem("sb_ln_ready")
    s_lo = kit.sem("sb_softplus_ready")
    s_t = kit.sem("sb_later_blocks_summed")
    s_x = kit.sem("sb_exponent_ready")
    s_w = kit.sem("sb_weights_raw")
    s_cut = kit.sem("sb_weights_ready")
    s_o = kit.sem("sb_out_ready")
    s_oh = kit.sem("sb_out_high_ready")
    s_of = kit.sem("sb_out_read")

    START = [0, 512, 896, 1152]
    BANK = [(0, 0), (1, 0), (2, 0), (2, 256)]
    SPANS = [(2, 896, 384, (2, 3)), (1, 512, 384, (1,)), (0, 0, 512, (0,))]
    NS = len(SPANS)

    def bank(h, b, q=None):
        n, c = BANK[b]
        c += (0 if q is None else q - b * P)
        return kit.psum[:, 3 * (h % 2) + n, c:BANK[b][1] + SEQ - b * P]

    def packed(buf, h, b, q=None):
        c = START[b] + (0 if q is None else q - b * P)
        return buf[:, h % 2, c:START[b] + SEQ - b * P]

    def own_queries(buf, h, n):
        _, c, w, blocks = SPANS[n]
        if len(blocks) == 1:
            return buf[:, h % 2, c:c + P].unsqueeze(1)
        return buf[:, h % 2, c:c + 3 * P].rearrange("p (b q) -> p b q", q=P)[:, 0:3:2, :]

    def later(h, b, q=None):
        c = {1: 0, 0: 2 * P}[b]
        return m.later[:, h % 2, c + (0 if q is None else q - (b + 1) * P):c + SEQ - (b + 1) * P]

    def rows(h):
        return slice((h % 2) * 64, (h % 2) * 64 + 64)

    def tensor(pe):
        def logits(h):
            for n, (_, _, _, blocks) in enumerate(SPANS):
                if h >= 2:
                    pe.wait_ge(s_w, NS * (h - 2) + n + 1)
                for b in blocks:
                    mm = pe.matmul(bank(h, b), m.kF[rows(h), h // 2, b * P:(b + 1) * P], m.qF[rows(h), h // 2, b * P:],
                                   start=(b != 3), stop=True, skip_group_check=True)
                mm.then_inc(s_z, 1)

        def exponents(h):
            for n, (_, _, _, blocks) in enumerate(SPANS):
                pe.wait_ge(s_lo, NS * h + n + 1)
                for b in blocks:
                    mm = pe.matmul(bank(h, b), m.neg_lower[:, :], packed(m.sp, h, b),
                                   start=False, stop=True, skip_group_check=True)
                    if b == 2:
                        mm = pe.matmul(bank(h, 2, 3 * P), m.neg_ones[:, :], packed(m.sp, h, 3),
                                       start=False, stop=True, skip_group_check=True)
                    elif b < 2:
                        pe.wait_ge(s_t, 2 * h + 2 - b)
                        mm = pe.matmul(bank(h, b, (b + 1) * P), m.neg_ones[:, :], later(h, b),
                                       start=False, stop=True, skip_group_check=True)
                mm.then_inc(s_x, 1)

        def out(h):
            if h >= 2:
                pe.wait_ge(s_of, h - 1)
            o = kit.psum[rows(h), 6 + h % 2, :]
            pe.wait_ge(s_cut, h + 1)
            for b in range(NT):
                mm = pe.matmul(o[:, b * P:], m.vTok[:, b, h * 64:(h + 1) * 64], packed(m.wt, h, b),
                               start=(b == 0), stop=(b == NT - 1), skip_group_check=True)
            mm.then_inc(s_o, 1)

        logits(0)
        for h in range(SB_HEADS + 1):
            if h + 1 < SB_HEADS:
                logits(h + 1)
            if h < SB_HEADS:
                exponents(h)
            if h >= 1:
                out(h - 1)

    def scalar(act):
        act.preload_act_table_set("natural_log_exp_and_others")

        def ln(h):
            for n, (bk, c, w, _) in enumerate(SPANS):
                act.wait_ge(s_z, NS * h + n + 1)
                if h >= 2 and n == 0:
                    act.wait_ge(s_x, NS * (h - 1))
                ins = act.activation(m.sp[:, h % 2, c:c + w], kit.psum[:, 3 * (h % 2) + bk, 0:w], ACT.Abs)
            ins.then_inc(s_abs, 1)
            act.wait_ge(s_abs, h + 1)
            t = m.sp[:, h % 2, :]
            act.activation(t, t, ACT.Exp, scale=-1.0).then_inc(s_exp, 1)
            act.wait_ge(s_exp, h + 1)
            act.activation(t, t, ACT.Ln, bias=m.one).then_inc(s_ln, 1)

        ln(0)
        for h in range(SB_HEADS + 1):
            if h + 1 < SB_HEADS:
                ln(h + 1)
            if h < SB_HEADS:
                if h >= 2:
                    act.wait_ge(s_o, h - 1)
                for n, (bk, c, w, _) in enumerate(SPANS):
                    act.wait_ge(s_x, NS * h + n + 1)
                    act.activation(m.wt[:, h % 2, c:c + w], kit.psum[:, 3 * (h % 2) + bk, 0:w], ACT.Exp)\
                       .then_inc(s_w, 1)
            if h >= 1:
                act.wait_ge(s_o, h)
                act.activation(m.xin.high[rows(h - 1), (h - 1) // 2, :], kit.psum[rows(h - 1), 6 + (h - 1) % 2, :], ACT.Copy)\
                   .then_inc(s_oh, 1)

    def vector(dve):
        step = kit.vector_chain(dve)

        def softplus(h):
            dve.wait_ge(s_ln, h + 1)
            for n, (bk, c, w, _) in enumerate(SPANS):
                sp = m.sp[:, h % 2, c:c + w]
                step.mark(dve.scalar_tensor_tensor(out=sp, in0=kit.psum[:, 3 * (h % 2) + bk, 0:w], scalar=0.0, in1=sp,
                                                   op0=ALU.max, op1=ALU.add))
                if n >= 1:
                    cut(h, n - 1, 1)
            cut(h, NS - 1, 0)

        def cut(h, n, newer):
            dve.wait_ge(kit.vector_step, step.n - newer)
            own = own_queries(m.sp, h, n)
            dve.tensor_tensor(own, own, across(m.upper_strict[:, :], own.shape[1]), ALU.mult).then_inc(s_lo, 1)

        def low(h):
            dve.wait_ge(s_oh, h + 1)
            dve.tensor_tensor(m.xin.low[rows(h), h // 2, :], kit.psum[rows(h), 6 + h % 2, :],
                              m.xin.high[rows(h), h // 2, :].bitcast(F32), ALU.subtract).then_inc(s_of, 1)

        softplus(0)
        for h in range(SB_HEADS + 1):
            if h + 1 < SB_HEADS:
                softplus(h + 1)
            if h >= 1:
                low(h - 1)

    def gpsimd(pool):
        def sums(h):
            if h >= 2:
                pool.wait_ge(s_x, NS * (h - 1))
            pool.wait_ge(s_lo, NS * h + 1)
            pool.tensor_copy(later(h, 1)[:, 0:P], packed(m.sp, h, 2)[:, 0:P])
            pool.tensor_tensor(later(h, 1, 3 * P), packed(m.sp, h, 2, 3 * P), packed(m.sp, h, 3), ALU.add)\
                .then_inc(s_t, 1)
            pool.wait_ge(s_lo, NS * h + 2)
            pool.wait_ge(s_t, 2 * h + 1)
            pool.tensor_copy(later(h, 0)[:, 0:P], packed(m.sp, h, 1)[:, 0:P])
            pool.tensor_tensor(later(h, 0, 2 * P), packed(m.sp, h, 1, 2 * P), later(h, 1), ALU.add).then_inc(s_t, 1)

        sums(0)
        for h in range(SB_HEADS):
            if h + 1 < SB_HEADS:
                sums(h + 1)
            for n in range(NS):
                pool.wait_ge(s_w, NS * h + n + 1)
                for b in SPANS[n][3]:
                    w = packed(m.wt, h, b)[:, 0:P]
                    ins = pool.affine_select(out=w, in_=w, compare_op=ALU.is_gt, fill=0.0, base=0, pattern=[[1, P]],
                                             channel_multiplier=-1)
            ins.then_inc(s_cut, 1)

    return tensor, vector, scalar, gpsimd


def second_project(nc, kit, m, a):
    gr = Gemm(kit, a["w_in_2"], KD, 0, RW_COLS, True)
    ga = Gemm(kit, a["w_in_2"], KD, RW_COLS, 3 * ATT, False)
    gi = Gemm(kit, a["w_in_2"], KD, RW_COLS + 3 * ATT, IDXW, False)
    s_rot = kit.sem("rotated")
    s_tr = kit.sem("rope_transposed")
    s_tf = kit.sem("rope_transpose_read")
    s_cs = kit.sem("rope_table_landed")

    def tensor(pe):
        for g in (gr, ga, gi):
            g.tensor(pe, m.x_tile)
        gi.wait_free(pe, gi.count - 1)
        n = 0
        for t in range(NT):
            pe.wait_ge(s_rot, t + 1)
            for j in range(4):
                if n >= 4:
                    pe.wait_ge(s_tf, n - 3)
                for q in range(4):
                    k = 4 * j + q
                    if j < 2:
                        mm = pe.transpose(kit.psum[:, n % 4, q * P:(q + 1) * P], m.qkTok[:, t, k * P:(k + 1) * P],
                                          m.ident[:, :])
                    elif j == 2:
                        mm = pe.transpose(kit.psum[:, n % 4, q * P:(q + 1) * P], m.idxTok[:, t, q * P:(q + 1) * P],
                                          m.ident[:, :])
                    elif q < 2:
                        if q == 0:
                            mm = pe.matmul(kit.psum[0:HD, n % 4, 0:P], m.idxTok[:, t, ATT:ATT + HD], m.ident[:, :],
                                           start=True, stop=True)
                        else:
                            mm = pe.matmul(kit.psum[64:P, n % 4, P:2 * P], m.idxTok[:, t, ATT:ATT + HD], m.ident[:, :],
                                           start=True, stop=True)
                mm.then_inc(s_tr, 1)
                n += 1

    def vector(dve):
        step = kit.vector_chain(dve)
        for n in range(gr.count):
            dve.wait_ge(kit.tile_free, gr.tile0 + n + 1)
            p, d = m.rwF[:, n, :], m.shift_tmp[:, n % 2, :]
            step(dve.tensor_tensor(d[:, 1:], p[:, :SEQ - 1], p[:, 1:], ALU.subtract))
            step(dve.tensor_scalar(d[:, 0:1], p[:, 0:1], -1.0, None, ALU.mult))
            step(dve.scalar_tensor_tensor(out=p, in0=d, scalar=m.col("mu", n), in1=p, op0=ALU.mult, op1=ALU.add))
        dve.wait_ge(s_cs, 16)

        def rotate(t, x, n):
            x = x.rearrange("p (h s d) -> p h s d", s=2, d=HD // 2)
            x1, x2 = x[:, :, 0, :], x[:, :, 1, :]
            cos, sin = (across(m.rope[:, t, q * 32:(q + 1) * 32], n) for q in range(2))
            v = [m.rope_tmp[:, q, 0:n * 32].rearrange("p (h d) -> p h d", d=32) for q in range(2)]
            step.mark(dve.tensor_tensor(v[0], x1, sin, ALU.mult))
            step(dve.tensor_tensor(v[1], x2, sin, ALU.mult))
            step.mark(dve.tensor_tensor(x1, x1, cos, ALU.mult))
            step(dve.tensor_tensor(x2, x2, cos, ALU.mult))
            step.mark(dve.tensor_tensor(x1, x1, v[1], ALU.subtract))
            step(dve.tensor_tensor(x2, x2, v[0], ALU.add))

        for t in range(NT):
            ga.wait_free(dve, NT + t)
            rotate(t, m.qkTok[:, t, :], 2 * NHEAD)
        for t in range(NT):
            gi.wait_free(dve, (gi.count // NT - 1) * NT + t)
            rotate(t, m.idxTok[:, t, 0:ATT + HD], NHEAD + 1)
            dve.tensor_copy(m.widx[:, t, :], m.idxTok[:, t, ATT + HD:IDXW]).then_inc(s_rot, 1)

    def scalar(act):
        for n in range(gr.count):
            ps = gr.wait_tile(act, n)
            act.activation(m.rwF[:, n, :], ps, ACT.Copy).then_inc(kit.tile_free, 1)
        for g in (ga, gi):
            for n in range(g.count):
                j, t, w = n // NT, n % NT, g.parts[n // NT][0]
                dst = m.idxTok[:, t, j * WIDE:j * WIDE + w] if g is gi else \
                    m.qkTok[:, t, j * WIDE:(j + 1) * WIDE] if j < 2 else m.vT[:, t, :]
                ps = g.wait_tile(act, n)
                act.activation(dst, ps[:, 0:w], ACT.Copy).then_inc(kit.tile_free, 1)
        n = 0
        for t in range(NT):
            blk = slice(t * P, (t + 1) * P)
            for j in range(4):
                act.wait_ge(s_tr, n + 1)
                ps = kit.psum[:, n % 4, :]
                pairs = ps.rearrange("p (q c) -> p q c", q=4)
                if j == 0:
                    act.activation(m.q_pad[0:HD, :, 0, blk], pairs[0:HD], ACT.Copy, scale=HD ** -0.5)
                    act.activation(m.q_pad[HD:P, :, 1, blk], pairs[HD:P], ACT.Copy, scale=HD ** -0.5).then_inc(s_tf, 1)
                elif j < 3:
                    act.activation((m.attk, m.idxF)[j - 1][:, :, blk], pairs, ACT.Copy).then_inc(s_tf, 1)
                else:
                    act.activation(m.kidx_pad[0:HD, 0, blk], ps[0:HD, 0:P], ACT.Copy)
                    act.activation(m.kidx_pad[HD:P, 1, blk], ps[HD:P, P:2 * P], ACT.Copy).then_inc(s_tf, 1)
                n += 1

    def gpsimd(pool):
        pool.dma_start(m.rope[:, :, :], a["rope"].rearrange("(t p) c -> p t c", p=P)).then_inc(s_cs, 16)
        kit.split_chunks(pool, gi.last_chunk)
        pool.wait_ge(kit.tile_ready, gi.tile0 + gi.count)
        pool.memset(m.q_pad[HD:P, :, 0, :], 0.0)
        pool.memset(m.q_pad[0:HD, :, 1, :], 0.0)
        pool.memset(m.kidx_pad[HD:P, 0, :], 0.0)
        pool.memset(m.kidx_pad[0:HD, 1, :], 0.0)

    return tensor, vector, scalar, gpsimd


def sparse_attend(nc, kit, m, a):
    s_ix = kit.sem("index_products_ready")
    s_relu = kit.sem("index_relu_ready")
    s_acc = kit.sem("index_terms_added")
    s_fut = kit.sem("future_filled")
    s_lg = kit.sem("logits_ready")
    s_bias = kit.sem("key_bias_ready")
    s_max = kit.sem("logit_max_ready")
    s_p = kit.sem("probabilities_ready")
    s_tr = kit.sem("probabilities_transposed")
    s_tc = kit.sem("probabilities_copied")
    s_o = kit.sem("sparse_out_ready")
    s_of = kit.sem("sparse_out_read")
    s_yt = kit.sem("sparse_out_transposed")
    s_yc = kit.sem("sparse_out_copied")
    IDX_SCALE = HD ** -0.5 * NHEAD ** -0.5
    STEPS = NT * NHEAD
    ROUNDS = TOPK // 8

    def split(i):
        t, h = i // NHEAD, i % NHEAD
        return t, h, (t + 1) * P, slice(t * P, (t + 1) * P)

    def score(t):
        at = t * (t + 1) // 2 * P
        return m.score[:, at:at + (t + 1) * P]

    def bias(t):
        at = t * (t + 1) // 2 * P
        return m.bias_r[:, at:at + (t + 1) * P]

    def tensor(pe):
        for i in range(STEPS):
            t, h, n, blk = split(i)
            if i >= 4:
                pe.wait_ge(s_relu, i - 3)
            pe.matmul(kit.psum[:, i % 4, 0:n], m.idxF[:, h // 2, blk], m.kidx_pad[:, h % 2, 0:n],
                      start=True, stop=True).then_inc(s_ix, 1)

        def logits(i):
            t, h, n, blk = split(i)
            if i < 3:
                pe.wait_ge(s_relu, STEPS)
            else:
                pe.wait_ge(s_p, i - 2)
            out = kit.psum[:, 1 + i % 3, 0:n]
            pe.matmul(out, m.q_pad[:, h // 2, h % 2, blk], m.attk[:, h // 2, 0:n], start=True, stop=False)
            if h == 0:
                pe.wait_ge(s_bias, t + 1)
            pe.matmul(out, m.ident_r[:, :], bias(t), start=False, stop=True).then_inc(s_lg, 1)

        def turn(i):
            t, h, n, blk = split(i)
            pe.wait_ge(s_p, i + 1)
            if i >= 2:
                pe.wait_ge(s_tc, i - 1)
            for b in range(t + 1):
                mm = pe.transpose(kit.psum[:, 4 + i % 2, b * P:(b + 1) * P], m.prob[:, i % 2, b * P:(b + 1) * P],
                                  m.ident[:, :])
            mm.then_inc(s_tr, 1)

        def out(i):
            t, h, n, blk = split(i)
            pe.wait_ge(s_tc, i + 1)
            if i >= 2:
                pe.wait_ge(s_of, i - 1)
            for b in range(t + 1):
                mm = pe.matmul(kit.psum[:, 6 + i % 2, h * 64:(h + 1) * 64], m.probT[:, i % 2, b * P:(b + 1) * P],
                               m.vT[:, b, h * 64:(h + 1) * 64], start=(b == 0), stop=(b == t))
            mm.then_inc(s_o, 1)

        def turn_out(t):
            pe.wait_ge(s_of, (t + 1) * NHEAD)
            if t >= 1:
                pe.wait_ge(s_yc, t)
            for q in range(NHP):
                mm = pe.transpose(kit.psum[:, 0, q * P:(q + 1) * P], m.ybTok[:, t % 2, q * P:(q + 1) * P], m.ident[:, :])
            mm.then_inc(s_yt, 1)

        for k in range(STEPS + 5):
            if k < STEPS:
                logits(k)
            if 2 <= k < STEPS + 2:
                turn(k - 2)
            if 3 <= k < STEPS + 3:
                out(k - 3)
            if k >= 5 and (k - 4) % NHEAD == 0:
                turn_out((k - 4) // NHEAD - 1)

    def scalar(act):
        for i in range(STEPS):
            t, h, n, blk = split(i)
            act.wait_ge(s_ix, i + 1)
            if i >= 2:
                act.wait_ge(s_acc, i - 1)
            act.activation(m.relu[:, i % 2, 0:n], kit.psum[:, i % 4, 0:n], ACT.Relu).then_inc(s_relu, 1)

        def exp(i):
            n = split(i)[2]
            act.wait_ge(s_max, i + 1)
            if i >= 2:
                act.wait_ge(s_tr, i - 1)
            act.activation(m.prob[:, i % 2, 0:n], kit.psum[:, 1 + i % 3, 0:n], ACT.Exp, bias=m.nmax[:, i % 4, :],
                           accum_out=m.psum_row[:, i % 4, :]).then_inc(s_p, 1)

        def copy(i):
            n = split(i)[2]
            act.wait_ge(s_tr, i + 1)
            if i >= 2:
                act.wait_ge(s_o, i - 1)
            else:
                act.wait_ge(s_acc, STEPS)
            act.activation(m.probT[:, i % 2, 0:n], kit.psum[:, 4 + i % 2, 0:n], ACT.Copy).then_inc(s_tc, 1)

        for k in range(STEPS + 5):
            if k < STEPS:
                exp(k)
            if 2 <= k < STEPS + 2:
                copy(k - 2)
            if k >= 5 and (k - 4) % NHEAD == 0:
                t = (k - 4) // NHEAD - 1
                act.wait_ge(s_yt, t + 1)
                act.activation(m.ybF[:, :, t * P:(t + 1) * P], kit.psum[:, 0, :].rearrange("p (q c) -> p q c", q=NHP),
                               ACT.Copy).then_inc(s_yc, 1)

    def gpsimd(pool):
        for t in range(NT):
            pool.wait_ge(s_acc, (t + 1) * NHEAD)
            last = score(t)[:, t * P:]
            pool.affine_select(out=last, in_=last, compare_op=ALU.is_ge, fill=FUTURE,
                               base=0, pattern=[[-1, P]], channel_multiplier=1).then_inc(s_fut, 1)

    def vector(dve):
        step = kit.vector_chain(dve)
        def choose(t, part=0, parts=1):
            sc, wk = score(t), m.work[:, 0:(t + 1) * P]
            if part == 0:
                dve.wait_ge(s_fut, t + 1)
            if t == 0:
                step(dve.tensor_scalar(sc, sc, FUTURE / 2, None, ALU.is_ge))
            else:
                if part == 0:
                    step(dve.tensor_scalar(wk, sc, IDX_SCALE, None, ALU.mult))
                for _ in range(ROUNDS // parts):
                    step(dve.max(m.best[:, :], wk))
                    step(dve.match_replace(wk, m.best[:, :], wk, REMOVED))
                if part < parts - 1:
                    return
                step(dve.tensor_scalar(wk, wk, REMOVED, None, ALU.is_equal))
                step(dve.scalar_tensor_tensor(out=sc, in0=sc, scalar=FUTURE / 2, in1=wk, op0=ALU.is_ge, op1=ALU.mult))
            dve.tensor_scalar(bias(t), sc, -FAR, FAR, ALU.mult, ALU.add).then_inc(s_bias, 1)

        def peak(i):
            t, h, n, blk = split(i)
            dve.wait_ge(s_lg, i + 1)
            dve.tensor_reduce(m.nmax[:, i % 4, :], kit.psum[:, 1 + i % 3, 0:n], AX_X, ALU.max, negate=True)\
               .then_inc(s_max, 1)

        def finish(i):
            t, h, n, blk = split(i)
            dve.wait_ge(s_p, i + 1)
            step(dve.reciprocal(m.prec[:, i % 2, :], m.psum_row[:, i % 4, :]))
            dve.wait_ge(s_o, i + 1)
            if t >= 2 and h == 0:
                dve.wait_ge(s_yt, t - 1)
            dve.tensor_scalar(m.ybTok[:, t % 2, h * 64:(h + 1) * 64], kit.psum[:, 6 + i % 2, h * 64:(h + 1) * 64],
                              m.prec[:, i % 2, :], None, ALU.mult).then_inc(s_of, 1)

        for i in range(STEPS):
            t, h, n, blk = split(i)
            dve.wait_ge(s_relu, i + 1)
            r, w, sc = m.relu[:, i % 2, 0:n], m.widx[:, t, h:h + 1], score(t)
            if h == 0:
                dve.tensor_scalar(sc, r, w, 0.0, ALU.mult, ALU.add).then_inc(s_acc, 1)
            else:
                dve.wait_ge(s_acc, i)
                dve.scalar_tensor_tensor(out=sc, in0=r, scalar=w, in1=sc, op0=ALU.mult, op1=ALU.add).then_inc(s_acc, 1)
            if i == NHEAD:
                choose(0)
            elif i >= 2 * NHEAD:
                choose(1, i - 2 * NHEAD, 2 * NHEAD)
        for k in range(STEPS + 3):
            if k < STEPS:
                peak(k)
            if k >= 3:
                finish(k - 3)
            if k < STEPS and k // NHEAD + 2 < NT:
                choose(k // NHEAD + 2, k % NHEAD, NHEAD)

    return tensor, vector, scalar, gpsimd


def head_sums(kit, m, pe, bank, t):
    for c in range(NT):
        n = 2 * (NT * t + c)
        mm = pe.matmul(kit.psum[:, bank, n:n + 2], m.sqF[:, t, c * P:(c + 1) * P],
                       m.halves.rearrange("p (g d) -> p g d", g=2)[:, :, 0], start=True, stop=True)
    return mm


def spread_heads(kit, m, pe, bank, t):
    for c in range(NT):
        n = 2 * (NT * t + c)
        for g in range(2):
            mm = pe.matmul(kit.psum[g * 64:g * 64 + 64, bank, c * P:(c + 1) * P],
                           m.by_head[:, n + g:n + g + 1].broadcast_to([P, 64]), m.ident[:, :], start=True, stop=True)
    return mm


def rwkv_prepare(nc, kit, m, a):
    s_up = kit.sem("lora_weights_landed")
    s_lin = kit.sem("lora_inputs_ready")
    s_lo = kit.sem("lora_products_ready")
    s_act = kit.sem("lora_products_read")
    s_kk = kit.sem("key_squares_ready")
    s_kn = kit.sem("key_norm_sums_ready")
    s_kr = kit.sem("key_norm_root")
    s_ki = kit.sem("key_norm_inverse_ready")
    s_kb = kit.sem("key_norm_inverse_spread")
    s_cs = kit.sem("decay_scan_ready")
    s_ex = kit.sem("decay_factors_ready")
    s_use = kit.sem("decay_factors_used")
    s_use2 = kit.sem("decay_factors_used_by_gpsimd")

    def gpsimd(pool):
        pool.dma_start(m.up_w[0:64, :], a["w_decay_up"]).then_inc(s_up, 16)
        pool.dma_start(m.up_w[64:P, :], a["a_up"]).then_inc(s_up, 16)
        for t in range(NHP):
            pool.wait_ge(s_ex, t + 1)
            k = m.rwF[:, 4 + t, :]
            pool.tensor_tensor(k, k, m.eF[t % 2][:, 2], ALU.mult).then_inc(s_use2, 1)

    def tensor(pe):
        pe.wait_ge(s_up, 32)
        pe.wait_ge(s_lin, 1)
        for n in range(2 * NHP):
            kind, t = n // NHP, n % NHP
            if n >= 4:
                pe.wait_ge(s_act, n - 3)
            f = slice(t * P, (t + 1) * P)
            if kind == 0:
                mm = pe.matmul(kit.psum[:, n % 4, :], m.up_w[0:64, f], m.rwF[0:64, 12, :], start=True, stop=True)
            else:
                mm = pe.matmul(kit.psum[:, n % 4, :], m.up_w[64:P, f], m.rwF[64:P, 12, :], start=True, stop=True)
            mm.then_inc(s_lo, 1)
        for t in range(NHP):
            pe.wait_ge(s_kk, t + 1)
            head_sums(kit, m, pe, 4, t).then_inc(s_kn, 1)
        pe.wait_ge(s_ki, 1)
        for t in range(NHP):
            spread_heads(kit, m, pe, t, t).then_inc(s_kb, 1)

    def scalar(act):
        act.activation(m.rwF[0:64, 12, :], m.rwF[0:64, 12, :], ACT.Tanh).then_inc(s_lin, 1)
        act.activation(m.rwF[:, 13, :], m.rwF[:, 13, :], ACT.Sigmoid).then_inc(s_lin, 1)
        for n in range(2 * NHP):
            kind, t = n // NHP, n % NHP
            act.wait_ge(s_lo, n + 1)
            ps = kit.psum[:, n % 4, :]
            if kind == 0:
                act.activation(m.sg[:, t, :], ps, ACT.Sigmoid, bias=m.col("w0", t)).then_inc(s_act, 1)
            else:
                act.activation(m.aF[:, t, :], ps, ACT.Sigmoid, bias=m.col("a0", t)).then_inc(s_act, 1)
        act.wait_ge(s_kn, NHP)
        act.activation(m.by_head[:, :], kit.psum[:, 4, 0:m.by_head.shape[1]], ACT.Sqrt).then_inc(s_kr, 1)
        for t in range(NHP):
            act.wait_ge(s_cs, t + 1)
            if t >= 2:
                act.wait_ge(s_use, 3 * (t - 1))
                act.wait_ge(s_use2, t - 1)
            e = m.eF[t % 2]
            for c in range(NT):
                blk = slice(c * P, (c + 1) * P)
                mid, nmid = m.mid[:, 0, t, c:c + 1], m.mid[:, 1, t, c:c + 1]
                act.activation(e[:, 0, blk], m.prev_cs[:, t % 2, blk], ACT.Exp, bias=mid, scale=-DECAY_UNIT)
                act.activation(e[:, 1, blk], m.cs[:, t % 2, blk], ACT.Exp, bias=mid, scale=-DECAY_UNIT)
                act.activation(e[:, 2, blk], m.cs[:, t % 2, blk], ACT.Exp, bias=nmid, scale=DECAY_UNIT)
            act.activation(m.emid[:, :, t], m.mid[:, 1, t, :], ACT.Exp).then_inc(s_ex, 1)

    def vector(dve):
        step = kit.vector_chain(dve)
        dve.wait_ge(s_act, 2 * NHP)
        for t in range(NHP):
            k, kk = m.rwF[:, 4 + t, :], m.kkF[:, t, :]
            step(dve.tensor_scalar(kk, k, m.col("k_k", t), None, ALU.mult))
            dve.tensor_tensor(m.sqF[:, t, :], kk, kk, ALU.mult).then_inc(s_kk, 1)
        for t in range(NHP):
            k, ae = m.rwF[:, 4 + t, :], m.tmpF[:, 0, :]
            step(dve.tensor_scalar(ae, m.aF[:, t, :], -1.0, m.col("k_a", t), ALU.add, ALU.mult))
            step(dve.scalar_tensor_tensor(out=k, in0=ae, scalar=1.0, in1=k, op0=ALU.add, op1=ALU.mult))
            if t == 0:
                dve.wait_ge(s_kr, 1)
                step(dve.tensor_scalar(m.by_head[:, :], m.by_head[:, :], 1e-12, None, ALU.max))
                dve.reciprocal(m.by_head[:, :], m.by_head[:, :]).then_inc(s_ki, 1)
            dve.wait_ge(s_kb, t + 1)
            step(dve.tensor_tensor(m.kkF[:, t, :], m.kkF[:, t, :], kit.psum[:, t, :], ALU.mult))
            step(dve.tensor_tensor(m.aF[:, t, :], m.aF[:, t, :], m.kkF[:, t, :], ALU.mult))

        def scan(t):
            if t >= 2:
                dve.wait_ge(s_ex, t - 1)
            cs, sg = m.cs[:, t % 2, :], m.sg[:, t, :]
            for c in range(NT):
                blk = slice(c * P, (c + 1) * P)
                step.mark(dve.tensor_tensor_scan(cs[:, blk], m.ones[:, :], sg[:, blk], 0.0, ALU.mult, ALU.add))
            step.wait()
            ends = cs.rearrange("p (c l) -> p c l", l=P)[:, :, P - 1]
            dve.tensor_scalar(m.mid[:, 0, t, :], ends, DECAY_UNIT / 2, None, ALU.mult)
            dve.tensor_scalar(m.mid[:, 1, t, :], ends, -DECAY_UNIT / 2, None, ALU.mult)
            dve.tensor_tensor(m.prev_cs[:, t % 2, :], cs, sg, ALU.subtract).then_inc(s_cs, 1)

        def scale(t):
            dve.wait_ge(s_ex, t + 1)
            e = m.eF[t % 2]
            for x, f in ((m.kkF, e[:, 0]), (m.rwF, e[:, 1]), (m.aF, e[:, 2])):
                dve.tensor_tensor(x[:, t, :], x[:, t, :], f, ALU.mult).then_inc(s_use, 1)

        for t in range(NHP + 1):
            if t < NHP:
                scan(t)
            if t >= 1:
                scale(t - 1)

    return tensor, vector, scalar, gpsimd


def rwkv_scan(nc, kit, m, a):
    s_tt = kit.sem("chunk_turned")
    s_tr = kit.sem("chunk_turn_read")
    s_pr = kit.sem("pair_products_ready")
    s_pm = kit.sem("pair_products_masked")
    s_lm = kit.sem("level_matrix_ready")
    s_u = kit.sem("level_u_ready")
    s_uc = kit.sem("level_u_copied")
    s_dx = kit.sem("x_change_ready")
    s_dy = kit.sem("x_turned")
    s_xu = kit.sem("x_updated")
    s_yu = kit.sem("y_updated")
    s_d = kit.sem("value_mix_ready")
    s_w = kit.sem("wy_products_ready")
    s_dc = kit.sem("mix_and_wy_copied")
    s_z = kit.sem("state_reads_ready")
    s_sa = kit.sem("corrections_ready")
    s_n = kit.sem("new_state_ready")
    s_nr = kit.sem("new_state_read")
    s_st = kit.sem("state_scaled")
    s_y = kit.sem("recurrent_out_ready")
    s_yc = kit.sem("recurrent_out_read")
    LEVELS = 7
    RINGP = 6
    PAIR_STEPS = 10

    def rows(g):
        return slice(g * 64, g * 64 + 64)

    def quad(bank):
        return kit.psum[:, bank, :].rearrange("p (q c) -> p q c", q=NHP)

    def pair_bank(k):
        return (4 + k) % RINGP

    def level_step(c, lv, g):
        return (c * (LEVELS - 1) + lv - 1) * 2 + g

    def y_step(c, lv, g):
        return (c * (LEVELS - 2) + lv - 1) * 2 + g

    def block(c):
        return slice(c * P, (c + 1) * P)

    def head(h):
        return slice(h * 64, (h + 1) * 64)

    kap = lambda g, q, blk: m.kkF[rows(g), q, blk]
    rho = lambda g, q, blk: m.rwF[rows(g), q, blk]
    bet = lambda g, q, blk: m.aF[rows(g), q, blk]
    gam = lambda g, q, blk: m.rwF[rows(g), 4 + q, blk]
    PAIRS = [(kap, bet), (bet, kap), (gam, kap), (bet, rho), (gam, rho)]
    GQ = [(g, q) for g in range(2) for q in range(NHP)]

    def tensor(pe):
        def turn(c):
            if c >= 1:
                pe.wait_ge(s_uc, level_step(c, 1, 0))
                pe.wait_ge(s_xu, level_step(c, 1, 0))
            for n, src in enumerate((m.kkF, m.aF, m.rwF, m.rwF)):
                off = (0, 0, 4, 8)[n]
                for q in range(NHP):
                    mm = pe.transpose(kit.psum[:, n, q * P:(q + 1) * P], src[:, off + q, block(c)], m.ident[:, :])
                mm.then_inc(s_tt, 1)

        def pairs(c, k0, k1):
            for k in range(k0, k1):
                (left, right), g = PAIRS[k // 2], k % 2
                if k < 2:
                    if c >= 1 and k == 0:
                        pe.wait_ge(s_yu, y_step(c, 1, 0))
                elif k < RINGP:
                    pe.wait_ge(s_tr, 4 * c + k - 1)
                else:
                    pe.wait_ge(s_pm, PAIR_STEPS * c + k - RINGP + 1)
                for q in range(NHP):
                    mm = pe.matmul(kit.psum[:, pair_bank(k), q * P:(q + 1) * P], left(g, q, block(c)),
                                   right(g, q, block(c)), start=True, stop=True)
                mm.then_inc(s_pr, 1)

        def level(c, lv):
            d = c % 2
            if lv == 1:
                pe.wait_ge(s_pm, PAIR_STEPS * (c + 1))
            def turn_x(lv, g):
                pe.wait_ge(s_xu, level_step(c, lv, g) + 1)
                for q in range(NHP):
                    mm = pe.transpose(quad(4 + g)[:, q], m.X[d][:, g, q, :], m.ident[:, :])
                mm.then_inc(s_dy, 1)

            for g in range(2):
                i = level_step(c, lv, g)
                pe.wait_ge(s_lm, i + 1)
                if lv > 1:
                    pe.wait_ge(s_xu, i - 1)
                for q in range(NHP):
                    mm = pe.matmul(quad(g)[:, q], m.level[:, g, q, :], m.X[d][:, g, q, :], start=True, stop=True)
                mm.then_inc(s_u, 1)
                if g == 0 and lv > 1:
                    turn_x(lv - 1, 1)
            for g in range(2):
                pe.wait_ge(s_uc, level_step(c, lv, g) + 1)
                if lv > 1:
                    pe.wait_ge(s_yu, y_step(c, lv - 1, g) + 1)
                for q in range(NHP):
                    mm = pe.matmul(quad(2 + g)[:, q], m.Y[:, g, q, :], m.U[:, g, q, :], start=True, stop=True)
                mm.then_inc(s_dx, 1)
            if lv < LEVELS - 1:
                turn_x(lv, 0)

        def mixes(c):
            d = c % 2
            pe.wait_ge(s_xu, level_step(c, LEVELS - 1, 1) + 1)
            if c >= 1:
                pe.wait_ge(s_yc, 2 * c)
            for g, q in GQ:
                mm = pe.matmul(kit.psum[:, 6, head(2 * q + g)], m.gk[d][:, g, q, :], m.vC[d][:, head(2 * q + g)],
                               start=True, stop=True)
            mm.then_inc(s_d, 1)
            for g, q in GQ:
                mm = pe.matmul(quad(7)[rows(g), q], m.kapC[d][:, head(2 * q + g)], m.X[d][:, g, q, :],
                               start=True, stop=True)
            mm.then_inc(s_w, 1)

        def state_reads(c):
            d = c % 2
            pe.wait_ge(s_dc, 2 * (c + 1))
            if c >= 1:
                pe.wait_ge(s_st, c)
            for g, q in GQ:
                z = kit.psum[:, 6 + g, q * 64:(q + 1) * 64]
                mm = pe.matmul(z, m.X[d][:, g, q, :], m.D[:, head(2 * q + g)], start=True, stop=(c == 0))
                if c > 0:
                    mm = pe.matmul(z, m.WT[rows(g), q, :], m.S[d][rows(g), q, :], start=False, stop=True)
            mm.then_inc(s_z, 1)

        def new_state(c):
            d = c % 2
            pe.wait_ge(s_sa, c + 1)
            if c == NT - 1:
                return
            for g, q in GQ:
                n, hd = kit.psum[rows(g), 6, q * 64:(q + 1) * 64], head(2 * q + g)
                pe.matmul(n, m.betC[d][:, hd], m.SA[:, hd], start=True, stop=False)
                mm = pe.matmul(n, m.gamC[d][:, hd], m.vC[d][:, hd], start=False, stop=True)
            mm.then_inc(s_n, 1)

        def outputs(c):
            d = c % 2
            for g, q in GQ:
                if g == 1 and q == 0 and c < NT - 1:
                    pe.wait_ge(s_nr, c + 1)
                y, hd = quad(7 - g)[rows(g), q], head(2 * q + g)
                pe.matmul(y, m.SA[:, hd], m.br[d][:, g, q, :], start=True, stop=False)
                mm = pe.matmul(y, m.vC[d][:, hd], m.gr[d][:, g, q, :], start=False, stop=(c == 0))
                if c > 0:
                    mm = pe.matmul(y, m.S[d][rows(g), q, :], rho(g, q, block(c)), start=False, stop=True)
            mm.then_inc(s_y, 1)

        for c in range(NT):
            turn(c)
            if c >= 1:
                mixes(c - 1)
            pairs(c, 0, 6)
            if c >= 1:
                state_reads(c - 1)
            pairs(c, 6, PAIR_STEPS)
            if c >= 1:
                new_state(c - 1)
            for lv in range(1, LEVELS):
                level(c, lv)
                if lv == 2 and c >= 1:
                    outputs(c - 1)
        for part in (mixes, state_reads, new_state, outputs):
            part(NT - 1)

    def scalar(act):
        def copies(c):
            d = c % 2
            if c >= 2:
                act.wait_ge(s_y, c - 1)
            for n, dst in enumerate((m.kapC, m.betC, m.gamC, m.vC)):
                act.wait_ge(s_tt, 4 * c + n + 1)
                act.activation(dst[d][:, :], kit.psum[:, n, :], ACT.Copy).then_inc(s_tr, 1)

        def mixes(c):
            act.wait_ge(s_d, c + 1)
            act.activation(m.D[:, :], kit.psum[:, 6, :], ACT.Copy).then_inc(s_dc, 1)
            act.wait_ge(s_w, c + 1)
            act.activation(m.WT, quad(7), ACT.Copy).then_inc(s_dc, 1)

        def corrections(c):
            act.wait_ge(s_z, c + 1)
            sa = m.SA[:, :].rearrange("p (q g d) -> p q g d", g=2, d=64)
            for g in range(2):
                ins = act.activation(sa[:, :, g, :], kit.psum[:, 6 + g, 0:NHP * 64].rearrange("p (q d) -> p q d", d=64),
                                     ACT.Copy, scale=-1.0)
            ins.then_inc(s_sa, 1)

        def outputs(c):
            act.wait_ge(s_y, c + 1)
            for g in range(2):
                act.activation(m.yaF[rows(g), :, block(c)], quad(7 - g)[rows(g)], ACT.Copy).then_inc(s_yc, 1)

        for c in range(NT):
            copies(c)
            if c >= 1:
                mixes(c - 1)
                corrections(c - 1)
            for lv in range(1, LEVELS):
                for g in range(2):
                    act.wait_ge(s_u, level_step(c, lv, g) + 1)
                    act.activation(m.U[:, g], quad(g), ACT.Copy).then_inc(s_uc, 1)
                if lv == 2 and c >= 1:
                    outputs(c - 1)
        for part in (mixes, corrections, outputs):
            part(NT - 1)

    def gpsimd(pool):
        for c in range(NT):
            for lv in range(1, LEVELS):
                for g in range(2):
                    i = level_step(c, lv, g)
                    pool.wait_ge(s_pm, PAIR_STEPS * c + g + 1)
                    if i >= 2:
                        pool.wait_ge(s_u, i - 1)
                    pool.tensor_tensor(m.level[:, g], m.kb[:, g], across(m.pair_mask[:, 1 + lv, :], NHP), ALU.mult)\
                        .then_inc(s_lm, 1)

    def vector(dve):
        step = kit.vector_chain(dve)

        def masks(c):
            d = c % 2
            if c >= 1:
                dve.wait_ge(s_lm, level_step(c, 1, 0))
            if c >= 2:
                dve.wait_ge(s_y, c - 1)
            for k in range(PAIR_STEPS):
                n, g = k // 2, k % 2
                dve.wait_ge(s_pr, PAIR_STEPS * c + k + 1)
                ps = quad(pair_bank(k))
                if n == 0:
                    step(dve.tensor_copy(m.kb[:, g], ps))
                    step(dve.tensor_tensor(m.Y[:, g], m.kb[:, g], across(m.pair_mask[:, 1, :], NHP), ALU.mult))
                    dve.tensor_tensor(m.Y[:, g], across(m.ident[:, :], NHP), m.Y[:, g], ALU.subtract).then_inc(s_pm, 1)
                elif n == 1:
                    x = m.X[d][:, g]
                    step(dve.tensor_tensor(x, ps, across(m.pair_mask[:, 0, :], NHP), ALU.mult))
                    dve.tensor_tensor(x, across(m.ident[:, :], NHP), x, ALU.subtract).then_inc(s_pm, 1)
                else:
                    dst = (m.gk, m.br, m.gr)[n - 2][d]
                    mask = m.upper_strict if n == 2 else m.upper
                    dve.tensor_tensor(dst[:, g], ps, across(mask[:, :], NHP), ALU.mult).then_inc(s_pm, 1)

        def new_state(c):
            dve.wait_ge(s_n, c + 1)
            old, s = m.S[c % 2][:, :, :], m.S[(c + 1) % 2][:, :, :]
            new = kit.psum[:, 6, 0:NHP * 64].rearrange("p (q d) -> p q d", d=64)
            if c > 0:
                ins = dve.tensor_tensor(s, old, new, ALU.add)
            else:
                ins = dve.tensor_copy(s, new)
            ins.then_inc(s_nr, 1)
            dve.wait_ge(s_nr, c + 1)
            step(dve.tensor_tensor(s, s, over(m.emid[:, c, :], 64), ALU.mult))
            dve.tensor_tensor(s, s, over(m.emid[:, c + 1, :], 64), ALU.mult).then_inc(s_st, 1)

        for c in range(NT):
            masks(c)
            for lv in range(1, LEVELS):
                for g in range(2):
                    x = m.X[c % 2][:, g]
                    dve.wait_ge(s_dx, level_step(c, lv, g) + 1)
                    dve.tensor_tensor(x, x, quad(2 + g), ALU.subtract).then_inc(s_xu, 1)
                if lv < LEVELS - 1:
                    for g in range(2):
                        dve.wait_ge(s_dy, y_step(c, lv, g) + 1)
                        dve.tensor_copy(m.Y[:, g], quad(4 + g)).then_inc(s_yu, 1)
                if lv == 1 and c >= 1:
                    new_state(c - 1)

    return tensor, vector, scalar, gpsimd


def rwkv_finish(nc, kit, m, a):
    s_up = kit.sem("gate_weights_landed")
    s_gl = kit.sem("gate_products_ready")
    s_gr = kit.sem("gate_products_read")
    s_mu = kit.sem("head_sums_ready")
    s_cen = kit.sem("head_centred")
    s_sq = kit.sem("head_squares_ready")
    s_var = kit.sem("head_square_sums_ready")
    s_rt = kit.sem("head_root_ready")
    s_inv = kit.sem("head_inverse_ready")
    s_spread = kit.sem("head_inverse_spread")
    s_bo = kit.sem("bonus_terms_ready")
    s_bp = kit.sem("bonus_sums_ready")
    s_yb = kit.sem("sparse_out_high")
    s_done = kit.sem("recurrent_out_gated")
    s_high = kit.sem("recurrent_out_high")

    def gpsimd(pool):
        pool.dma_start(m.g_up[:, :], a["g_up"]).then_inc(s_up, 16)
        kit.split_chunks(pool, kit.split_done + SPLIT)

    def tensor(pe):
        for t in range(NHP):
            pe.matmul(kit.psum[:, t, :], m.halves[:, :], m.yaF[:, t, :], start=True, stop=True).then_inc(s_mu, 1)
        for t in range(NHP):
            pe.wait_ge(s_bo, t + 1)
            pe.matmul(kit.psum[:, 4 + t, :], m.halves[:, :], m.bonus[:, t, :], start=True, stop=True).then_inc(s_bp, 1)
        for t in range(NHP):
            pe.wait_ge(s_sq, t + 1)
            head_sums(kit, m, pe, 0, t).then_inc(s_var, 1)
        pe.wait_ge(s_up, 16)
        for t in range(NHP):
            pe.wait_ge(s_gr, t + 1)
            pe.matmul(kit.psum[:, 4 + t, :], m.g_up[:, t * P:(t + 1) * P], m.rwF[:, 13, :], start=True, stop=True)\
              .then_inc(s_gl, 1)
        pe.wait_ge(s_inv, 1)
        for t in range(NHP):
            spread_heads(kit, m, pe, t, t).then_inc(s_spread, 1)

    def scalar(act):
        for t in range(NHP):
            act.wait_ge(s_cen, t + 1)
            act.activation(m.sqF[:, t, :], m.yaF[:, t, :], ACT.Square).then_inc(s_sq, 1)
        act.wait_ge(s_var, NHP)
        act.activation(m.by_head[:, :], kit.psum[:, 0, 0:m.by_head.shape[1]], ACT.Sqrt, bias=m.eps["lnx"], scale=1.0 / HD)\
           .then_inc(s_rt, 1)
        for t in range(NHP):
            act.wait_ge(s_done, t + 1)
            if t == 0:
                act.wait_ge(s_bp, NHP)
            act.activation(m.yaR.high[:, t, :], m.yaF[:, t, :], ACT.Copy).then_inc(s_high, 1)
        for t in range(NHP):
            act.activation(m.ybR.high[:, t, :], m.ybF[:, t, :], ACT.Copy).then_inc(s_yb, 1)

    def vector(dve):
        step = kit.vector_chain(dve)
        for t in range(NHP):
            dve.wait_ge(s_mu, t + 1)
            y = m.yaF[:, t, :]
            dve.scalar_tensor_tensor(out=y, in0=kit.psum[:, t, :], scalar=-1.0 / HD, in1=y, op0=ALU.mult, op1=ALU.add)\
               .then_inc(s_cen, 1)
        for t in range(NHP):
            dve.scalar_tensor_tensor(out=m.bonus[:, t, :], in0=m.rwF[:, t, :], scalar=m.col("r_k", t),
                                     in1=m.rwF[:, 4 + t, :], op0=ALU.mult, op1=ALU.mult).then_inc(s_bo, 1)
        for t in range(NHP):
            dve.wait_ge(s_bp, t + 1)
            dve.tensor_tensor(m.bonus[:, t, :], m.rwF[:, 8 + t, :], kit.psum[:, 4 + t, :], ALU.mult).then_inc(s_gr, 1)
        dve.wait_ge(s_rt, 1)
        dve.reciprocal(m.by_head[:, :], m.by_head[:, :]).then_inc(s_inv, 1)
        for t in range(NHP):
            y = m.yaF[:, t, :]
            dve.wait_ge(s_spread, t + 1)
            step(dve.tensor_tensor(y, y, kit.psum[:, t, :], ALU.mult))
            step(dve.tensor_scalar(y, y, m.col("lnx_g", t), m.col("lnx_b", t), ALU.mult, ALU.add))
            step(dve.tensor_tensor(y, y, m.bonus[:, t, :], ALU.add))
            dve.wait_ge(s_gl, t + 1)
            dve.tensor_tensor(y, y, kit.psum[:, 4 + t, :], ALU.mult).then_inc(s_done, 1)
        for t in range(NHP):
            dve.wait_ge(s_high, t + 1)
            step.mark(dve.tensor_tensor(m.yaR.low[:, t, :], m.yaF[:, t, :], m.yaR.high[:, t, :].bitcast(F32), ALU.subtract))
        step.wait()
        for t in range(NHP):
            dve.wait_ge(s_yb, t + 1)
            dve.tensor_tensor(m.ybR.low[:, t, :], m.ybF[:, t, :], m.ybR.high[:, t, :].bitcast(F32), ALU.subtract)

    return tensor, vector, scalar, gpsimd


def merge(nc, kit, m, a):
    PARTS = D // WIDE
    gate0 = RW_COLS + 3 * ATT + IDXW
    plan = []
    for j in range(PARTS):
        plan.append((Gemm(kit, a["w_in_2"], KD, gate0 + j * WIDE, WIDE, True),
                     Gemm(kit, a["w_in_2"], KD, gate0 + D + j * WIDE, WIDE, True),
                     Gemm(kit, a["w_o_rwkv"], RW // P, j * WIDE, WIDE, True),
                     Gemm(kit, a["w_o_att"], ATT // P, j * WIDE, WIDE, True)))
    s_used = kit.sem("gates_used")
    s_sum = kit.sem("merged_ready")
    s_high = kit.sem("merged_high_ready")

    def tensor(pe):
        for ga, gb, ya, yb in plan:
            ga.tensor(pe, m.x_tile)
            gb.tensor(pe, m.x_tile)
            ya.tensor(pe, lambda k: Split(m.yaR.high[:, k, :], m.yaR.low[:, k, :]))
            yb.tensor(pe, lambda k: Split(m.ybR.high[:, k, :], m.ybR.low[:, k, :]))

    def scalar(act):
        for j, (ga, gb, ya, yb) in enumerate(plan):
            ga.take_over(act)
            for g, dst in ((ga, m.gate_a), (gb, m.gate_b)):
                for n in range(4):
                    ps = g.wait_tile(act, n)
                    if j >= 1:
                        act.wait_ge(s_used, 4 * (j - 1) + n + 1)
                    act.activation(dst[:, n, :], ps, ACT.Sigmoid).then_inc(kit.tile_free, 1)
            for n in range(4):
                act.wait_ge(s_sum, 4 * j + n + 1)
                act.activation(m.mergedR.high[:, 4 * j + n, :], m.gate_a[:, n, :], ACT.Copy).then_inc(s_high, 1)

    def vector(dve):
        for j, (ga, gb, ya, yb) in enumerate(plan):
            gb.wait_free(dve, 3)
            for g, gate in ((ya, m.gate_a), (yb, m.gate_b)):
                for n in range(4):
                    ps = g.wait_tile(dve, n)
                    dve.tensor_tensor(gate[:, n, :], gate[:, n, :], ps, ALU.mult).then_inc(kit.tile_free, 1)
            yb.wait_free(dve, 3)
            for n in range(4):
                dve.tensor_tensor(m.gate_a[:, n, :], m.gate_a[:, n, :], m.gate_b[:, n, :], ALU.add).then_inc(s_sum, 1)
            for n in range(4):
                dve.wait_ge(s_high, 4 * j + n + 1)
                dve.tensor_tensor(m.mergedR.low[:, 4 * j + n, :], m.gate_a[:, n, :],
                                  m.mergedR.high[:, 4 * j + n, :].bitcast(F32), ALU.subtract).then_inc(s_used, 1)

    def gpsimd(pool):
        kit.split_chunks(pool, plan[-1][-1].last_chunk + SPLIT)

    return tensor, vector, scalar, gpsimd


def ffn(nc, kit, m, a, final):
    PARTS = [(0, 12), (12, 10)]
    plan, down = [], []
    for f0, nf in PARTS:
        sub = []
        for c in range(0, nf * P, WIDE):
            n = min(WIDE, nf * P - c)
            sub.append((Gemm(kit, a["w_ffn_in"], KD, f0 * P + c, n, True),
                        Gemm(kit, a["w_ffn_in"], KD, D_FF2 + f0 * P + c, n, True)))
        plan.append(sub)
        down.append(Gemm(kit, a["w_ffn_out"], nf, 0, D, False, k_from=f0))
    t, v, act_norm, pool_out, rows, add = norm_rows(nc, kit, m, 1.0, None, "last", "norm", "last", gemms=(down[1],),
                                                    final=final)
    s_mul = kit.sem("ffn_hidden_ready")
    s_high = kit.sem("ffn_high_ready")
    s_hid = kit.sem("ffn_split_ready")
    HALF = [0, 12]

    def tensor(pe):
        for q, sub in enumerate(plan):
            for gg, gu in sub:
                gg.tensor(pe, m.x_tile)
                gu.tensor(pe, m.x_tile)
            down[q].tensor(pe, m.hidden_tile, before=lambda k, q=q: pe.wait_ge(s_hid, HALF[q] + k))

    def scalar(act):
        n = 0
        for q, sub in enumerate(plan):
            for gg, gu in sub:
                gg.take_over(act)
                for i in range(gg.count):
                    ps = gg.wait_tile(act, i)
                    if n + i >= 4:
                        act.wait_ge(s_hid, n + i - 3)
                    act.activation(m.gate_a[:, (n + i) % 4, :], ps, ACT.Silu).then_inc(kit.tile_free, 1)
                for i in range(gu.count):
                    act.wait_ge(s_mul, n + i + 1)
                    if q == 1 and n + i == HALF[1]:
                        act.wait_ge(kit.tile_ready, down[0].tile0 + down[0].count)
                    act.activation(m.hid.high[:, n + i - HALF[q], :], m.gate_a[:, (n + i) % 4, :], ACT.Copy)\
                       .then_inc(s_high, 1)
                n += gu.count
        act_norm(act)

    def vector(dve):
        n = 0
        for q, sub in enumerate(plan):
            for gg, gu in sub:
                gu.take_over(dve)
                for i in range(gu.count):
                    ps = gu.wait_tile(dve, i)
                    gt = m.gate_a[:, (n + i) % 4, :]
                    dve.tensor_tensor(gt, gt, ps, ALU.mult).then_inc(kit.tile_free, 1)
                    gu.wait_free(dve, i)
                    dve.engine_nop().then_inc(s_mul, 1)
                for i in range(gu.count):
                    dve.wait_ge(s_high, n + i + 1)
                    k = n + i - HALF[q]
                    dve.tensor_tensor(m.hid.low[:, k, :], m.gate_a[:, (n + i) % 4, :],
                                      m.hid.high[:, k, :].bitcast(F32), ALU.subtract).then_inc(s_hid, 1)
                n += gu.count
            add(dve, down[q], 1.0, q == 1)
        v(dve)

    def gpsimd(pool):
        rows(pool)
        kit.split_chunks(pool, down[1].last_chunk + SPLIT)
        pool_out(pool)

    return tensor, vector, scalar, gpsimd


HID = 16
BIG = 20768


class Memory:

    def __init__(self, kit):
        self.h = self.own(kit, "residual", NT, D)
        xin = kit.tensor_sb("x_split", [P, 2, KD, SEQ], F32R)
        self.xin = Split(xin[:, 0], xin[:, 1])
        consts = kit.tensor_sb("constants", [P, 7, P])
        self.ident, self.ones, self.upper, self.upper_strict, self.halves, self.neg_ones, self.neg_lower = \
            (consts[:, n] for n in range(7))
        self.ident_r = kit.tensor_sb("exact_identity", [P, P], F32R)[:, :]
        self.pair_mask = self.own(kit, "pair_masks", 8, P)
        self.par_cols = self.own(kit, "parameter_columns", 2, P)
        self.head_rows = self.own(kit, "head_rows", 3, SSM_HEADS)
        self.eps_mem = kit.tensor_sb("epsilons", [P, 5])
        self.eps = {k: self.eps_mem[:, n:n + 1] for n, k in enumerate(("ln", "norm", "lnx", "rms"))}
        self.one = self.eps_mem[:, 4:5]
        self.stats = kit.tensor_sb("norm_stats", [P, NT, 2, 6])
        self.mv = kit.tensor_sb("mean_variance", [P, NT, 2])
        self.ms, self.std, self.rstd = (self.own(kit, n, NT) for n in ("mean_square", "deviation", "inverse_deviation"))
        self.gss, self.gstd = (kit.tensor_sb(n, [P, NT, SSM_GROUPS]) for n in ("group_squares", "group_deviation"))
        self.by_head = self.gss[:, :, :].rearrange("p a b -> p (a b)")
        self.best = kit.tensor_sb("best", [P, 8])
        self.widx = kit.tensor_sb("index_weights", [P, NT, 8])
        self.nmax, self.psum_row = (kit.tensor_sb(n, [P, 4, 1]) for n in ("neg_max", "prob_sum"))
        self.prec = kit.tensor_sb("prob_inverse", [P, 2, 1])
        self.mid = kit.tensor_sb("half_chunk_decay", [P, 2, NHP, NT])
        self.emid = kit.tensor_sb("exp_half_chunk_decay", [P, NT, NHP])
        self.rows_mem = kit.tensor_sb("gain_rows", [P, 2 * D])
        self.rows = self.part(self.rows_mem, 0, 2, D)
        self.small = kit.tensor_sb("heads_by_token", [P, 8 * P])
        big_at = kit.nc.sbuf_base
        self.big = kit.tensor_sb("big", [P, BIG])
        hid = kit.nc.alloc_sbuf_tensor_at("hidden_split", [P, 2, HID, SEQ], F32R, offset=big_at)
        self.hid = Split(hid[:, 0], hid[:, 1])
        self.col0, at = {}, 0
        for name, n in ROWS:
            self.col0[name] = at
            at += n
        self.spare = kit.nc.alloc_sbuf_tensor_at("recurrent_second_set", [P, SPLIT * 2 * KC * WIDE], F32,
                                                 offset=kit.split_at)
        b, r, s = self.big, self.rows_mem, self.small
        self.par_rows = self.part(b, 0, 2, P)
        self.dt_raw, self.dt_abs, self.dt, self.da, self.ncs, self.ecs, self.eend, self.wend = \
            (self.part(s, n * P, NT, SSM_HEADS) for n in range(8))
        self.ytmp = self.part(b, 10752, 2, HPG * 64)
        self.bcF = self.part(b, 0, 2 * SSM_GROUPS, SEQ)
        self.past_r = self.hid.low[:, 8, 0:P]
        self.xring = self.part(b, 8192, 8, SEQ)
        self.decay = self.part(b, 8192, 3, HPG, P)
        self.xdt = self.part(b, 10240, 2, HPG * 64)
        self.xw = self.part(b, 9728, 2, HPG * 64)
        self.xT_tok = self.part(b, BIG - 8192, NT, D_INNER)
        self.y = self.xT_tok
        self.bTok = self.h
        self.state = self.part(r, 0, SSM_GROUPS, HPG * 64)
        self.gate_tmp = self.part(b, 0, 2, WIDE)
        self.sq_tmp = self.part(b, 1024, 256)
        self.relu_tmp, self.sq_tmp2 = self.part(b, 16384, 2, SEQ), self.part(b, 17408, 2, SEQ)
        self.unit = self.part(b, 16384, NT, D)
        self.qF, self.kF = self.part(b, 0, KD, SEQ), self.part(b, 4096, KD, SEQ)
        self.vTok = self.part(b, 8192, NT, D)
        self.sp, self.wt = self.part(b, 12288, 2, 1280), self.part(b, 14848, 2, 1280)
        self.later = self.part(b, 17408, 2, 5 * P)
        self.rwF = self.part(b, 0, RW_COLS // P, SEQ)
        self.qkTok = self.part(b, 7168, NT, 2 * ATT)
        self.vT = self.part(b, 11264, NT, ATT)
        self.idxTok = self.part(b, 13312, NT, IDXW)
        self.shift_tmp = self.part(b, 15648, 2, SEQ)
        self.attk = self.part(b, 17696, NHP, SEQ)
        self.q_pad, self.kidx_pad = self.part(self.spare, 0, NHP, 2, SEQ), self.part(self.spare, 4096, 2, SEQ)
        self.rope_tmp = self.part(b, 19744, 2, SEQ)
        self.idxF = self.part(r, 0, 4, SEQ)
        self.rope = self.part(s, 512, NT, HD)
        self.relu, self.score, self.work = self.part(b, 7168, 2, SEQ), self.part(b, 8192, 1280), self.part(b, 9472, SEQ)
        self.bias_r = self.hid.low[:, 0:3, :].rearrange("p a b -> p (a b)")
        self.prob, self.probT = self.part(b, 9984, 2, SEQ), self.part(b, 7168, 2, SEQ)
        self.ybTok = self.part(b, 19744, 2, ATT)
        self.ybF = self.part(b, 13312, NHP, SEQ)
        self.kkF, self.aF, self.sg = (self.part(b, 7168 + 2048 * n, NHP, SEQ) for n in range(3))
        self.yaF = self.kkF
        self.sqF = self.part(b, 15360, NHP, SEQ)
        self.tmpF = self.part(b, 17408, 1, SEQ)
        self.eF = [self.part(b, 17920, 3, SEQ), self.part(r, 512, 3, SEQ)]
        self.cs, self.prev_cs = self.part(s, 0, 2, SEQ), self.part(b, 19456, 2, SEQ)
        self.up_w = self.part(r, 0, RW)
        places = [self.part(b, 11264, 2, NHP, P), self.part(b, 12288, 2, NHP, P)] + \
            [self.part(b, 15360 + 1024 * n, 2, NHP, P) for n in range(5)]
        self.kb, X0, self.Y, self.U, self.level, gk0, br0 = places
        w = self.spare
        self.X, self.gk, self.br, self.gr = (
            [first, self.part(w, 1024 * n, 2, NHP, P)]
            for n, first in enumerate((X0, gk0, br0, self.part(s, 0, 2, NHP, P))))
        self.kapC, self.betC, self.gamC, self.vC = (
            [self.part(r, WIDE * n, WIDE), self.part(w, 4096 + WIDE * n, WIDE)] for n in range(4))
        self.D, self.SA, self.WT = self.part(w, 6144, WIDE), self.part(w, 6656, WIDE), self.part(w, 7168, NHP, P)
        self.S = [self.part(b, 6144, NHP, 64), self.part(b, 6400, NHP, 64)]
        self.bonus = self.part(b, 17408, NHP, SEQ)
        self.g_up = self.part(r, 0, RW)
        self.yaR = Split(self.hid.high[:, 0:4], self.hid.high[:, 4:8])
        self.ybR = Split(self.hid.high[:, 8:12], self.hid.high[:, 12:16])
        self.mergedR = Split(self.hid.low[:, 0:8], self.hid.low[:, 8:16])
        self.gate_a, self.gate_b = self.part(b, 16384, 4, SEQ), self.part(b, 18432, 4, SEQ)

    def x_tile(self, k):
        return Split(self.xin.high[:, k, :], self.xin.low[:, k, :])

    def hidden_tile(self, k):
        return Split(self.hid.high[:, k, :], self.hid.low[:, k, :])

    def merged_tile(self, k):
        return Split(self.mergedR.high[:, k, :], self.mergedR.low[:, k, :])

    def y_tile(self, k):
        if k < KD:
            return self.x_tile(k)
        return Split(self.hid.high[:, k - KD, :], self.hid.high[:, k, :])

    def own(self, kit, name, *dims):
        return self.part(kit.tensor_sb(name, [P, int(np.prod(dims))]), 0, *dims)

    def part(self, mem, at, *dims):
        ap = mem[:, at:at + int(np.prod(dims))]
        names = "abcd"[:len(dims)]
        if len(dims) == 1:
            return ap
        return ap.rearrange(f"p ({' '.join(names)}) -> p {' '.join(names)}", **dict(zip(names, dims)))

    def col(self, name, k):
        return self.par_cols[:, 0, self.col0[name] + k:self.col0[name] + k + 1]


def build(nc, a, out):
    with ExitStack() as ctx:
        kit = Kit(nc, ctx)
        m = Memory(kit)
        m.x_landed = [kit.sem(f"x_landed{t}") for t in range(NT)]
        m.h_landed = kit.sem("residual_landed")
        m.parameter_rows_landed = kit.sem("parameter_rows_landed")
        m.constants_cut = kit.sem("constants_cut")
        m.normf = a["normf_g"]
        m.ln_rows = {"mix1": (a["ln_mix_g"][0, :], a["ln_mix_b"][0, :]), "mlp1": (a["ln_mlp_g"][0, :], a["ln_mlp_b"][0, :]),
                     "mix2": (a["ln_mix_g"][1, :], a["ln_mix_b"][1, :]), "mlp2": (a["ln_mlp_g"][1, :], a["ln_mlp_b"][1, :])}

        plan = [
            ("setup", lambda: setup(nc, kit, m, a)),
            ("mamba_in", lambda: mamba_in(nc, kit, m, a)),
            ("mamba_scan", lambda: mamba_scan(nc, kit, m, a)),
            ("mamba_gate", lambda: mamba_gate(nc, kit, m, a)),
            ("mix1", lambda: project_norm(nc, kit, m, a["w_out"], X_TILES, m.y_tile, ALPHA, "mix1", late=True)),
            ("mlp1", lambda: mlp(nc, kit, m, a["mlp_w1"][0], a["mlp_w2"][0], "mlp1")),
            ("sb_project", lambda: sb_project(nc, kit, m, a)),
            ("sb_attend", lambda: sb_attend(nc, kit, m, a)),
            ("mix2", lambda: project_norm(nc, kit, m, a["sb_w_o"], KD, m.x_tile, ALPHA, "mix2")),
            ("mlp2", lambda: mlp(nc, kit, m, a["mlp_w1"][1], a["mlp_w2"][1], "mlp2")),
            ("norm1", lambda: norm_only(nc, kit, m, "norm1", "norm1_g", "norm")),
            ("second_project", lambda: second_project(nc, kit, m, a)),

            ("sparse", lambda: sparse_attend(nc, kit, m, a)),
            ("rwkv_prepare", lambda: rwkv_prepare(nc, kit, m, a)),
            ("rwkv_scan", lambda: rwkv_scan(nc, kit, m, a)),
            ("rwkv_finish", lambda: rwkv_finish(nc, kit, m, a)),
            ("merge", lambda: merge(nc, kit, m, a)),
            ("norm2", lambda: project_norm(nc, kit, m, a["w_out_2"], KD, m.merged_tile, 1.0, "norm2", gain="norm2_g",
                                           mode="rms", eps="norm")),
            ("last", lambda: ffn(nc, kit, m, a, out)),
        ]
        phases = []
        for name, make in plan:
            kit.phase_tile0 = kit.tiles
            phases.append(make())
        block = ctx.enter_context(nc.Block())

        def run(eng, which):
            for n, phase in enumerate(phases):
                if phase[which] is not None:
                    phase[which](eng)
                eng.drain().then_inc(kit.phase_done, 1)
                eng.wait_ge(kit.phase_done, 4 * (n + 1))

        @block.sync
        def _(sp):
            x = a["x"].rearrange("b (t p) d -> (b p) t d", p=P)
            for t in range(NT):
                sp.dma_start(m.h[:, t, :], x[:, t, :]).then_inc(m.x_landed[t], 16)
            for i, (w, k, nk, c, n) in enumerate(kit.chunks):
                if i == RING:
                    load_parameters(m, a, sp)
                if i >= RING:
                    sp.wait_ge(kit.chunk_split, i - RING + 1)
                src = w[k * P:(k + nk) * P, c:c + n].rearrange("(k p) n -> p k n", p=P)
                sp.dma_start(kit.ring[i % RING][:, 0:nk, 0:n], src).then_inc(kit.chunk_landed[i % RING], 16)

        @block.tensor
        def _(pe):
            run(pe, 0)

        @block.vector
        def _(dve):
            run(dve, 1)

        @block.scalar
        def _(act):
            run(act, 2)

        @block.gpsimd
        def _(pool):
            run(pool, 3)


_INS = [("x", "x"), ("w_in", "ssm_w_in"), ("conv_w", "ssm_conv_w"), ("conv_b", "ssm_conv_b"), ("dt_bias", "ssm_dt_bias"),
        ("a_log", "ssm_a_log"), ("ssm_d", "ssm_d"), ("norm_w", "ssm_norm_w"), ("w_out", "ssm_w_out"),
        ("sb_w_k", "sb_w_k"), ("sb_w_v", "sb_w_v"), ("sb_w_q", "sb_w_q"), ("sb_w_o", "sb_w_o"),
        ("mlp_w1", "mlp_w1"), ("mlp_w2", "mlp_w2"), ("ln_mix_g", "ln_mix_g"), ("ln_mix_b", "ln_mix_b"),
        ("ln_mlp_g", "ln_mlp_g"), ("ln_mlp_b", "ln_mlp_b"), ("norm1_g", "norm1_g_2"), ("w_in_2", "w_in_2"),
        ("mu", "tshift_mu_2"), ("w_decay_up", "w_decay_up_2"), ("w0", "w0_2"), ("a_up", "a_up_2"), ("a0", "a0_2"),
        ("g_up", "g_up_2"), ("k_k", "k_k_2"), ("k_a", "k_a_2"), ("r_k", "r_k_2"), ("lnx_g", "lnx_g_2"),
        ("lnx_b", "lnx_b_2"), ("w_o_rwkv", "w_o_rwkv_2"), ("w_o_att", "w_o_att_2"), ("w_out_2", "w_out_2"),
        ("norm2_g", "norm2_g_2"), ("w_ffn_in", "w_ffn_in_2"), ("w_ffn_out", "w_ffn_out_2"), ("normf_g", "normf_g_2")]
_ONE_LAYER = ["w_in", "conv_w", "conv_b", "dt_bias", "a_log", "ssm_d", "norm_w", "w_out", "sb_w_q", "sb_w_o"]


def kernel(**inputs):
    import numpy as _np
    import concourse.bacc as _bacc
    from concourse import mybir as _mybir
    from concourse.bass_utils import run_bass_kernel_spmd as _run

    nc = _bacc.Bacc("TRN2", target_bir_lowering=False, num_devices=1)
    arrays, a = {}, {}
    for name, source in _INS:
        v = _np.ascontiguousarray(inputs[source])
        if name in _ONE_LAYER:
            v = v[0]
        if name == "r_k":
            v = v.reshape(-1)
        arrays[f"in_{name}"] = v
        a[name] = nc.dram_tensor(f"in_{name}", v.shape, _mybir.dt.from_np(v.dtype), kind="ExternalInput").ap()
    table = host_rope()
    arrays["in_rope"] = table
    a["rope"] = nc.dram_tensor("in_rope", table.shape, _mybir.dt.from_np(table.dtype), kind="ExternalInput").ap()
    out = nc.dram_tensor("out_dram", (1, SEQ, D), F32, kind="ExternalOutput").ap()
    build(nc, a, out.rearrange("b s d -> (b s) d"))
    r = _run(nc, [arrays], core_ids=[0])
    return r.results[0]["out_dram"]
```
